# Optimizing a Trainium2 kernel written in Bass

```python
import math
import jax, jax.numpy as jnp
from jax import lax
import numpy as np

D_MODEL = 1024
BATCH = 1
SEQ = 1024
DEPTH = 1
DEC_BATCH = 8
DEC_SEQ = 16
PAST_LEN = 256

CHUNK = 64
MIX_WIDTH = D_MODEL
SSD_WIDTH = MIX_WIDTH // 2
SSD_HEAD_DIM = 64
SSD_HEADS = SSD_WIDTH // SSD_HEAD_DIM
SSD_GROUPS = 2
SSD_REP = SSD_HEADS // SSD_GROUPS
SSD_STATE = 128
SSD_CONV = 4
SSD_BLOCK = 64
SSD_XBC = SSD_WIDTH + 2 * SSD_GROUPS * SSD_STATE
SSD_NORM_GROUP = SSD_WIDTH // SSD_GROUPS
SSD_NORM_EPS = 1e-5
ATT_WIDTH = MIX_WIDTH - SSD_WIDTH
ATT_HEAD_DIM = 64
ATT_HEADS = ATT_WIDTH // (2 * ATT_HEAD_DIM)
ATT_V_DIM = 2 * ATT_HEAD_DIM
ATT_NORM_EPS = 1e-5
Q_BLOCK = 128
ROPE_THETA = 10000.0
MEM_LEN = 256
MEM_HEADS = 4
MEM_HEAD_DIM = D_MODEL // MEM_HEADS
FFN_HIDDEN = -(-8 * D_MODEL // (3 * 256)) * 256
NORM_EPS = 1e-6
IN_COLS = SSD_WIDTH + SSD_XBC + SSD_HEADS + 3 * ATT_WIDTH
IN_SPLITS = [SSD_WIDTH, SSD_WIDTH + SSD_XBC, SSD_WIDTH + SSD_XBC + SSD_HEADS,
             SSD_WIDTH + SSD_XBC + SSD_HEADS + ATT_WIDTH,
             SSD_WIDTH + SSD_XBC + SSD_HEADS + 2 * ATT_WIDTH]

kernel_name = 'hybrid_ssd_diffattn_stream_step'

def rms_norm(x, g, eps=NORM_EPS):
    xf = x.astype(jnp.float32)
    y = xf * lax.rsqrt(jnp.mean(xf * xf, axis=-1, keepdims=True) + eps)
    return (y * g.astype(jnp.float32)).astype(x.dtype)

def rope(x, pos):
    d = x.shape[-1]
    inv = jnp.power(ROPE_THETA, -jnp.arange(0, d, 2, dtype=jnp.float32) / d)
    ang = pos[:, None] * inv[None, :]
    cos = jnp.cos(ang)[None, :, None, None, :]
    sin = jnp.sin(ang)[None, :, None, None, :]
    xf = x.astype(jnp.float32)
    x1, x2 = xf[..., : d // 2], xf[..., d // 2:]
    return jnp.concatenate([x1 * cos - x2 * sin, x2 * cos + x1 * sin], axis=-1).astype(x.dtype)

def causal_conv(buf, u, w, b):
    ext = jnp.concatenate([buf.astype(u.dtype), u], axis=1)
    y = lax.conv_general_dilated(ext, w[:, None, :].astype(u.dtype), window_strides=(1,), padding='VALID',
                                 dimension_numbers=('NWC', 'WIO', 'NWC'), feature_group_count=u.shape[-1])
    return y + b.astype(u.dtype), ext[:, -(SSD_CONV - 1):]

def ssd_scan(x, dt, a, bmat, cmat, h0, blk):
    bsz, l, _, p = x.shape
    nc = l // blk
    xdt = (x * dt[..., None]).reshape(bsz, nc, blk, SSD_GROUPS, SSD_REP, p)
    bm = bmat.reshape(bsz, nc, blk, SSD_GROUPS, SSD_STATE)
    cm = cmat.reshape(bsz, nc, blk, SSD_GROUPS, SSD_STATE)
    ad = (dt * a).reshape(bsz, nc, blk, SSD_GROUPS, SSD_REP).transpose(0, 3, 4, 1, 2)
    acum = jnp.cumsum(ad, axis=-1)
    tri = jnp.tril(jnp.ones((blk, blk), dtype=bool))
    lmat = jnp.exp(jnp.where(tri, acum[..., :, None] - acum[..., None, :], -jnp.inf))
    cb = jnp.einsum('bclgn,bcsgn->bgcls', cm, bm)
    y_diag = jnp.einsum('bgrcls,bcsgrp->bclgrp', cb[:, :, None] * lmat, xdt)
    decay_in = jnp.exp(acum[..., -1:] - acum)
    chunk_states = jnp.einsum('bclgn,bgrcl,bclgrp->bcgrpn', bm, decay_in, xdt)
    chunk_decay = jnp.exp(acum[..., -1])

    def step(s, inp):
        st, dc = inp
        return s * dc[..., None, None] + st, s

    h0g = h0.reshape(bsz, SSD_GROUPS, SSD_REP, p, SSD_STATE)
    final, prev = lax.scan(step, h0g, (jnp.moveaxis(chunk_states, 1, 0), jnp.moveaxis(chunk_decay, -1, 0)))
    prev = jnp.moveaxis(prev, 0, 1)
    y_off = jnp.einsum('bclgn,bcgrpn,bgrcl->bclgrp', cm, prev, jnp.exp(acum))
    y = (y_diag + y_off).reshape(bsz, l, SSD_HEADS, p)
    return y, final.reshape(bsz, SSD_HEADS, p, SSD_STATE)

def diff_attn_block(q, k, v, qpos, kpos, lam):
    s = jnp.einsum('bqhcd,bkhcd->bhcqk', q.astype(jnp.float32), k.astype(jnp.float32)) / math.sqrt(ATT_HEAD_DIM)
    visible = (kpos[None, :] // CHUNK) <= (qpos[:, None] // CHUNK)
    p = jax.nn.softmax(jnp.where(visible, s, -jnp.inf), axis=-1)
    att = p[:, :, 0] - lam * p[:, :, 1]
    return jnp.einsum('bhqk,bkhe->bqhe', att, v.astype(jnp.float32))

def diff_attention(q, k, v, qpos, kpos, lam):
    bsz, sq = q.shape[0], q.shape[1]
    if sq % Q_BLOCK != 0:
        return diff_attn_block(q, k, v, qpos, kpos, lam)
    nb = sq // Q_BLOCK
    qb = jnp.moveaxis(q.reshape(bsz, nb, Q_BLOCK, ATT_HEADS, 2, ATT_HEAD_DIM), 1, 0)
    pb = qpos.reshape(nb, Q_BLOCK)
    out = lax.map(lambda t: diff_attn_block(t[0], k, v, t[1], kpos, lam), (qb, pb))
    return jnp.moveaxis(out, 0, 1).reshape(bsz, sq, ATT_HEADS, ATT_V_DIM)

def memory_kv(mem, g_mem, wk_x, wv_x):
    mn = rms_norm(mem, g_mem)
    b = mem.shape[0]
    mk = (mn @ wk_x).reshape(b, MEM_LEN, MEM_HEADS, MEM_HEAD_DIM)
    mv = (mn @ wv_x).reshape(b, MEM_LEN, MEM_HEADS, MEM_HEAD_DIM)
    return mk, mv

def layer_step(x, conv_buf, ssm0, k_past, v_past, mem_k, mem_v, lam_init,
               w_in, conv_w, conv_b, dt_bias, a_log, d_skip, ssm_norm_w,
               lam_q1, lam_k1, lam_q2, lam_k2, subln_w, w_out, wq_x, wo_x,
               g_pre_mix, g_post_mix, g_pre_x, g_post_x, g_pre_ffn, g_post_ffn,
               w_gate, w_up, w_down):
    f32 = jnp.float32
    bsz, l, _ = x.shape
    dtype = x.dtype
    past = k_past.shape[1]
    pos = past + jnp.arange(l, dtype=jnp.int32)

    hn = rms_norm(x, g_pre_mix)
    z, xbc, dt_raw, q, k, v = jnp.split(hn @ w_in, IN_SPLITS, axis=-1)

    xbc, conv_new = causal_conv(conv_buf, xbc, conv_w, conv_b)
    xbc = jax.nn.silu(xbc.astype(f32))
    xs, bm, cm = jnp.split(xbc, [SSD_WIDTH, SSD_WIDTH + SSD_GROUPS * SSD_STATE], axis=-1)
    dt = jax.nn.softplus(dt_raw.astype(f32) + dt_bias.astype(f32))
    a = -jnp.exp(a_log.astype(f32))
    blk = SSD_BLOCK if l % SSD_BLOCK == 0 else l
    xh = xs.reshape(bsz, l, SSD_HEADS, SSD_HEAD_DIM)
    y, ssm_new = ssd_scan(xh, dt, a, bm.reshape(bsz, l, SSD_GROUPS, SSD_STATE),
                          cm.reshape(bsz, l, SSD_GROUPS, SSD_STATE), ssm0.astype(f32), blk)
    y = y + d_skip.astype(f32)[:, None] * xh
    y = y.reshape(bsz, l, SSD_WIDTH) * jax.nn.silu(z.astype(f32))
    yg = y.reshape(bsz, l, SSD_GROUPS, SSD_NORM_GROUP)
    yg = yg * lax.rsqrt(jnp.mean(yg * yg, axis=-1, keepdims=True) + SSD_NORM_EPS)
    y_ssd = (yg.reshape(bsz, l, SSD_WIDTH) * ssm_norm_w.astype(f32)).astype(dtype)

    posf = pos.astype(f32)
    q = rope(q.reshape(bsz, l, ATT_HEADS, 2, ATT_HEAD_DIM), posf)
    k = rope(k.reshape(bsz, l, ATT_HEADS, 2, ATT_HEAD_DIM), posf)
    v = v.reshape(bsz, l, ATT_HEADS, ATT_V_DIM)
    k_all = jnp.concatenate([k_past.astype(dtype), k], axis=1)
    v_all = jnp.concatenate([v_past.astype(dtype), v], axis=1)
    kpos = jnp.arange(past + l, dtype=jnp.int32)
    lam = (jnp.exp(jnp.sum(lam_q1.astype(f32) * lam_k1.astype(f32)))
           - jnp.exp(jnp.sum(lam_q2.astype(f32) * lam_k2.astype(f32))) + lam_init)
    o = diff_attention(q, k_all, v_all, pos, kpos, lam)
    o = o * lax.rsqrt(jnp.mean(o * o, axis=-1, keepdims=True) + ATT_NORM_EPS) * subln_w.astype(f32) * (1.0 - lam_init)
    y_att = o.reshape(bsz, l, ATT_WIDTH).astype(dtype)

    mix = jnp.concatenate([y_ssd, y_att], axis=-1) @ w_out
    h = x + rms_norm(mix, g_post_mix)

    qx = (rms_norm(h, g_pre_x) @ wq_x).reshape(bsz, l, MEM_HEADS, MEM_HEAD_DIM)
    s = jnp.einsum('bqhd,bmhd->bhqm', qx.astype(f32), mem_k.astype(f32)) / math.sqrt(MEM_HEAD_DIM)
    p = jax.nn.softmax(s, axis=-1)
    ox = jnp.einsum('bhqm,bmhd->bqhd', p, mem_v.astype(f32)).reshape(bsz, l, D_MODEL).astype(dtype)
    h = h + rms_norm(ox @ wo_x, g_post_x)

    hn = rms_norm(h, g_pre_ffn)
    f = (jax.nn.silu(hn @ w_gate) * (hn @ w_up)) @ w_down
    h = h + rms_norm(f, g_post_ffn)
    return h, k, v, ssm_new.astype(dtype), conv_new

def setup_inputs(seed: int = 0) -> dict:
    key = jax.random.key(seed)
    ks = iter(jax.random.split(key, 48))
    L = DEPTH

    def nrm(shape, scale):
        return jax.random.normal(next(ks), shape, jnp.float32) * scale

    def gain(n):
        return 1.0 + nrm((L, n), 0.05)

    dt0 = jnp.exp(jax.random.uniform(next(ks), (L, SSD_HEADS), jnp.float32,
                                     minval=math.log(1e-3), maxval=math.log(1e-1)))
    return {
        'x_prompt': nrm((BATCH, SEQ, D_MODEL), 1.0),
        'x_sample': nrm((DEC_BATCH, DEC_SEQ, D_MODEL), 1.0),
        'cache_attn_k': nrm((L, DEC_BATCH, PAST_LEN, ATT_HEADS, 2, ATT_HEAD_DIM), 1.0),
        'cache_attn_v': nrm((L, DEC_BATCH, PAST_LEN, ATT_HEADS, ATT_V_DIM), 1.0),
        'state_ssm': nrm((L, DEC_BATCH, SSD_HEADS, SSD_HEAD_DIM, SSD_STATE), 0.1),
        'state_conv': nrm((L, DEC_BATCH, SSD_CONV - 1, SSD_XBC), 1.0),
        'cache_mem_k': nrm((L, DEC_BATCH, MEM_LEN, MEM_HEADS, MEM_HEAD_DIM), 1.0),
        'cache_mem_v': nrm((L, DEC_BATCH, MEM_LEN, MEM_HEADS, MEM_HEAD_DIM), 1.0),
        'mem_prompt': nrm((BATCH, MEM_LEN, D_MODEL), 1.0),
        'w_in': nrm((L, D_MODEL, IN_COLS), D_MODEL ** -0.5),
        'conv_w': nrm((L, SSD_CONV, SSD_XBC), SSD_CONV ** -0.5),
        'conv_b': nrm((L, SSD_XBC), 0.02),
        'dt_bias': dt0 + jnp.log(-jnp.expm1(-dt0)),
        'a_log': jnp.log(jax.random.uniform(next(ks), (L, SSD_HEADS), jnp.float32, minval=1.0, maxval=16.0)),
        'd_skip': 1.0 + nrm((L, SSD_HEADS), 0.1),
        'ssm_norm_w': gain(SSD_WIDTH),
        'lam_q1': nrm((L, ATT_HEAD_DIM), 0.1),
        'lam_k1': nrm((L, ATT_HEAD_DIM), 0.1),
        'lam_q2': nrm((L, ATT_HEAD_DIM), 0.1),
        'lam_k2': nrm((L, ATT_HEAD_DIM), 0.1),
        'subln_w': gain(ATT_V_DIM),
        'w_out': nrm((L, MIX_WIDTH, D_MODEL), MIX_WIDTH ** -0.5),
        'g_mem': gain(D_MODEL),
        'wq_x': nrm((L, D_MODEL, D_MODEL), D_MODEL ** -0.5),
        'wk_x': nrm((L, D_MODEL, D_MODEL), D_MODEL ** -0.5),
        'wv_x': nrm((L, D_MODEL, D_MODEL), D_MODEL ** -0.5),
        'wo_x': nrm((L, D_MODEL, D_MODEL), D_MODEL ** -0.5),
        'g_pre_mix': gain(D_MODEL),
        'g_post_mix': gain(D_MODEL),
        'g_pre_x': gain(D_MODEL),
        'g_post_x': gain(D_MODEL),
        'g_pre_ffn': gain(D_MODEL),
        'g_post_ffn': gain(D_MODEL),
        'w_gate': nrm((L, D_MODEL, FFN_HIDDEN), D_MODEL ** -0.5),
        'w_up': nrm((L, D_MODEL, FFN_HIDDEN), D_MODEL ** -0.5),
        'w_down': nrm((L, FFN_HIDDEN, D_MODEL), FFN_HIDDEN ** -0.5),
    }

def reference(x_prompt, x_sample, cache_attn_k, cache_attn_v, state_ssm, state_conv, cache_mem_k, cache_mem_v,
              mem_prompt, w_in, conv_w, conv_b, dt_bias, a_log, d_skip, ssm_norm_w,
              lam_q1, lam_k1, lam_q2, lam_k2, subln_w, w_out, g_mem, wq_x, wk_x, wv_x, wo_x,
              g_pre_mix, g_post_mix, g_pre_x, g_post_x, g_pre_ffn, g_post_ffn, w_gate, w_up, w_down):
    dtype = x_prompt.dtype
    bp = x_prompt.shape[0]
    hp, hs = x_prompt, x_sample
    pk, pv, pssm, pconv, pmk, pmv, sk, sv, sssm, sconv = ([] for _ in range(10))
    for i in range(DEPTH):
        lam_init = 0.8 - 0.6 * math.exp(-0.3 * i)
        lw = (w_in[i], conv_w[i], conv_b[i], dt_bias[i], a_log[i], d_skip[i], ssm_norm_w[i],
              lam_q1[i], lam_k1[i], lam_q2[i], lam_k2[i], subln_w[i], w_out[i], wq_x[i], wo_x[i],
              g_pre_mix[i], g_post_mix[i], g_pre_x[i], g_post_x[i], g_pre_ffn[i], g_post_ffn[i],
              w_gate[i], w_up[i], w_down[i])
        mk, mv = memory_kv(mem_prompt, g_mem[i], wk_x[i], wv_x[i])
        hp, k_new, v_new, ssm_new, conv_new = layer_step(
            hp,
            jnp.zeros((bp, SSD_CONV - 1, SSD_XBC), dtype),
            jnp.zeros((bp, SSD_HEADS, SSD_HEAD_DIM, SSD_STATE), jnp.float32),
            jnp.zeros((bp, 0, ATT_HEADS, 2, ATT_HEAD_DIM), dtype),
            jnp.zeros((bp, 0, ATT_HEADS, ATT_V_DIM), dtype),
            mk, mv, lam_init, *lw)
        pk.append(k_new); pv.append(v_new); pssm.append(ssm_new); pconv.append(conv_new)
        pmk.append(mk); pmv.append(mv)
        hs, k_new, v_new, ssm_new, conv_new = layer_step(
            hs, state_conv[i], state_ssm[i], cache_attn_k[i], cache_attn_v[i],
            cache_mem_k[i], cache_mem_v[i], lam_init, *lw)
        sk.append(k_new); sv.append(v_new); sssm.append(ssm_new); sconv.append(conv_new)
    return (hp, hs,
            jnp.stack(pk), jnp.stack(pv), jnp.stack(pssm), jnp.stack(pconv), jnp.stack(pmk), jnp.stack(pmv),
            jnp.stack(sk), jnp.stack(sv), jnp.stack(sssm), jnp.stack(sconv))


_drawn_inputs = setup_inputs


def setup_inputs(seed=0):
    import zlib

    import numpy as np

    out = dict(_drawn_inputs(seed))
    spreads = {}
    factors = {}
    for name, (base, spread) in spreads.items():
        noise = np.random.default_rng([zlib.crc32(name.encode()), seed]).standard_normal(out[name].shape)
        drawn = base * np.exp(spread * noise) if base else spread * noise
        out[name] = __import__('jax').numpy.asarray(drawn.astype(out[name].dtype))
    for name, factor in factors.items():
        out[name] = (out[name] * factor).astype(out[name].dtype)
    return out
```

```python
from contextlib import ExitStack

import numpy as np

import concourse.bass as bass
from concourse import mybir

P = 128
D = 1024
KT = D // P
SEQ, DB, DS, PAST, MEM = 1024, 8, 16, 256, 256
NS = DB * DS
NTOK = SEQ + NS
NT = NTOK // P
NC = 384
CH = NTOK // NC
FT = 2816 // P
NG = FT // 2
H, DH = 4, 128
SH, SP_ = 8, 64
XP = 3 + SEQ + DB * (3 + DS)
WI = 1024
BIG = -1e30

F32 = mybir.dt.float32
F32R = mybir.dt.float32r
ALU = mybir.AluOpType
ACT = mybir.ActivationFunctionType
AX = mybir.AxisListType.X

I_MK, I_MV, I_TM, I_XB, I_WO, I_WQ, I_WX, I_FF = 0, 8, 16, 32, 40, 48, 56, 64
N_ITEMS = I_FF + 6 * NG

C_ID, C_TP, C_TS, C_BS, C_BB, C_COS, C_SIN = 0, 128, 256, 384, 512, 520, 808
C_C0, C_C1 = 1096, 1097
C_END = 1098
G_MEM, G_PREMIX, G_POSTMIX, G_PREX, G_POSTX, G_PREF, G_POSTF = (8 * i for i in range(7))
V_CW = 56
V_CB = 88
V_SSM = 96
V_SUB = 100
V_END = 101
R_DTB, R_ALOG, R_DSK, R_LAM = 0, 8, 16, 24
R_END = 280


def build(nc, xT, memT, wall, wdt, consts, vecs, rows, kc, vc, h0, sconv, cmk, cmv,
          y_o, k_o, v_o, ssm_o, conv_o, mk_o, mv_o, zs_d, q_d, h_d):
    with ExitStack() as ctx:
        def sb(name, shape, dt=F32):
            return ctx.enter_context(nc.sbuf_tensor(name, shape, dt))

        def sem(name):
            return ctx.enter_context(nc.semaphore(name))

        raw = [sb(f"w_raw{i}", [P, WI]) for i in range(2)]
        whi = [sb(f"w_hi{i}", [P, WI], F32R) for i in range(4)]
        wlo = [sb(f"w_lo{i}", [P, WI], F32R) for i in range(4)]
        one = sb("one", [P, 1])
        cst = sb("cst", [P, C_END])
        vec = sb("vec", [P, V_END])
        ones = sb("ones", [P, P])
        eps6 = sb("eps6", [P, 1])
        eps5 = sb("eps5", [P, 1])
        nlam = sb("nlam", [P, 1])
        lams = sb("lams", [P, 2])
        coef = sb("coef", [P, 1])
        cred = sb("cred", [P, 4])

        def overlay(*groups):
            made, sizes = {}, []
            for group in groups:
                with ExitStack() as inner:
                    total = 0
                    for name, shape, dt in group:
                        made[name] = inner.enter_context(nc.sbuf_tensor(name, shape, dt))
                        total += -(-4 * int(np.prod(shape[1:])) // 64) * 64
                    sizes.append(total)
            sb(f"hold_{groups[0][0][0]}", [P, max(sizes) // 4])
            return made

        T = {}
        T.update(overlay([("H", [P, KT, NTOK], F32)],
                         [(f"hid_{a}{g}{f}", [P, NTOK], F32R) for g in range(2) for f in range(2) for a in "hl"]))
        T.update(overlay([("NH", [P, KT, NTOK], F32R)],
                         [("YT", [P, KT, NTOK], F32)],
                         [("MIX", [P, KT, NTOK], F32)],
                         [("xE", [P, H, MEM], F32), ("xPT", [P, 2 * H * P], F32), ("xQbd", [P, DB, KT, 64], F32)],
                         [("Hback", [P, KT, NTOK], F32)]))
        T.update(overlay([("NL", [P, KT, NTOK], F32R)],
                         [("NLf", [P, KT, NTOK], F32)],
                         [("adb", [P, SH, P], F32), ("E", [P, SH, P], F32), ("MT", [P, SH, P], F32),
                          ("h0t", [P, DB, 512], F32), ("cbm", [P, 2, P], F32), ("Btm", [P, 2, P], F32),
                          ("sqs", [P, 512], F32)],
                         [("V", [P, NT, 512], F32), ("E0", [P, SEQ], F32), ("E1", [P, SEQ], F32),
                          ("ATT", [P, SEQ], F32), ("PTs", [P, SEQ], F32)],
                         [("Kb0", [P, H, PAST], F32), ("Kb1", [P, H, PAST], F32), ("Vb0", [P, 2, 512], F32),
                          ("Vb1", [P, 2, 512], F32), ("Vs", [P, 512], F32), ("Es", [P, PAST + DS], F32),
                          ("Pn", [P, DB, P], F32), ("Pp", [P, 2, PAST], F32), ("PTb", [P, 3, P], F32),
                          ("oTs", [P, H, P], F32)],
                         [("mkT", [P, KT, MEM], F32), ("mvt", [P, 2, D], F32), ("cK", [P, KT, MEM], F32),
                          ("cV", [P, 2, D], F32), ("sE", [64, MEM], F32), ("sPT", [P, 2, 64], F32)]))
        T.update(overlay([("XC", [P, KT, NTOK], F32)],
                         [(f"stg{i}", [P, NT, 256], F32) for i in range(4)],
                         [("mraw", [P, KT, MEM], F32), ("mhi", [P, KT, MEM], F32R), ("mlo", [P, KT, MEM], F32R),
                          ("mvs", [P, 2, D], F32)],
                         [("KTt", [P, H, SEQ], F32), ("QTt", [P, H, SEQ], F32), ("KTs", [P, H, P], F32),
                          ("QTs", [P, H, P], F32)],
                         [("Qbd", [P, DB, H, P], F32)],
                         [("YH", [P, KT, NTOK], F32R)],
                         [("QX", [P, KT, NTOK], F32)],
                         [("ACC", [P, KT, NTOK], F32)]))
        T.update(overlay([("sq", [P, KT, NC], F32), ("rstd", [P, NC], F32)],
                         [("wdr", [P, KT, 8], F32), ("wdh", [P, KT, 8], F32R), ("wdl", [P, KT, 8], F32R),
                          ("rpA", [P, 256], F32), ("rpB", [P, 256], F32), ("dts", [P, NT * 8, 6], F32)],
                         [("xp0", [P, XP], F32), ("xp1", [P, XP], F32), ("acc", [P, NTOK], F32),
                          ("cvo", [P, KT, 27], F32), ("cvi", [P, KT, 24], F32)],
                         [("xs", [P, 512], F32), ("xdt", [P, 512], F32), ("xdd", [P, 512], F32),
                          ("ST", [P, 512], F32), ("zt", [P, 512], F32), ("yA", [P, 512], F32),
                          ("sm", [P, 128], F32), ("yoT", [P, 512], F32)],
                         [("qkr0", [P, 2, 512], F32), ("qkr1", [P, 2, 512], F32), ("on", [P, 512], F32),
                          ("at_sm", [P, 64], F32)],
                         [("xm", [P, 32], F32)],
                         [(f"sg{i}", [P, NC], F32) for i in range(2)] + [(f"hr{i}", [P, NC], F32) for i in range(2)]))
        dt_t = sb("dt_t", [P, NT, SH])
        ad_t = sb("ad_t", [P, NT, SH])
        row = sb("row", [P, R_END])
        g = T.__getitem__

        bank = [ctx.enter_context(nc.psum_tensor(f"bank{i}", [P, 1024], F32)) for i in range(4)]
        B = [bank[i // 2][:, 512 * (i % 2):512 * (i % 2) + 512] for i in range(8)]
        TT = nc.vector.tensor_tensor
        TS = nc.vector.tensor_scalar
        STT = nc.vector.scalar_tensor_tensor
        CP = nc.vector.tensor_copy
        act_f = nc.scalar.activation
        mm = nc.tensor.matmul
        ident = cst[:, C_ID:C_ID + P]

        ld = {n: sem("ld_" + n) for n in ("cst", "vec", "row", "mem", "x0", "x1", "x2", "wdt", "scv", "h0", "Hb0", "Hb1", "Hb2")}
        w_raw = [sem(f"w_raw_in{i}") for i in range(2)]
        w_hi = sem("w_hi_done")
        w_ready = sem("w_ready")
        w_used = sem("w_used")
        setup = sem("setup_done")
        n_sq, n_sum, n_std, n_t, n_hi, n_lo, n_res = (sem("norm_" + x) for x in
                                                      ("squares", "sums", "std", "scaled", "high", "ready", "residual"))
        lin_mm, lin_ev = sem("lin_mm"), sem("lin_evac")
        tm_mm, tm_ev = sem("tm_mm"), sem("tm_evac")
        st_out = [sem(f"stage_out{i}") for i in range(4)]
        mem_mm, mem_ev, mem_out = sem("mem_mm"), sem("mem_evac"), sem("mem_out")
        dve_c, act_c = sem("dve_chain"), sem("act_chain")
        out_s = sem("out_stores")

        chain = {"dve": 0, "act": 0}

        def dlink(eng, ins):
            chain["dve"] += 1
            ins.then_inc(dve_c, 1)
            eng.wait_ge(dve_c, chain["dve"])

        def alink(eng, ins):
            chain["act"] += 1
            ins.then_inc(act_c, 1)
            eng.wait_ge(act_c, chain["act"])

        def three(out, pairs, release=()):
            n = len(pairs)
            for i, (ah, al, bh, bl) in enumerate(pairs):
                m = mm(out, ah, bh, start=(i == 0), stop=False)
                if i in release:
                    m.then_inc(w_used, 1)
                mm(out, ah, bl, start=False, stop=False)
                m = mm(out, al, bh, start=False, stop=(i == n - 1))
            return m

        def chunk_no(stage, c):
            return 1 + 3 * stage + c

        def norm_act_sum(act, n, src, w, ready, gate=None):
            for s, v in ready:
                act.wait_ge(s, v)
            if n:
                act.wait_ge(n_sum, n)
            act_f(g("sq")[:, :, 0:w], src, ACT.Square).then_inc(n_sq, 1)
            act.wait_ge(n_sum, n + 1)
            if n:
                act.wait_ge(n_t, n)
            act_f(g("rstd")[:, 0:w], B[7][:, 0:w], ACT.Sqrt, bias=eps6[:, :], scale=1.0 / D).then_inc(n_std, 1)

        def norm_pe(pe, n, w):
            pe.wait_ge(n_sq, n + 1)
            if n:
                pe.wait_ge(n_std, n)
            for k in range(KT):
                m = mm(B[7][:, 0:w], ones[:, :], g("sq")[:, k, 0:w], start=(k == 0), stop=(k == KT - 1))
            m.then_inc(n_sum, 1)

        def norm_dve_pre(dve, n, src, tmp, lo, hi, gain, w):
            dve.wait_ge(n_std, n + 1)
            dlink(dve, nc.vector.reciprocal(g("rstd")[:, 0:w], g("rstd")[:, 0:w]))
            for k in range(KT):
                m = STT(out=tmp[:, k, :], in0=src[:, k, :], scalar=vec[:, gain + k:gain + k + 1],
                        in1=g("rstd")[:, 0:w], op0=ALU.mult, op1=ALU.mult)
            m.then_inc(n_t, 1)
            dve.wait_ge(n_t, n + 1)
            split_dve(dve, hi_no[n], tmp, hi, lo)

        def split_dve(dve, n, src, hi, lo):
            dve.wait_ge(n_hi, n + 1)
            TT(lo, src, hi.bitcast(F32), ALU.subtract).then_inc(n_lo, 1)

        def norm_act_hi(act, n, tmp, hi):
            act.wait_ge(n_t, n + 1)
            act_f(hi, tmp, ACT.Copy).then_inc(n_hi, 1)

        def norm_dve_post(dve, n, src, res, gain, w, inc):
            dve.wait_ge(n_std, n + 1)
            dlink(dve, nc.vector.reciprocal(g("rstd")[:, 0:w], g("rstd")[:, 0:w]))
            for k in range(KT):
                m = STT(out=src[:, k, :], in0=src[:, k, :], scalar=vec[:, gain + k:gain + k + 1],
                        in1=g("rstd")[:, 0:w], op0=ALU.mult, op1=ALU.mult)
            m.then_inc(n_t, 1)
            dve.wait_ge(n_t, n + 1)
            TT(res, res, src, ALU.add).then_inc(n_res, 1)

        hi_no = {0: 0}
        for c in range(CH):
            hi_no[chunk_no(0, c)] = 1 + c
            hi_no[chunk_no(2, c)] = 7 + c
            hi_no[chunk_no(4, c)] = 13 + c
        SPLIT_Y, SPLIT_OX = 4, 10

        def cs(c):
            return slice(NC * c, NC * c + NC)

        def lin_pe(pe, base, turn, xh, xl):
            with pe.Fori(0, KT // 4) as i:
                for s in range(4):
                    pe.wait_ge(w_ready, base + s + 1 + 4 * i)
                    for c in range(CH):
                        pe.wait_ge(lin_ev, 3 * KT * turn + 3 * s + c + 1 + 12 * i)
                        three(B[3 * (s % 2) + c][:, 0:NC],
                              [(whi[s][:, P * k:P * k + P], wlo[s][:, P * k:P * k + P], xh[:, k, cs(c)], xl[:, k, cs(c)])
                               for k in range(KT)], release=((0,) if c == 0 else ())).then_inc(lin_mm, 1)

        def lin_evac(eng, copy, turn, dst):
            for m in range(KT):
                for c in range(CH):
                    eng.wait_ge(lin_mm, 3 * (KT * turn + m) + c + 1)
                    copy(dst[:, m, cs(c)], B[3 * (m % 2) + c][:, 0:NC]).then_inc(lin_ev, 1)

        def tok(t):
            return slice(P * t, P * t + P)

        def bc(ap, shape):
            return ap.broadcast_to(shape)

        def tm_no(kind, jj, t):
            return 18 * kind + 9 * jj + t

        s_dt, s_dtm, s_dtu = sem("dt_ready"), sem("dt_mm"), sem("dt_act")
        s_wdt = sem("wdt_split")
        s_pad = sem("conv_pads")
        cv_done, xc_done, cv_out = sem("conv_done"), sem("xbc_ready"), sem("conv_out")
        (s_adb, s_p1, s_cols, s_exps, s_D, s_E, s_xb, s_mt, s_xdt, s_xdd, s_off, s_yd, s_stm, s_stu, s_yA, s_ysq,
         s_y, s_yt, s_yte) = (sem("ssd_" + n) for n in
                              ("adb", "first", "cols", "exps", "diff", "decay", "copies", "mixed", "xdt", "xdd", "yoff",
                               "ydiag", "states", "state", "yraw", "yrms", "ynorm", "ytrans", "yout"))
        ld_z = [sem(f"ld_z{i}") for i in range(2)]
        s_yo1, s_yo2, s_xb8, s_nb = sem("ssd_yoff_t"), sem("ssd_yoff_copy"), sem("ssd_xddb"), sem("ssd_newstate")
        s_nbm = sem("ssd_newstate_mm")
        ld_qk = [sem(f"ld_qk{i}") for i in range(2)]
        ld_v = sem("ld_v")
        a_tr, a_tre, a_S, a_nb, a_exp, a_att, a_T, a_Te, a_pv, a_o, a_on, a_yt, a_yte = (
            sem("att_" + n) for n in ("qk_trans", "qk_copy", "scores", "max", "exp", "probs", "ptrans", "pcopy", "pv",
                                      "ocopy", "onorm", "otrans", "oout"))
        ld_kb = [sem(f"ld_kc{i}") for i in range(2)]
        b_q, b_S, b_nb, b_exp, b_p, b_T, b_Te, b_pv, b_o, b_ot, b_ote = (
            sem("smp_" + n) for n in ("qbd", "scores", "max", "exp", "probs", "ptrans", "pcopy", "pv", "ocopy", "otrans",
                                      "otok"))
        ld_mkv, ld_cm = sem("ld_mem_kv"), sem("ld_cache_mem")
        x_S, x_nb, x_exp, x_p, x_T, x_Te, x_pv, x_o = (
            sem("x_" + n) for n in ("scores", "max", "exp", "probs", "ptrans", "pcopy", "pv", "out"))
        y_q, y_S, y_nb, y_exp, y_p, y_T, y_Te, y_pv, ys_o = (
            sem("xs_" + n) for n in ("qbd", "scores", "max", "exp", "probs", "ptrans", "pcopy", "pv", "out"))
        f_up, f_sg, f_hr, f_hh, f_hl, f_dn, f_de, f_acc = (
            sem("ffn_" + n) for n in ("up", "silu", "hidden", "high", "low", "down", "down_add", "acc_zero"))
        h_out, y_out = sem("h_store"), sem("y_store")
        rp_c, a_rs, ld_vs, y_z = sem("rope_chain"), sem("att_rms"), sem("ld_vs"), sem("xs_zero")

        block = ctx.enter_context(nc.Block())

        @block.sync
        def _(sp):
            sp.dma_start(g("mraw")[:], memT).then_inc(ld["mem"], 16)
            sp.dma_start(vec[:], vecs).then_inc(ld["vec"], 16)
            for i in range(2):
                sp.dma_start(raw[i][:], wall[i]).then_inc(w_raw[i], 16)
            for c in range(CH):
                sp.dma_start(g("H")[:, :, cs(c)], xT[:, :, cs(c)]).then_inc(ld[f"x{c}"], 16)
            sp.dma_start(row[:], rows.partition_broadcast(P)).then_inc(ld["row"], 16)
            sp.dma_start(cst[:], consts).then_inc(ld["cst"], 16)
            with sp.Fori(1, N_ITEMS // 2) as i:
                for s in range(2):
                    sp.wait_ge(w_ready, 2 * i + s - 1)
                    sp.dma_start(raw[s][:], wall[2 * i + s]).then_inc(w_raw[s], 16)

        @block.gpsimd
        def _(pool):
            pool.memset(one[:], 1.0).then_inc(w_hi, 1)
            pool.wait_ge(w_hi, 1)

            def split(n, s, first):
                pool.wait_ge(w_raw[s % 2], 16 * (n // 2 + 1) if first else (n - s % 2) * 8 + 16)
                if not first:
                    pool.wait_ge(w_used, n - 3)
                pool.tensor_tensor(whi[s][:], raw[s % 2][:], bc(one[:, 0:1], [P, WI]), ALU.mult).then_inc(w_hi, 1)
                pool.wait_ge(w_hi, n + 2)
                pool.tensor_tensor(wlo[s][:], raw[s % 2][:], whi[s][:].bitcast(F32), ALU.subtract).then_inc(w_ready, 1)

            for n in range(4):
                split(n, n, True)
            with pool.Fori(1, N_ITEMS // 4) as i:
                for s in range(4):
                    split(4 * i + s, s, False)
            for n in range(N_ITEMS // 4 * 4, N_ITEMS):
                split(n, n % 4, False)

        @block.tensor
        def _(pe):
            pe.wait_ge(setup, 1)
            norm_pe(pe, 0, MEM)
            pe.wait_ge(n_lo, 1)
            for m in range(KT):
                pe.wait_ge(w_ready, I_MK + m + 1)
                if m >= 6:
                    pe.wait_ge(mem_ev, m - 5)
                three(B[m % 6][:, 0:MEM], [(whi[m % 4][:, tok(k)], wlo[m % 4][:, tok(k)], g("mhi")[:, k, :], g("mlo")[:, k, :])
                                           for k in range(KT)], release=(0,) if m else ()).then_inc(mem_mm, 1)
            for c in range(CH):
                norm_pe(pe, chunk_no(0, c), NC)
            for j in range(4):
                s = 2 * (j % 2)
                pe.wait_ge(w_ready, I_MV + 2 * j + 2)
                for t in range(2):
                    n = KT + 2 * j + t
                    pe.wait_ge(mem_ev, n - 5)
                    three(B[n % 6][:, 0:256],
                          [(g("mhi")[:, k, tok(t)], g("mlo")[:, k, tok(t)],
                            whi[s + k // 4][:, 256 * (k % 4):256 * (k % 4) + 256],
                            wlo[s + k // 4][:, 256 * (k % 4):256 * (k % 4) + 256]) for k in range(KT)],
                          release=((0,) if t == 0 else (4,))).then_inc(mem_mm, 1)
            pe.wait_ge(mem_ev, 2 * KT)
            pe.wait_ge(n_lo, 1 + CH)
            with pe.Fori(0, 4) as i:
                for jj in range(2):
                    s = 2 * jj
                    pe.wait_ge(w_ready, I_TM + 2 * jj + 2 + 4 * i)
                    for t in range(NT):
                        pe.wait_ge(tm_ev, tm_no(0, jj, t) + 1 + 18 * i)
                        three(B[(9 * jj + t) % 6][:, 0:256],
                              [(g("NH")[:, k, tok(t)], g("NL")[:, k, tok(t)],
                                whi[s + k // 4][:, 256 * (k % 4):256 * (k % 4) + 256],
                                wlo[s + k // 4][:, 256 * (k % 4):256 * (k % 4) + 256]) for k in range(KT)],
                              release=((0,) if t == 0 else (4,) if t == NT - 1 else ())).then_inc(tm_mm, 1)
            pe.wait_ge(s_wdt, 1)
            for t in range(NT):
                m = three(B[6][:, SH * t:SH * t + SH],
                          [(g("NH")[:, k, tok(t)], g("NL")[:, k, tok(t)], g("wdh")[:, k, :], g("wdl")[:, k, :])
                           for k in range(KT)])
            m.then_inc(s_dtm, 1)
            pe.wait_ge(tm_ev, 6 + 72)
            lin_pe(pe, I_XB, 0, g("NH"), g("NL"))

            pe.wait_ge(xc_done, KT)
            pe.wait_ge(s_dt, 1)
            XC = g("XC")
            for t in range(NT):
                smp = t == NT - 1
                tri = cst[:, C_TS:C_TS + P] if smp else cst[:, C_TP:C_TP + P]
                blk = cst[:, C_BS:C_BS + P] if smp else ones[:, :]
                pe.wait_ge(s_adb, t + 1)
                if t:
                    pe.wait_ge(s_D, t)
                    pe.wait_ge(s_mt, t)
                    pe.wait_ge(s_xdt, t)
                    pe.wait_ge(s_xb, t)
                    pe.wait_ge(s_yte, t)
                for h in range(SH):
                    mm(B[h // 4][:, tok(h % 4)], g("adb")[:, h, :], tri, start=True, stop=True)
                mm(B[2][:, 256:264], tri, ad_t[:, t, :], start=True, stop=True)
                mm(B[2][:, 264:272], blk, ad_t[:, t, :], start=True, stop=True)
                if smp:
                    for b in range(DB):
                        mm(B[2][:, 272 + 8 * b:280 + 8 * b], bc(cst[:, C_BB + b:C_BB + b + 1], [P, P]), ad_t[:, t, :],
                           start=True, stop=True)
                for gr in range(2):
                    mm(B[2][:, tok(gr)], XC[:, 4 + gr, tok(t)], XC[:, 6 + gr, tok(t)], start=True, stop=True)
                for j in range(4):
                    nc.tensor.transpose(B[3][:, tok(j)], XC[:, j, tok(t)], ident)
                for j in range(2):
                    m = nc.tensor.transpose(B[4][:, tok(j)], XC[:, 4 + j, tok(t)], ident)
                m.then_inc(s_p1, 1)
                if t:
                    pe.wait_ge(s_yA, t)
                if not smp:
                    pe.wait_ge(s_stu, t + 1)
                    for gr in range(2):
                        m = mm(B[5][:, 256 * gr:256 * gr + 256], XC[:, 6 + gr, tok(t)], g("ST")[:, 256 * gr:256 * gr + 256],
                               start=True, stop=True)
                    m.then_inc(s_off, 1)
                else:
                    pe.wait_ge(ld["h0"], 16)
                    for b in range(DB):
                        for j in range(4):
                            lo = P * t + DS * b
                            m = mm(B[5][:, P * j + DS * b:P * j + DS * b + DS], g("h0t")[:, b, tok(j)],
                                   XC[:, 6 + j // 2, lo:lo + DS], start=True, stop=True)
                    m.then_inc(s_yo1, 1)
                    pe.wait_ge(s_yo2, 1)
                    for j in range(4):
                        m = nc.tensor.transpose(B[5][:, tok(j)], g("yoT")[:, tok(j)], ident)
                    m.then_inc(s_off, 1)
                pe.wait_ge(s_mt, t + 1)
                pe.wait_ge(s_xdt, t + 1)
                for h in range(SH):
                    m = mm(B[6][:, SP_ * h:SP_ * h + SP_], g("MT")[:, h, :], g("xdt")[:, SP_ * h:SP_ * h + SP_],
                           start=True, stop=True)
                m.then_inc(s_yd, 1)
                pe.wait_ge(s_xdd, t + 1)
                pe.wait_ge(s_xb, t + 1)
                if not smp:
                    for gr in range(2):
                        m = mm(B[7][:, 256 * gr:256 * gr + 256], g("Btm")[:, gr, :], g("xdd")[:, 256 * gr:256 * gr + 256],
                               start=True, stop=True)
                    m.then_inc(s_stm, 1)
                pe.wait_ge(s_y, t + 1)
                for j in range(4):
                    m = nc.tensor.transpose(B[4][:, tok(j)], g("yA")[:, tok(j)], ident)
                m.then_inc(s_yt, 1)
                if smp:
                    for b in range(DB):
                        pe.wait_ge(s_xb8, b + 1)
                        if b >= 2:
                            pe.wait_ge(s_nb, b - 1)
                        for gr in range(2):
                            m = mm(B[7 if b % 2 else 0][:, 256 * gr:256 * gr + 256], g("Btm")[:, gr, :],
                                   g("adb")[:].rearrange("p h q -> p (h q)")[:, 512 * (b % 2) + 256 * gr:512 * (b % 2) + 256 * gr + 256],
                                   start=True, stop=True)
                        m.then_inc(s_nbm, 1)

            for t in range(NT):
                for w in range(2):
                    n = 2 * t + w
                    pe.wait_ge(ld_qk[t % 2], 32 * (t // 2 + 1))
                    if n >= 2:
                        pe.wait_ge(a_tre, n - 1)
                    else:
                        pe.wait_ge(s_yA, NT)
                    for h in range(H):
                        m = nc.tensor.transpose(B[6 + w][:, tok(h)], g(f"qkr{t % 2}")[:, w, tok(h)], ident)
                    m.then_inc(a_tr, 1)
            pe.wait_ge(a_tre, 2 * NT)
            pe.wait_ge(ld_v, 16)
            pe.wait_ge(s_nb, DB)
            pe.wait_ge(s_yte, NT)

            def scores(u):
                t, h = divmod(u, H)
                W = P * (t + 1)
                for c in range(2):
                    if u:
                        pe.wait_ge(a_exp, 2 * (u - 1) + c + 1)
                    r = slice(64 * c, 64 * c + 64)
                    for w0 in range(0, W, 512):
                        w1 = min(W, w0 + 512)
                        m = mm(bank[c][:, w0:w1], g("QTt")[r, h, tok(t)], g("KTt")[r, h, w0:w1], start=True, stop=True)
                    m.then_inc(a_S, 1)

            def apply(u):
                t, h = divmod(u, H)
                pe.wait_ge(a_att, u + 1)
                if u:
                    pe.wait_ge(a_Te, u)
                for k in range(t + 1):
                    m = nc.tensor.transpose(B[4 + k // 4][:, tok(k % 4)], g("ATT")[:, tok(k)], ident)
                m.then_inc(a_T, 1)
                pe.wait_ge(a_Te, u + 1)
                if h == 0 and t:
                    pe.wait_ge(a_on, t)
                for k in range(t + 1):
                    m = mm(B[6][:, tok(h)], g("PTs")[:, tok(k)], g("V")[:, k, tok(h)], start=(k == 0), stop=(k == t))
                m.then_inc(a_pv, 1)

            def o_trans(t):
                pe.wait_ge(a_on, t + 1)
                if t:
                    pe.wait_ge(a_yte, t)
                for h in range(H):
                    m = nc.tensor.transpose(B[7][:, tok(h)], g("on")[:, tok(h)], ident)
                m.then_inc(a_yt, 1)

            U = H * (NT - 1)
            scores(0)
            for u in range(U):
                if u + 1 < U:
                    scores(u + 1)
                apply(u)
                if u % H == 1 and u > H:
                    o_trans(u // H - 1)
            o_trans(NT - 2)

            pe.wait_ge(b_q, 1)
            pe.wait_ge(a_exp, 2 * U)
            for b in range(DB):
                sl = b % 2
                pe.wait_ge(ld_kb[sl], 32 * (b // 2 + 1))
                if b >= 2:
                    pe.wait_ge(b_exp, b - 1)
                for h in range(H):
                    mm(B[sl][:, 0:PAST], g("Qbd")[:, b, h, :], g(f"Kb{sl}")[:, h, :], start=(h == 0), stop=(h == H - 1))
                for h in range(H):
                    m = mm(B[sl][:, PAST:PAST + DS], g("Qbd")[:, b, h, :], g("KTs")[:, h, DS * b:DS * b + DS],
                           start=(h == 0), stop=(h == H - 1))
                m.then_inc(b_S, 1)
                pe.wait_ge(b_p, b + 1)
                if b:
                    pe.wait_ge(b_Te, b)
                for k in range(2):
                    nc.tensor.transpose(B[2][:, tok(k)], g("Pp")[:, sl, tok(k)], ident)
                nc.tensor.transpose(B[2][:, tok(2)], g("Pn")[:, b, :], ident).then_inc(b_T, 1)
                pe.wait_ge(b_Te, b + 1)
                for h in range(H):
                    o = B[4 + b // 4][:, P * (b % 4) + 32 * h:P * (b % 4) + 32 * h + 32]
                    for k in range(2):
                        mm(o, g(f"Vb{sl}")[:, k, tok(h)], g("PTb")[:, k, 32 * h:32 * h + 32], start=(k == 0), stop=False)
                    m = mm(o, g("Vs")[:, tok(h)], g("PTb")[:, 2, 32 * h:32 * h + 32], start=False, stop=True)
                m.then_inc(b_pv, 1)
            pe.wait_ge(b_o, 1)
            for h in range(H):
                m = nc.tensor.transpose(B[6][:, tok(h)], g("oTs")[:, h, :], ident)
            m.then_inc(a_pv, 1)
            o_trans(NT - 1)

            def linear(base, turn, xh, xl, ready):
                pe.wait_ge(n_lo, ready)
                lin_pe(pe, base, turn, xh, xl)

            linear(I_WO, 1, g("YH"), g("NL"), SPLIT_Y + CH)
            for c in range(CH):
                norm_pe(pe, chunk_no(1, c), NC)
            for c in range(CH):
                norm_pe(pe, chunk_no(2, c), NC)
            linear(I_WQ, 2, g("NH"), g("NL"), 7 + CH)

            pe.wait_ge(lin_ev, 6 + 9 * KT)
            pe.wait_ge(ld_mkv, 32)
            QX = g("QX")
            for t in range(NT - 1):
                if t:
                    pe.wait_ge(x_exp, H * t)
                for h in range(H):
                    o = B[h // 2][:, MEM * (h % 2):MEM * (h % 2) + MEM]
                    for k in range(2):
                        m = mm(o, QX[:, 2 * h + k, tok(t)], g("mkT")[:, 2 * h + k, :], start=(k == 0), stop=(k == 1))
                m.then_inc(x_S, 1)
                pe.wait_ge(x_p, t + 1)
                if t:
                    pe.wait_ge(x_Te, t)
                for h in range(H):
                    for k in range(2):
                        m = nc.tensor.transpose(B[2 + h // 2][:, tok(2 * (h % 2) + k)], g("xE")[:, h, tok(k)], ident)
                m.then_inc(x_T, 1)
                pe.wait_ge(x_Te, t + 1)
                if t:
                    pe.wait_ge(x_o, t)
                for h in range(H):
                    for e in range(2):
                        for k in range(2):
                            m = mm(B[4 + h // 2][:, tok(2 * (h % 2) + e)], g("mvt")[:, k, tok(2 * h + e)],
                                   g("xPT")[:, tok(2 * h + k)], start=(k == 0), stop=(k == 1))
                m.then_inc(x_pv, 1)

            pe.wait_ge(y_q, 1)
            pe.wait_ge(x_exp, H * (NT - 1))
            pe.wait_ge(x_o, NT - 1)
            for b in range(DB):
                pe.wait_ge(ld_cm, 32 * (b + 1))
                if b:
                    pe.wait_ge(y_exp, b)
                for k in range(KT):
                    m = mm(B[0][0:64, 0:MEM], g("xQbd")[:, b, k, :], g("cK")[:, k, :], start=(k == 0), stop=(k == KT - 1))
                m.then_inc(y_S, 1)
                pe.wait_ge(y_p, b + 1)
                for k in range(2):
                    m = nc.tensor.transpose(B[1][:, 64 * k:64 * k + 64], g("sE")[:, tok(k)], ident[0:64, 0:64])
                m.then_inc(y_T, 1)
                pe.wait_ge(y_Te, b + 1)
                for h in range(H):
                    for e in range(2):
                        o = B[2 + b // 4][:, P * (b % 4) + DS * (2 * h + e):P * (b % 4) + DS * (2 * h + e) + DS]
                        for k in range(2):
                            m = mm(o, g("cV")[:, k, tok(2 * h + e)], g("sPT")[:, k, DS * h:DS * h + DS],
                                   start=(k == 0), stop=(k == 1))
                m.then_inc(y_pv, 1)
            linear(I_WX, 3, g("NH"), g("NL"), SPLIT_OX + CH)
            for c in range(CH):
                norm_pe(pe, chunk_no(3, c), NC)
            for c in range(CH):
                norm_pe(pe, chunk_no(4, c), NC)

            pe.wait_ge(n_lo, 16)
            NH, NL = g("NH"), g("NL")

            def up(g_no, n0, s0, ready):
                for f in range(2):
                    for w in range(2):
                        pe.wait_ge(w_ready, ready + 2 * f + w)
                        s = (s0 + 2 * f + w) % 4
                        for c in range(CH):
                            if w == 0:
                                pe.wait_ge(f_hr, n0 + 3 * f + c + 1)
                            m = three(B[3 * w + c][:, 0:NC],
                                      [(whi[s][:, tok(k)], wlo[s][:, tok(k)], NH[:, k, cs(c)], NL[:, k, cs(c)])
                                       for k in range(KT)], release=((0,) if c == 0 else ()))
                            m.then_inc(f_up, 1)

            def down(par, n0, s0, ready, hid):
                pe.wait_ge(w_ready, ready)
                pe.wait_ge(f_hl, hid)
                for m_ in range(KT):
                    for c in range(CH):
                        q = 3 * m_ + c
                        pe.wait_ge(f_de, n0 + q + 1)
                        last = q == 3 * KT - 1
                        three(B[6 + q % 2][:, 0:NC],
                              [(whi[(s0 + f) % 4][:, tok(m_)], wlo[(s0 + f) % 4][:, tok(m_)],
                                g(f"hid_h{par}{f}")[:, cs(c)], g(f"hid_l{par}{f}")[:, cs(c)]) for f in range(2)],
                              release=((0,) if q == 0 else (1,) if last else ())).then_inc(f_dn, 1)

            up(0, 0, 0, I_FF + 1)
            with pe.Fori(0, (NG - 1) // 2) as i:
                for x in range(2):
                    up(1 + x, 6 * (1 + x) + 12 * i, 2 * x, I_FF + 5 + 6 * x + 12 * i)
                    down(x, 24 * x + 48 * i, 2 * x, I_FF + 10 + 6 * x + 12 * i, 6 + 6 * x + 12 * i)
            down(0, 24 * (NG - 1), 0, N_ITEMS, 6 * NG)
            for c in range(CH):
                norm_pe(pe, chunk_no(5, c), NC)

        @block.scalar
        def _(act):
            H_, NH, NLf = g("H"), g("NH"), g("NLf")
            act.wait_ge(setup, 1)
            norm_act_sum(act, 0, g("mraw")[:], MEM, [(ld["mem"], 16)])
            norm_act_hi(act, 0, g("mraw")[:], g("mhi")[:])
            act.wait_ge(n_lo, 1)
            for m in range(KT):
                act.wait_ge(mem_mm, m + 1)
                act_f(g("mraw")[:, m, :], B[m % 6][:, 0:MEM], ACT.Copy).then_inc(mem_ev, 1)
            act.wait_ge(mem_ev, KT)
            act.dma_start(mk_o, g("mraw")[:]).then_inc(mem_out, 16)
            for c in range(CH):
                n = chunk_no(0, c)
                norm_act_sum(act, n, H_[:, :, cs(c)], NC, [(ld[f"x{c}"], 16)])
                norm_act_hi(act, n, NLf[:, :, cs(c)], NH[:, :, cs(c)])
            for j in range(4):
                for t in range(2):
                    n = KT + 2 * j + t
                    act.wait_ge(mem_mm, n + 1)
                    act_f(g("mvs")[:, t, 256 * j:256 * j + 256], B[n % 6][:, 0:256], ACT.Copy).then_inc(mem_ev, 1)
            act.wait_ge(mem_ev, 2 * KT)
            act.dma_start(mv_o.rearrange("(t p) c -> p t c", p=P), g("mvs")[:]).then_inc(mem_out, 16)
            act.wait_ge(n_lo, 1 + CH)
            act.dma_start(g("wdr")[:], wdt).then_inc(ld["wdt"], 16)
            act.wait_ge(ld["row"], 16)
            act.wait_ge(setup, 2)
            act_f(row[:, R_LAM:R_LAM + 2], row[:, R_LAM:R_LAM + 2], ACT.Exp).then_inc(s_dtu, 1)
            act_f(row[:, R_ALOG:R_ALOG + SH], row[:, R_ALOG:R_ALOG + SH], ACT.Exp).then_inc(s_dtu, 1)
            act.wait_ge(ld["wdt"], 16)
            act_f(g("wdh")[:], g("wdr")[:], ACT.Copy).then_inc(s_dtu, 1)
            act.wait_ge(mem_out, 32)
            dram = [zs_d, q_d, k_o, v_o]

            def store(kind, jj):
                j = 2 * kind + jj
                act.wait_ge(tm_ev, 6 + 9 * (j + 1))
                act.dma_start(dram[kind].rearrange("(t p) c -> p t c", p=P)[:, :, 256 * jj:256 * jj + 256],
                              g(f"stg{j % 4}")[:]).then_inc(st_out[j % 4], 16)

            for kind, f in ((0, ACT.Silu), (3, ACT.Copy)):
                for jj in range(2):
                    j = 2 * kind + jj
                    if kind == 3 and jj == 0:
                        store(1, 0)
                        store(1, 1)
                        store(2, 0)
                        store(2, 1)
                    if j >= 4:
                        act.wait_ge(st_out[j % 4], 16)
                    for t in range(NT):
                        n = tm_no(kind, jj, t)
                        act.wait_ge(tm_mm, n + 1)
                        act_f(g(f"stg{j % 4}")[:, t, :], B[(9 * jj + t) % 6][:, 0:256], f).then_inc(tm_ev, 1)
                    store(kind, jj)
            D6 = g("dts")
            act.wait_ge(s_dtm, 1)
            act.wait_ge(s_dt, 1)
            act_f(D6[:, :, 1], D6[:, :, 0], ACT.Abs).then_inc(s_dtu, 1)
            act.wait_ge(s_dtu, 4)
            act_f(D6[:, :, 2], D6[:, :, 1], ACT.Exp, scale=-1.0).then_inc(s_dtu, 1)
            act.wait_ge(s_dtu, 5)
            act_f(D6[:, :, 3], D6[:, :, 2], ACT.Ln, bias=1.0).then_inc(s_dtu, 1)
            act.wait_ge(s_dt, 2)
            act.dma_start(g("cvi")[:], sconv).then_inc(ld["scv"], 16)
            act.wait_ge(ld["scv"], 16)
            for i in range(4):
                act.wait_ge(st_out[i], 32)

            def xp_s(m):
                return g(f"xp{m % 2}")[:, 3 + SEQ:XP].rearrange("p (b s) -> p b s", b=DB)

            def silu(m):
                act.wait_ge(cv_done, m + 1)
                act_f(g("XC")[:, m, :], g("acc")[:], ACT.Silu).then_inc(xc_done, 1)

            for m in range(KT):
                if m >= 2:
                    act.wait_ge(cv_done, m - 1)
                act_f(xp_s(m)[:, :, 0:3], g("cvi")[:, m, :].rearrange("p (b s) -> p b s", b=DB), ACT.Copy)
                for c in range(CH):
                    act.wait_ge(lin_mm, 3 * m + c + 1)
                    src = B[3 * (m % 2) + c]
                    if c < 2:
                        act_f(g(f"xp{m % 2}")[:, 3 + NC * c:3 + NC * c + NC], src[:, 0:NC], ACT.Copy).then_inc(lin_ev, 1)
                    else:
                        w = SEQ - NC * c
                        act_f(g(f"xp{m % 2}")[:, 3 + NC * c:3 + SEQ], src[:, 0:w], ACT.Copy)
                        act_f(xp_s(m)[:, :, 3:], src[:, w:NC].rearrange("p (b s) -> p b s", b=DB), ACT.Copy).then_inc(lin_ev, 1)
                if m:
                    silu(m - 1)
            silu(KT - 1)
            act.dma_start(conv_o, g("cvo")[:]).then_inc(cv_out, 16)
            act.dma_start(g("h0t")[:], h0).then_inc(ld["h0"], 16)
            act.wait_ge(cv_out, 16)
            act.wait_ge(xc_done, KT)

            sm = g("sm")
            for t in range(NT):
                smp = t == NT - 1
                if t:
                    act.wait_ge(s_yA, t)
                act.dma_start(g("zt")[:], zs_d[P * t:P * t + P, :]).then_inc(ld_z[0], 16)
                act.wait_ge(s_p1, t + 1)
                if t:
                    act.wait_ge(s_stm, t)
                act_f(g("Btm")[:].rearrange("p a n -> p (a n)"), B[4][:, 0:256], ACT.Copy)
                act_f(g("xs")[:], B[3][:, :], ACT.Copy).then_inc(s_xb, 1)
                act.wait_ge(s_cols, t + 1)
                if smp:
                    act_f(sm[:, 48:112], sm[:, 48:112], ACT.Exp)
                act_f(sm[:, 24:48], sm[:, 0:24], ACT.Exp).then_inc(s_exps, 1)
                act.wait_ge(s_D, t + 1)
                act_f(g("E")[:], g("E")[:], ACT.Exp).then_inc(s_E, 1)
                if smp:
                    act.wait_ge(s_yo1, 1)
                    act_f(g("yoT")[:], B[5][:, :], ACT.Copy).then_inc(s_yo2, 1)
                act.wait_ge(s_yA, t + 1)
                for gr in range(2):
                    x = act_f(g("sqs")[:, 0:256], g("yA")[:, 256 * gr:256 * gr + 256], ACT.Square,
                              accum_out=sm[:, 112 + gr:113 + gr])
                    alink(act, x)
                alink(act, act_f(sm[:, 114:116], sm[:, 112:114], ACT.Ln, bias=eps5[:, :], scale=1.0 / 256))
                act_f(sm[:, 116:118], sm[:, 114:116], ACT.Exp, scale=-0.5).then_inc(s_ysq, 1)
                act.wait_ge(s_yt, t + 1)
                for j in range(4):
                    x = act_f(g("YT")[:, j, tok(t)], B[4][:, tok(j)], ACT.Copy, scale=vec[:, V_SSM + j:V_SSM + j + 1])
                x.then_inc(s_yte, 1)
                if t == NT - 2:
                    act.wait_ge(s_stu, t + 2)
                    act.dma_start(ssm_o[0], g("ST")[:]).then_inc(out_s, 16)
            act.wait_ge(s_nb, DB)
            act.dma_start(ssm_o[1:1 + DB].rearrange("b n q -> n b q"), g("h0t")[:]).then_inc(out_s, 16)
            act.wait_ge(out_s, 32)

            def load_qk(t):
                if t >= 2:
                    act.wait_ge(a_tr, 2 * t - 2)
                act.dma_start(g(f"qkr{t % 2}")[:, 0, :], q_d[P * t:P * t + P, :]).then_inc(ld_qk[t % 2], 16)
                act.dma_start(g(f"qkr{t % 2}")[:, 1, :], k_o[P * t:P * t + P, :]).then_inc(ld_qk[t % 2], 16)

            act.dma_start(g("V")[:], v_o.rearrange("(t p) c -> p t c", p=P)).then_inc(ld_v, 16)
            load_qk(0)
            load_qk(1)
            for t in range(NT):
                for w in range(2):
                    n = 2 * t + w
                    act.wait_ge(a_tr, n + 1)
                    if t < NT - 1:
                        dst = g("QTt" if w == 0 else "KTt")[:, :, tok(t)]
                    else:
                        dst = g("QTs" if w == 0 else "KTs")[:]
                    act_f(dst, B[6 + w][:, :].rearrange("p (h q) -> p h q", h=H), ACT.Copy).then_inc(a_tre, 1)
                if t + 2 < NT:
                    load_qk(t + 2)
            asm = g("at_sm")

            def exps(u):
                t, h = divmod(u, H)
                W = P * (t + 1)
                for c in range(2):
                    act.wait_ge(a_nb, 2 * u + c + 1)
                    if u:
                        act.wait_ge(a_att, u)
                    act_f(g(f"E{c}")[:, 0:W], bank[c][:, 0:W], ACT.Exp, bias=asm[:, c:c + 1], scale=0.125,
                          accum_out=asm[:, 2 + c:3 + c]).then_inc(a_exp, 1)

            def copy_pt(u):
                t = u // H
                act.wait_ge(a_T, u + 1)
                if u:
                    act.wait_ge(a_pv, u)
                W = P * (t + 1)
                for w0 in range(0, W, 512):
                    w1 = min(W, w0 + 512)
                    x = act_f(g("PTs")[:, w0:w1], B[4 + w0 // 512][:, 0:w1 - w0], ACT.Copy)
                x.then_inc(a_Te, 1)

            def o_norm(t):
                act.wait_ge(a_pv, 4 * (t + 1) if t < NT - 1 else U + 1)
                if t:
                    act.wait_ge(a_on, t)
                    act.wait_ge(a_yt, t)
                for h in range(H):
                    x = act_f(g("on")[:, tok(h)], B[6][:, tok(h)], ACT.Square, accum_out=asm[:, 8 + h:9 + h])
                    alink(act, x)
                alink(act, act_f(asm[:, 12:16], asm[:, 8:12], ACT.Ln, bias=eps5[:, :], scale=1.0 / DH))
                act_f(asm[:, 16:20], asm[:, 12:16], ACT.Exp, scale=-0.5).then_inc(a_rs, 1)

            def o_evac(t):
                act.wait_ge(a_yt, t + 1)
                act_f(g("YT")[:, 4:8, tok(t)], B[7][:, :].rearrange("p (h q) -> p h q", h=H), ACT.Copy,
                      scale=vec[:, V_SUB:V_SUB + 1]).then_inc(a_yte, 1)

            U = H * (NT - 1)
            exps(0)
            for u in range(U):
                if u + 1 < U:
                    exps(u + 1)
                copy_pt(u)
                if u % H == H - 1:
                    o_norm(u // H)
                if u % H == 1 and u > H:
                    o_evac(u // H - 1)
            o_evac(NT - 2)

            def load_kb(b):
                if b >= 2:
                    act.wait_ge(b_pv, b - 1)
                act.dma_start(g(f"Kb{b % 2}")[:], kc[b]).then_inc(ld_kb[b % 2], 16)
                act.dma_start(g(f"Vb{b % 2}")[:], vc[b].rearrange("(t p) c -> p t c", p=P)).then_inc(ld_kb[b % 2], 16)

            act.wait_ge(a_pv, U)
            load_kb(0)
            load_kb(1)
            act.dma_start(g("Vs")[:], v_o[SEQ:NTOK, :]).then_inc(ld_vs, 16)
            act.wait_ge(ld_vs, 16)
            for b in range(DB):
                act.wait_ge(b_nb, b + 1)
                act_f(g("Es")[:, :], B[b % 2][:, 0:PAST + DS], ACT.Exp, bias=asm[:, 0:1], scale=0.125,
                      accum_out=asm[:, 2:3]).then_inc(b_exp, 1)
                act.wait_ge(b_T, b + 1)
                act_f(g("PTb")[:].rearrange("p a n -> p (a n)"), B[2][:, 0:384], ACT.Copy).then_inc(b_Te, 1)
                if b + 2 < DB:
                    load_kb(b + 2)
            o_norm(NT - 1)
            o_evac(NT - 1)

            def split_act(s, src, hi, w=None):
                act_f(hi, src, ACT.Copy).then_inc(n_hi, 1)

            act.wait_ge(a_yte, NT)
            act.wait_ge(s_yte, NT)
            for c in range(CH):
                split_act(SPLIT_Y + c, g("YT")[:, :, cs(c)], g("YH")[:, :, cs(c)])
            lin_evac(act, lambda o, i: act_f(o, i, ACT.Copy), 1, g("MIX"))
            for c in range(CH):
                norm_act_sum(act, chunk_no(1, c), g("MIX")[:, :, cs(c)], NC, [(lin_ev, 6 + 6 * KT)])
            for c in range(CH):
                n = chunk_no(2, c)
                norm_act_sum(act, n, H_[:, :, cs(c)], NC, [(n_res, c + 1)])
                norm_act_hi(act, n, NLf[:, :, cs(c)], NH[:, :, cs(c)])
            lin_evac(act, lambda o, i: act_f(o, i, ACT.Copy), 2, g("QX"))

            act.wait_ge(lin_mm, 9 * KT)
            act.dma_start(g("mkT")[:], mk_o).then_inc(ld_mkv, 16)
            act.dma_start(g("mvt")[:], mv_o.rearrange("(t p) c -> p t c", p=P)).then_inc(ld_mkv, 16)
            act.dma_start(g("cK")[:], cmk[0]).then_inc(ld_cm, 16)
            act.dma_start(g("cV")[:], cmv[0].rearrange("(t p) c -> p t c", p=P)).then_inc(ld_cm, 16)
            xm = g("xm")
            for t in range(NT - 1):
                act.wait_ge(x_nb, t + 1)
                if t:
                    act.wait_ge(x_T, t)
                for h in range(H):
                    x = act_f(g("xE")[:, h, :], B[h // 2][:, MEM * (h % 2):MEM * (h % 2) + MEM], ACT.Exp,
                              bias=xm[:, 4 + h:5 + h], scale=1.0 / 16, accum_out=xm[:, 8 + h:9 + h])
                    x.then_inc(x_exp, 1)
                act.wait_ge(x_T, t + 1)
                if t:
                    act.wait_ge(x_pv, t)
                for j in range(2):
                    x = act_f(g("xPT")[:, 512 * j:512 * j + 512], B[2 + j][:, :], ACT.Copy)
                x.then_inc(x_Te, 1)
            for b in range(DB):
                act.wait_ge(y_nb, b + 1)
                act_f(g("sE")[:, :], B[0][0:64, 0:MEM], ACT.Exp, bias=xm[0:64, 1:2], scale=1.0 / 16,
                      accum_out=xm[0:64, 2:3]).then_inc(y_exp, 1)
                act.wait_ge(y_T, b + 1)
                act_f(g("sPT")[:].rearrange("p a n -> p (a n)"), B[1][:, 0:128], ACT.Copy).then_inc(y_Te, 1)
                if b + 1 < DB:
                    act.wait_ge(y_pv, b + 1)
                    act.dma_start(g("cK")[:], cmk[b + 1]).then_inc(ld_cm, 16)
                    act.dma_start(g("cV")[:], cmv[b + 1].rearrange("(t p) c -> p t c", p=P)).then_inc(ld_cm, 16)
            act.wait_ge(ys_o, 2)
            act.wait_ge(x_o, NT - 1)
            for c in range(CH):
                split_act(SPLIT_OX + c, g("QX")[:, :, cs(c)], NH[:, :, cs(c)])
            lin_evac(act, lambda o, i: act_f(o, i, ACT.Copy), 3, g("QX"))
            for c in range(CH):
                norm_act_sum(act, chunk_no(3, c), g("QX")[:, :, cs(c)], NC, [(lin_ev, 6 + 12 * KT)])
            for c in range(CH):
                n = chunk_no(4, c)
                norm_act_sum(act, n, H_[:, :, cs(c)], NC, [(n_res, CH + c + 1)])
                norm_act_hi(act, n, NLf[:, :, cs(c)], NH[:, :, cs(c)])
                act.dma_start(h_d[:, :, cs(c)], H_[:, :, cs(c)]).then_inc(h_out, 16)
            act.wait_ge(h_out, 16 * CH)

            for gi in range(NG):
                for f in range(2):
                    for c in range(CH):
                        n = 6 * gi + 3 * f + c
                        act.wait_ge(f_up, 2 * (n - c) + c + 1)
                        if n >= 2:
                            act.wait_ge(f_hr, 3 + n - 1)
                        act_f(g(f"sg{n % 2}")[:], B[c][:, 0:NC], ACT.Silu).then_inc(f_sg, 1)
                        act.wait_ge(f_hr, 3 + n + 1)
                        if c == 0 and f == 0 and gi >= 2:
                            act.wait_ge(f_dn, 24 * (gi - 1))
                        act_f(g(f"hid_h{gi % 2}{f}")[:, cs(c)], g(f"hr{n % 2}")[:], ACT.Copy).then_inc(f_hh, 1)
            act.wait_ge(f_dn, 24 * NG)
            act.dma_start(g("Hback")[:], h_d).then_inc(ld["Hb0"], 16)
            act.wait_ge(f_hl, 6 * NG)
            for c in range(CH):
                norm_act_sum(act, chunk_no(5, c), g("ACC")[:, :, cs(c)], NC, [(f_de, 2 + 24 * NG)])
            for c in range(CH):
                act.wait_ge(n_res, 2 * CH + c + 1)
                act.dma_start(y_o[:, :, cs(c)], g("Hback")[:, :, cs(c)]).then_inc(y_out, 16)
            act.wait_ge(y_out, 16 * CH)

        @block.vector
        def _(dve):
            link = lambda ins: dlink(dve, ins)
            H_, NH, NL, NLf = g("H"), g("NH"), g("NL"), g("NLf")
            nc.vector.memset(ones[:], 1.0)
            nc.vector.memset(eps6[:], 1e-6)
            nc.vector.memset(eps5[:], 1e-5).then_inc(setup, 1)
            nc.vector.memset(cred[:, 0:1], 0.0).then_inc(lin_ev, 6)
            nc.vector.memset(cred[:, 1:2], 0.0).then_inc(tm_ev, 6)
            nc.vector.memset(cred[:, 2:3], 0.0).then_inc(f_hr, 3)
            nc.vector.memset(cred[:, 3:4], 0.0).then_inc(f_de, 2)
            dve.wait_ge(ld["vec"], 16)
            norm_dve_pre(dve, 0, g("mraw"), g("mraw")[:], g("mlo")[:], g("mhi")[:], G_MEM, MEM)
            for c in range(CH):
                norm_dve_pre(dve, chunk_no(0, c), H_[:, :, cs(c)], NLf[:, :, cs(c)], NL[:, :, cs(c)], NH[:, :, cs(c)],
                             G_PREMIX, NC)
            dve.wait_ge(ld["row"], 16)
            lq = row[:, R_LAM:R_LAM + 256].rearrange("p (a b d) -> p a b d", a=2, b=2)
            link(TT(lq[:, :, 0, :], lq[:, :, 0, :], lq[:, :, 1, :], ALU.mult))
            link(nc.vector.tensor_reduce(lams[:], lq[:, :, 0, :], AX, ALU.add))
            CP(row[:, R_LAM:R_LAM + 2], lams[:]).then_inc(setup, 1)
            dve.wait_ge(s_dtu, 3)
            TT(g("wdl")[:], g("wdr")[:], g("wdh")[:].bitcast(F32), ALU.subtract).then_inc(s_wdt, 1)
            link(TT(nlam[:], row[:, R_LAM + 1:R_LAM + 2], row[:, R_LAM:R_LAM + 1], ALU.subtract))
            link(TS(nlam[:], nlam[:], -0.2, None, ALU.add))
            link(TS(row[:, R_ALOG:R_ALOG + SH], row[:, R_ALOG:R_ALOG + SH], -1.0, None, ALU.mult))
            dve.wait_ge(ld["cst"], 16)
            link(TT(coef[:], cst[:, C_C1:C_C1 + 1], nlam[:], ALU.mult))
            link(TT(coef[:], coef[:], cst[:, C_C0:C_C0 + 1], ALU.add))
            link(TS(vec[:, V_SUB:V_SUB + 1], vec[:, V_SUB:V_SUB + 1], 0.8, None, ALU.mult))
            for kind in (1, 2):
                for jj in range(2):
                    j = 2 * kind + jj
                    dve.wait_ge(tm_ev, 6 + 9 * j)
                    if j >= 4:
                        dve.wait_ge(st_out[j % 4], 16)
                    for t in range(NT):
                        n = tm_no(kind, jj, t)
                        dve.wait_ge(tm_mm, n + 1)
                        X = B[(9 * jj + t) % 6][:, 0:256].rearrange("p (g d) -> p g d", d=32)
                        cos = bc(cst[:, C_COS + 32 * t:C_COS + 32 * t + 32].unsqueeze(1), [P, 8, 32])
                        sin = bc(cst[:, C_SIN + 32 * t:C_SIN + 32 * t + 32].unsqueeze(1), [P, 8, 32])
                        A = g("rpA")[:].rearrange("p (g d) -> p g d", d=32)
                        R = g("rpB")[:].rearrange("p (g d) -> p g d", d=32)
                        TT(A, X, cos, ALU.mult)
                        TT(R, X, sin, ALU.mult).then_inc(rp_c, 1)
                        dve.wait_ge(rp_c, 2 * (n - 18) + 1)
                        A4 = g("rpA")[:].rearrange("p (g x d) -> p g x d", x=2, d=32)
                        R4 = g("rpB")[:].rearrange("p (g x d) -> p g x d", x=2, d=32)
                        O4 = g(f"stg{j % 4}")[:, t, :].rearrange("p (g x d) -> p g x d", x=2, d=32)
                        TT(O4[:, :, 0, :], A4[:, :, 0, :], R4[:, :, 1, :], ALU.subtract).then_inc(rp_c, 1)
                        TT(O4[:, :, 1, :], A4[:, :, 1, :], R4[:, :, 0, :], ALU.add).then_inc(tm_ev, 1)
                        dve.wait_ge(tm_ev, 6 + n + 1)
            D6 = g("dts")
            dve.wait_ge(s_dtm, 1)
            TT(D6[:, :, 0].rearrange("p (t h) -> p t h", h=SH), B[6][:, 0:72].rearrange("p (t h) -> p t h", h=SH),
               bc(row[:, R_DTB:R_DTB + SH].unsqueeze(1), [P, NT, SH]), ALU.add).then_inc(s_dt, 1)
            dve.wait_ge(s_dtu, 6)
            u, e, ln = D6[:, :, 0], D6[:, :, 2], D6[:, :, 3]
            t1, t2 = D6[:, :, 4], D6[:, :, 5]
            link(TS(t1, e, 1.0, None, ALU.add))
            link(TS(t1, t1, -1.0, 1e-30, ALU.add, ALU.max))
            link(nc.vector.reciprocal(t2, t1))
            link(TT(t2, t2, e, ALU.mult))
            link(TT(t2, t2, ln, ALU.mult))
            link(TS(t1, e, 5.9e-8, None, ALU.min))
            link(TT(t2, t2, t1, ALU.max))
            link(TS(t1, u, 0.0, None, ALU.max))
            link(TT(dt_t[:].rearrange("p t h -> p (t h)"), t1, t2, ALU.add))
            TT(ad_t[:], dt_t[:], bc(row[:, R_ALOG:R_ALOG + SH].unsqueeze(1), [P, NT, SH]), ALU.mult).then_inc(s_dt, 1)
            dve.wait_ge(s_dt, 2)
            for i in range(2):
                link(nc.vector.memset(g(f"xp{i}")[:, 0:3], 0.0))
            acc = g("acc")
            accs = acc[:, SEQ:NTOK].rearrange("p (b s) -> p b s", b=DB)
            for m in range(KT):
                x = g(f"xp{m % 2}")
                xs_ = x[:, 3 + SEQ:XP].rearrange("p (b s) -> p b s", b=DB)
                dve.wait_ge(lin_ev, 6 + 3 * (m + 1))
                if m:
                    dve.wait_ge(xc_done, m)
                w = [vec[:, V_CW + 4 * m + j:V_CW + 4 * m + j + 1] for j in range(4)]
                cb = vec[:, V_CB + m:V_CB + m + 1]
                TS(acc[:, 0:SEQ], x[:, 0:SEQ], w[0], cb, ALU.mult, ALU.add)
                link(TS(accs, xs_[:, :, 0:DS], w[0], cb, ALU.mult, ALU.add))
                for j in range(1, 4):
                    STT(out=acc[:, 0:SEQ], in0=x[:, j:j + SEQ], scalar=w[j], in1=acc[:, 0:SEQ], op0=ALU.mult, op1=ALU.add)
                    if j < 3:
                        link(STT(out=accs, in0=xs_[:, :, j:j + DS], scalar=w[j], in1=accs, op0=ALU.mult, op1=ALU.add))
                    else:
                        STT(out=accs, in0=xs_[:, :, j:j + DS], scalar=w[j], in1=accs, op0=ALU.mult, op1=ALU.add)
                CP(g("cvo")[:, m, 0:3], x[:, SEQ:SEQ + 3])
                CP(g("cvo")[:, m, 3:27].rearrange("p (b s) -> p b s", b=DB), xs_[:, :, DS:DS + 3]).then_inc(cv_done, 1)

            dve.wait_ge(xc_done, KT)
            dve.wait_ge(cv_out, 16)
            sm, E, MT, yA, xs, xdt, xdd, ST = (g(n) for n in ("sm", "E", "MT", "yA", "xs", "xdt", "xdd", "ST"))

            def heads(ap):
                return ap.rearrange("p (h q) -> p h q", h=SH)

            nc.vector.memset(ST[:], 0.0).then_inc(s_stu, 1)
            for t in range(NT):
                smp = t == NT - 1
                tri = cst[:, C_TS:C_TS + P] if smp else cst[:, C_TP:C_TP + P]
                CP(g("adb")[:], bc(ad_t[:, t, :].unsqueeze(2), [P, SH, P])).then_inc(s_adb, 1)
                dve.wait_ge(s_p1, t + 1)
                if smp:
                    CP(sm[:, 48:112], B[2][:, 272:336])
                link(CP(sm[:, 0:16], B[2][:, 256:272]))
                TT(sm[:, 16:24], sm[:, 8:16], sm[:, 0:8], ALU.subtract).then_inc(s_cols, 1)
                for h in range(SH):
                    m = TS(E[:, h, :], B[h // 4][:, tok(h % 4)], sm[:, h:h + 1], 0.0, ALU.subtract, ALU.min)
                m.then_inc(s_D, 1)
                dve.wait_ge(s_xb, t + 1)
                TT(heads(xdt[:]), heads(xs[:]), bc(dt_t[:, t, :].unsqueeze(2), [P, SH, SP_]), ALU.mult).then_inc(s_xdt, 1)
                dve.wait_ge(s_xdt, t + 1)
                dve.wait_ge(s_exps, t + 1)
                TT(heads(xdd[:]), heads(xdt[:]), bc(sm[:, 40:48].unsqueeze(2), [P, SH, SP_]), ALU.mult).then_inc(s_xdd, 1)
                link(TT(g("cbm")[:], B[2][:, 0:256].rearrange("p (a l) -> p a l", a=2), bc(tri.unsqueeze(1), [P, 2, P]), ALU.mult))
                dve.wait_ge(s_E, t + 1)
                TT(MT[:].rearrange("p (a r) l -> p a r l", a=2), E[:].rearrange("p (a r) l -> p a r l", a=2),
                   bc(g("cbm")[:].unsqueeze(2), [P, 2, 4, P]), ALU.mult).then_inc(s_mt, 1)
                dve.wait_ge(s_off, t + 1)
                link(TT(heads(yA[:]), heads(B[5][:, :]), bc(sm[:, 24:32].unsqueeze(2), [P, SH, SP_]), ALU.mult))
                link(TT(heads(xs[:]), heads(xs[:]), bc(row[:, R_DSK:R_DSK + SH].unsqueeze(2), [P, SH, SP_]), ALU.mult))
                if not smp:
                    link(TT(heads(ST[:]), heads(ST[:]), bc(sm[:, 32:40].unsqueeze(2), [P, SH, SP_]), ALU.mult))
                dve.wait_ge(s_yd, t + 1)
                link(TT(yA[:], yA[:], B[6][:, :], ALU.add))
                if not smp:
                    dve.wait_ge(s_stm, t + 1)
                    TT(ST[:], ST[:], B[7][:, :], ALU.add).then_inc(s_stu, 1)
                link(TT(yA[:], yA[:], xs[:], ALU.add))
                dve.wait_ge(ld_z[0], 16 * (t + 1))
                TT(yA[:], yA[:], g("zt")[:], ALU.mult).then_inc(s_yA, 1)
                dve.wait_ge(s_yA, t + 1)
                dve.wait_ge(s_ysq, t + 1)
                TT(yA[:].rearrange("p (a q) -> p a q", a=2), yA[:].rearrange("p (a q) -> p a q", a=2),
                   bc(sm[:, 116:118].unsqueeze(2), [P, 2, 256]), ALU.mult).then_inc(s_y, 1)
                dve.wait_ge(s_yt, t + 1)
                if smp:
                    adf = g("adb")[:].rearrange("p h q -> p (h q)")

                    def part(b):
                        if b >= 2:
                            dve.wait_ge(s_nbm, b - 1)
                        TS(adf[:, 512 * (b % 2):512 * (b % 2) + 512], xdd[:], cst[:, C_BB + b:C_BB + b + 1], None,
                           ALU.mult).then_inc(s_xb8, 1)
                    part(0)
                    for b in range(DB):
                        if b + 1 < DB:
                            part(b + 1)
                        hb = g("h0t")[:, b, :]
                        link(TT(heads(hb), heads(hb), bc(sm[:, 48 + 8 * b:56 + 8 * b].unsqueeze(2), [P, SH, SP_]), ALU.mult))
                        dve.wait_ge(s_nbm, b + 1)
                        TT(hb, hb, B[7 if b % 2 else 0][:, :], ALU.add).then_inc(s_nb, 1)

            asm = g("at_sm")
            E0, E1, ATT = g("E0"), g("E1"), g("ATT")

            def maxes(u):
                t, h = divmod(u, H)
                W = P * (t + 1)
                for c in range(2):
                    dve.wait_ge(a_S, 2 * u + c + 1)
                    link(nc.vector.memset(bank[c][0:64, W - 64:W], BIG))
                    link(nc.vector.tensor_reduce(asm[:, 4 + c:5 + c], bank[c][:, 0:W], AX, ALU.max))
                    if u:
                        dve.wait_ge(a_exp, 2 * (u - 1) + c + 1)
                    TS(asm[:, c:c + 1], asm[:, 4 + c:5 + c], -0.125, None, ALU.mult).then_inc(a_nb, 1)

            def probs(u):
                t, h = divmod(u, H)
                W = P * (t + 1)
                dve.wait_ge(a_exp, 2 * u + 2)
                link(nc.vector.reciprocal(asm[:, 6:8], asm[:, 2:4]))
                link(TT(asm[:, 7:8], asm[:, 7:8], nlam[:, :], ALU.mult))
                if u:
                    dve.wait_ge(a_T, u)
                link(TS(ATT[:, 0:W], E0[:, 0:W], asm[:, 6:7], None, ALU.mult))
                STT(out=ATT[:, 0:W], in0=E1[:, 0:W], scalar=asm[:, 7:8], in1=ATT[:, 0:W], op0=ALU.mult,
                    op1=ALU.add).then_inc(a_att, 1)

            def o_scale(t):
                dve.wait_ge(a_rs, t + 1)
                if t:
                    dve.wait_ge(a_yt, t)
                TT(g("on")[:].rearrange("p (h e) -> p h e", h=H), B[6][:, :].rearrange("p (h e) -> p h e", h=H),
                   bc(asm[:, 16:20].unsqueeze(2), [P, H, DH]), ALU.mult).then_inc(a_on, 1)

            U = H * (NT - 1)
            dve.wait_ge(out_s, 32)
            dve.wait_ge(a_tre, 2 * NT)
            maxes(0)
            for u in range(U):
                probs(u)
                if u + 1 < U:
                    maxes(u + 1)
                if u % H == H - 1:
                    o_scale(u // H)

            dve.wait_ge(a_pv, U)
            nc.vector.memset(g("Pn")[:], 0.0)
            link(nc.vector.memset(g("Qbd")[:], 0.0))
            for h in range(H):
                for c in range(2):
                    r = slice(64 * c, 64 * c + 64)
                    m = CP(g("Qbd")[r, :, h, 32 * h + 16 * c:32 * h + 16 * c + 16],
                           g("QTs")[r, h, :].rearrange("p (b q) -> p b q", b=DB))
            m.then_inc(b_q, 1)
            for b in range(DB):
                dve.wait_ge(b_S, b + 1)
                if b:
                    dve.wait_ge(b_T, b)
                link(nc.vector.tensor_reduce(asm[:, 4:5], B[b % 2][:, 0:PAST + DS], AX, ALU.max))
                TS(asm[:, 0:1], asm[:, 4:5], -0.125, None, ALU.mult).then_inc(b_nb, 1)
                dve.wait_ge(b_exp, b + 1)
                link(nc.vector.reciprocal(asm[:, 6:7], asm[:, 2:3]))
                link(TT(asm[:, 6:7], asm[:, 6:7], coef[:, :], ALU.mult))
                TS(g("Pp")[:, b % 2, :], g("Es")[:, 0:PAST], asm[:, 6:7], None, ALU.mult)
                TS(g("Pn")[:, b, DS * b:DS * b + DS], g("Es")[:, PAST:PAST + DS], asm[:, 6:7], None, ALU.mult).then_inc(b_p, 1)
            dve.wait_ge(b_pv, DB)
            for i in range(2):
                o5 = B[4 + i][:, :].rearrange("p (b h c q) -> p b h c q", b=4, h=H, c=2)
                ot = g("oTs")[:, :, 64 * i:64 * i + 64].rearrange("p h (b q) -> p b h q", b=4)
                link(CP(ot, o5[:, :, :, 0, :]))
                m = TT(ot, ot, o5[:, :, :, 1, :], ALU.add)
                if i:
                    m.then_inc(b_o, 1)
            o_scale(NT - 1)

            for c in range(CH):
                split_dve(dve, SPLIT_Y + c, g("YT")[:, :, cs(c)], g("YH")[:, :, cs(c)], NL[:, :, cs(c)])
            for c in range(CH):
                norm_dve_post(dve, chunk_no(1, c), g("MIX")[:, :, cs(c)], H_[:, :, cs(c)], G_POSTMIX, NC, None)
            for c in range(CH):
                norm_dve_pre(dve, chunk_no(2, c), H_[:, :, cs(c)], NLf[:, :, cs(c)], NL[:, :, cs(c)], NH[:, :, cs(c)],
                             G_PREX, NC)

            xm = g("xm")
            QX = g("QX")
            dve.wait_ge(lin_ev, 6 + 9 * KT)
            nc.vector.memset(g("xQbd")[:], 0.0).then_inc(y_z, 1)
            dve.wait_ge(y_z, 1)
            for h in range(H):
                for k in range(2):
                    m = CP(g("xQbd")[:, :, 2 * h + k, DS * h:DS * h + DS],
                           QX[:, 2 * h + k, SEQ:NTOK].rearrange("p (b q) -> p b q", b=DB))
            m.then_inc(y_q, 1)

            def x_evac(t):
                dve.wait_ge(x_pv, t + 1)
                for j in range(2):
                    m = CP(QX[:, 4 * j:4 * j + 4, tok(t)], B[4 + j][:, :].rearrange("p (a q) -> p a q", a=4))
                m.then_inc(x_o, 1)

            for t in range(NT - 1):
                dve.wait_ge(x_S, t + 1)
                for j in range(2):
                    m = nc.vector.tensor_reduce(xm[:, 2 * j:2 * j + 2], B[j][:, :].rearrange("p (a n) -> p a n", a=2), AX, ALU.max)
                link(m)
                TS(xm[:, 4:8], xm[:, 0:4], -1.0 / 16, None, ALU.mult).then_inc(x_nb, 1)
                dve.wait_ge(x_exp, H * (t + 1))
                link(nc.vector.reciprocal(xm[:, 12:16], xm[:, 8:12]))
                TT(g("xE")[:], g("xE")[:], bc(xm[:, 12:16].unsqueeze(2), [P, H, MEM]), ALU.mult).then_inc(x_p, 1)
                x_evac(t)
            for b in range(DB):
                dve.wait_ge(y_S, b + 1)
                link(nc.vector.tensor_reduce(xm[0:64, 0:1], B[0][0:64, 0:MEM], AX, ALU.max))
                TS(xm[0:64, 1:2], xm[0:64, 0:1], -1.0 / 16, None, ALU.mult).then_inc(y_nb, 1)
                dve.wait_ge(y_exp, b + 1)
                link(nc.vector.reciprocal(xm[0:64, 3:4], xm[0:64, 2:3]))
                TS(g("sE")[:], g("sE")[:], xm[0:64, 3:4], None, ALU.mult).then_inc(y_p, 1)
            dve.wait_ge(y_pv, DB)
            for i in range(2):
                CP(QX[:, :, SEQ + 64 * i:SEQ + 64 * i + 64].rearrange("p a (b q) -> p b a q", b=4),
                   B[2 + i][:, :].rearrange("p (b a q) -> p b a q", b=4, a=KT)).then_inc(ys_o, 1)
            for c in range(CH):
                split_dve(dve, SPLIT_OX + c, QX[:, :, cs(c)], NH[:, :, cs(c)], NL[:, :, cs(c)])
            for c in range(CH):
                norm_dve_post(dve, chunk_no(3, c), QX[:, :, cs(c)], H_[:, :, cs(c)], G_POSTX, NC, None)
            for c in range(CH):
                norm_dve_pre(dve, chunk_no(4, c), H_[:, :, cs(c)], NLf[:, :, cs(c)], NL[:, :, cs(c)], NH[:, :, cs(c)],
                             G_PREF, NC)

            ACC = g("ACC")
            nc.vector.memset(ACC[:], 0.0).then_inc(f_acc, 1)
            dve.wait_ge(h_out, 16 * CH)
            dve.wait_ge(f_acc, 1)

            def hidden(gi):
                for f in range(2):
                    for c in range(CH):
                        n = 6 * gi + 3 * f + c
                        dve.wait_ge(f_sg, n + 1)
                        dve.wait_ge(f_up, 2 * (n - c) + 3 + c + 1)
                        if n >= 2:
                            dve.wait_ge(f_hh, n - 1)
                        TT(g(f"hr{n % 2}")[:], g(f"sg{n % 2}")[:], B[3 + c][:, 0:NC], ALU.mult).then_inc(f_hr, 1)
                        dve.wait_ge(f_hh, n + 1)
                        TT(g(f"hid_l{gi % 2}{f}")[:, cs(c)], g(f"hr{n % 2}")[:],
                           g(f"hid_h{gi % 2}{f}")[:, cs(c)].bitcast(F32), ALU.subtract).then_inc(f_hl, 1)

            def add_down(gi):
                for q in range(3 * KT):
                    dve.wait_ge(f_dn, 24 * gi + q + 1)
                    a = ACC[:, q // 3, cs(q % 3)]
                    TT(a, a, B[6 + q % 2][:, 0:NC], ALU.add).then_inc(f_de, 1)

            hidden(0)
            for gi in range(1, NG):
                hidden(gi)
                add_down(gi - 1)
            add_down(NG - 1)
            dve.wait_ge(ld["Hb0"], 16)
            for c in range(CH):
                norm_dve_post(dve, chunk_no(5, c), ACC[:, :, cs(c)], g("Hback")[:, :, cs(c)], G_POSTF, NC, None)


def _consts():
    p = np.arange(P)
    c = np.zeros((P, C_END), np.float32)
    c[:, C_ID:C_ID + P] = np.eye(P)
    c[:, C_TP:C_TP + P] = p[:, None] <= p[None, :]
    same = p[:, None] // DS == p[None, :] // DS
    c[:, C_TS:C_TS + P] = same & (p[:, None] <= p[None, :])
    c[:, C_BS:C_BS + P] = same
    c[:, C_BB:C_BB + DB] = p[:, None] // DS == np.arange(DB)
    c[:, C_C1] = p // DS % 2
    c[:, C_C0] = 1 - c[:, C_C1]
    pos = np.concatenate([np.arange(SEQ), PAST + np.arange(NS) % DS]).astype(np.float32)
    inv = np.power(np.float32(10000.0), -np.arange(0, 64, 2, dtype=np.float32) / np.float32(64))
    ang = (pos[:, None] * inv[None, :]).astype(np.float32).reshape(NT, P, 32).transpose(1, 0, 2).reshape(P, -1)
    c[:, C_COS:C_COS + 288] = np.cos(ang.astype(np.float64))
    c[:, C_SIN:C_SIN + 288] = np.sin(ang.astype(np.float64))
    return c


def kernel(x_prompt, x_sample, cache_attn_k, cache_attn_v, state_ssm, state_conv, cache_mem_k, cache_mem_v,
           mem_prompt, w_in, conv_w, conv_b, dt_bias, a_log, d_skip, ssm_norm_w,
           lam_q1, lam_k1, lam_q2, lam_k2, subln_w, w_out, g_mem, wq_x, wk_x, wv_x, wo_x,
           g_pre_mix, g_post_mix, g_pre_x, g_post_x, g_pre_ffn, g_post_ffn, w_gate, w_up, w_down):
    import concourse.bacc as _bacc
    from concourse.bass_utils import run_bass_kernel_spmd as _run

    A = np.asarray

    def feat(x):
        x = A(x)
        return x.T.reshape(-1, P, x.shape[0]).transpose(1, 0, 2)

    def fm(w):
        w = A(w)
        return w.reshape(w.shape[0] // P, P, -1, P).transpose(2, 1, 0, 3).reshape(-1, P, WI)

    def tm(w):
        w = A(w)
        return w.reshape(2, 4, P, -1, 256).transpose(3, 0, 2, 1, 4).reshape(-1, P, WI)

    x = np.concatenate([A(x_prompt)[0], A(x_sample).reshape(NS, D)])
    wi = A(w_in)[0]
    q0 = 512 + 1024 + 8
    gate, upw, down = fm(A(w_gate)[0]), fm(A(w_up)[0]), A(w_down)[0].reshape(FT, P, D)
    ups = [np.stack([gate[2 * g], upw[2 * g], gate[2 * g + 1], upw[2 * g + 1]]) for g in range(NG)]
    downs = [down[2 * g:2 * g + 2] for g in range(NG)]
    ff = [ups[0]]
    for g in range(1, NG):
        ff += [ups[g], downs[g - 1]]
    ff.append(downs[-1])
    wall = np.concatenate([fm(A(wk_x)[0]), tm(A(wv_x)[0]), tm(np.concatenate([wi[:, 0:512], wi[:, q0:]], axis=1)),
                           fm(wi[:, 512:1536]), fm(A(w_out)[0]), fm(A(wq_x)[0]), fm(A(wo_x)[0])] + ff)
    gains = [A(v)[0].reshape(KT, P).T for v in (g_mem, g_pre_mix, g_post_mix, g_pre_x, g_post_x, g_pre_ffn, g_post_ffn)]
    vecs = np.concatenate(gains + [A(conv_w)[0].T.reshape(KT, P, 4).transpose(1, 0, 2).reshape(P, 32),
                                   A(conv_b)[0].reshape(KT, P).T, A(ssm_norm_w)[0].reshape(4, P).T,
                                   A(subln_w)[0].reshape(P, 1)], axis=1)
    rows = np.concatenate([A(v)[0] for v in (dt_bias, a_log, d_skip, lam_q1, lam_k1, lam_q2, lam_k2)])
    arrays = {
        "xT": feat(x),
        "memT": feat(A(mem_prompt)[0]),
        "wall": wall,
        "wdt": wi[:, 1536:1544].reshape(KT, P, 8).transpose(1, 0, 2),
        "consts": _consts(),
        "vecs": vecs,
        "rows": rows,
        "kc": A(cache_attn_k)[0].reshape(DB, PAST, H, DH).transpose(0, 3, 2, 1),
        "vc": A(cache_attn_v)[0].reshape(DB, PAST, 512),
        "h0": A(state_ssm)[0].reshape(DB, 512, P).transpose(2, 0, 1),
        "sconv": A(state_conv)[0].reshape(DB, 3, KT, P).transpose(3, 2, 0, 1).reshape(P, KT, 24),
        "cmk": A(cache_mem_k)[0].reshape(DB, MEM, KT, P).transpose(0, 3, 2, 1),
        "cmv": A(cache_mem_v)[0].reshape(DB, MEM, D),
    }
    arrays = {k: np.ascontiguousarray(v) for k, v in arrays.items()}
    outs = {"y": (P, KT, NTOK), "k": (NTOK, 512), "v": (NTOK, 512), "ssm": (1 + DB, P, 512), "conv": (P, KT, 27),
            "mk": (P, KT, MEM), "mv": (MEM, D)}
    scratch = {"zs": (NTOK, 512), "q": (NTOK, 512), "h": (P, KT, NTOK)}
    nc = _bacc.Bacc("TRN2", target_bir_lowering=False, num_devices=1)
    args = [nc.dram_tensor("in_" + k, a.shape, mybir.dt.from_np(a.dtype), kind="ExternalInput").ap()
            for k, a in arrays.items()]
    args += [nc.dram_tensor("out_" + k, s, F32, kind="ExternalOutput").ap() for k, s in outs.items()]
    args += [nc.dram_tensor("scratch_" + k, s, F32, kind="Internal").ap() for k, s in scratch.items()]
    build(nc, *args)
    r = _run(nc, [{"in_" + k: a for k, a in arrays.items()}], core_ids=[0]).results[0]
    o = {k: r["out_" + k] for k in outs}
    y = o["y"].transpose(2, 1, 0).reshape(NTOK, D)
    conv = o["conv"].transpose(2, 1, 0).reshape(27, D)
    ssm = o["ssm"].transpose(0, 2, 1).reshape(1 + DB, SH, SP_, P)
    return (y[:SEQ][None], y[SEQ:].reshape(DB, DS, D),
            o["k"][:SEQ].reshape(1, 1, SEQ, 4, 2, 64), o["v"][:SEQ].reshape(1, 1, SEQ, 4, 128),
            ssm[:1][None], conv[:3].reshape(1, 1, 3, D),
            o["mk"].transpose(2, 1, 0).reshape(1, 1, MEM, 4, 256), o["mv"].reshape(1, 1, MEM, 4, 256),
            o["k"][SEQ:].reshape(1, DB, DS, 4, 2, 64), o["v"][SEQ:].reshape(1, DB, DS, 4, 128),
            ssm[1:][None], conv[3:].reshape(1, DB, 3, D))
```

```python
from contextlib import ExitStack

import numpy as np

import concourse.bass as bass
from concourse import mybir

P = 128
D = 1024
KT = D // P
SEQ, DB, DS, PAST, MEM = 1024, 8, 16, 256, 256
NS = DB * DS
NTOK = SEQ + NS
NT = NTOK // P
NC = 384
CH = NTOK // NC
FT = 2816 // P
NG = FT // 2
H, DH = 4, 128
SH, SP_ = 8, 64
XP = 3 + SEQ + DB * (3 + DS)
WI = 1024
BIG = -1e30

F32 = mybir.dt.float32
F32R = mybir.dt.float32r
ALU = mybir.AluOpType
ACT = mybir.ActivationFunctionType
AX = mybir.AxisListType.X

I_TM, I_XB, I_WO, I_WQ, I_WX, I_FF = 0, 32, 40, 48, 56, 64
N_ITEMS = I_FF + 6 * NG

C_ID, C_TP, C_TS, C_BS, C_BB, C_COS, C_SIN = 0, 128, 256, 384, 512, 520, 808
C_C0, C_C1 = 1096, 1097
C_END = 1098
G_MEM, G_PREMIX, G_POSTMIX, G_PREX, G_POSTX, G_PREF, G_POSTF = (8 * i for i in range(7))
V_CW = 56
V_CB = 88
V_SSM = 96
V_SUB = 100
V_END = 101
R_DTB, R_ALOG, R_DSK, R_LAM = 0, 8, 16, 24
R_END = 280


def build(nc, xT, memT, wall, wdt, consts, vecs, rows, kc, vc, h0, sconv, cmk, cmv,
          y_o, k_o, v_o, ssm_o, conv_o, mk_o, mv_o, zs_d, q_d, h_d):
    with ExitStack() as ctx:
        def sb(name, shape, dt=F32):
            return ctx.enter_context(nc.sbuf_tensor(name, shape, dt))

        def sem(name):
            return ctx.enter_context(nc.semaphore(name))

        raw = [sb(f"w_raw{i}", [P, WI]) for i in range(2)]
        whi = [sb(f"w_hi{i}", [P, WI], F32R) for i in range(4)]
        wlo = [sb(f"w_lo{i}", [P, WI], F32R) for i in range(4)]
        one = sb("one", [P, 1])
        cst = sb("cst", [P, C_END])
        vec = sb("vec", [P, V_END])
        ones = sb("ones", [P, P])
        eps6 = sb("eps6", [P, 1])
        eps5 = sb("eps5", [P, 1])
        nlam = sb("nlam", [P, 1])
        lams = sb("lams", [P, 2])
        coef = sb("coef", [P, 1])
        cred = sb("cred", [P, 5])

        def overlay(*groups):
            made, sizes = {}, []
            for group in groups:
                with ExitStack() as inner:
                    total = 0
                    for name, shape, dt in group:
                        made[name] = inner.enter_context(nc.sbuf_tensor(name, shape, dt))
                        total += -(-4 * int(np.prod(shape[1:])) // 64) * 64
                    sizes.append(total)
            sb(f"hold_{groups[0][0][0]}", [P, max(sizes) // 4])
            return made

        T = {}
        T.update(overlay([("H", [P, KT, NTOK], F32)],
                         [("mraw", [P, KT, MEM], F32), ("mhi", [P, KT, MEM], F32R), ("mlo", [P, KT, MEM], F32R),
                          ("mvs", [P, 2, D], F32)],
                         [("QL", [P, H, SEQ], F32R), ("KL", [P, H, SEQ], F32R)],
                         [x for b in range(4) for x in ((f"Kb{b}", [P, H, PAST], F32), (f"Vb{b}", [P, 2, 512], F32))],
                         [(f"hid_{a}{g}{f}", [P, NTOK], F32R) for g in range(2) for f in range(2) for a in "hl"]))
        T.update(overlay([("NH", [P, KT, NTOK], F32R)],
                         [("YT", [P, KT, NTOK], F32)],
                         [("MIX", [P, KT, NTOK], F32)],
                         [("xQbd", [P, DB, KT, 64], F32), ("xE0", [P, H, MEM], F32), ("xE1", [P, H, MEM], F32),
                          ("xPT", [P, 2 * H * P], F32), ("cK1", [P, KT, MEM], F32)],
                         [("Hback", [P, KT, NTOK], F32)]))
        T.update(overlay([("NL", [P, KT, NTOK], F32R)],
                         [("NLf", [P, KT, NTOK], F32)],
                         [("yA2", [P, 2, 512], F32), ("E", [P, SH, P], F32), ("MT", [P, SH, P], F32),
                          ("h0t", [P, DB, 512], F32), ("cbm", [P, 2, P], F32), ("Btm", [P, 2, P], F32),
                          ("sqs", [P, 512], F32)],
                         [("V", [P, NT, 512], F32), ("E00", [P, SEQ], F32), ("E10", [P, SEQ], F32),
                          ("ATT0", [P, SEQ], F32), ("PTs", [P, SEQ], F32)],
                         [("Kb6", [P, H, PAST], F32), ("Kb7", [P, H, PAST], F32), ("Vb6", [P, 2, 512], F32),
                          ("Vb7", [P, 2, 512], F32), ("Vs", [P, 512], F32), ("Es", [P, 2, PAST + DS], F32),
                          ("Pn", [P, DB, P], F32), ("Pp", [P, 2, PAST], F32), ("PTb", [P, 2, 3 * P], F32),
                          ("oTs", [P, H, P], F32)],
                         [("mkT", [P, KT, MEM], F32), ("mvt", [P, 2, D], F32), ("cK0", [P, KT, MEM], F32),
                          ("cV0", [P, 2, D], F32), ("sE0", [64, MEM], F32), ("sE1", [64, MEM], F32),
                          ("sPT", [P, 2, 64], F32)]))
        T.update(overlay([("XC", [P, KT, NTOK], F32)],
                         [(f"stg{i}", [P, NT, 256], F32) for i in range(4)],
                         [("KTt", [P, H, SEQ], F32R), ("QTt", [P, H, SEQ], F32R), ("KTs", [P, H, P], F32),
                          ("QTs", [P, H, P], F32)],
                         [("Qbd", [P, DB, H, P], F32), ("Kb4", [P, H, PAST], F32), ("Vb4", [P, 2, 512], F32),
                          ("Kb5", [P, H, PAST], F32), ("Vb5", [P, 2, 512], F32)],
                         [("YH", [P, KT, NTOK], F32R)],
                         [("QX", [P, KT, NTOK], F32)],
                         [("ACC", [P, KT, NTOK], F32)]))
        T.update(overlay([("sq0", [P, 2, NC], F32), ("sq1", [P, 2, NC], F32), ("rstd", [P, NC], F32),
                          ("rstdp", [P, NC], F32), ("sqt", [P, NC], F32), ("sqa", [P, CH, NC], F32)],
                         [("wdr", [P, KT, 8], F32), ("wdh", [P, KT, 8], F32R), ("wdl", [P, KT, 8], F32R),
                          ("rpA", [P, 256], F32), ("rpB", [P, 256], F32), ("dts", [P, NT * 8, 6], F32)],
                         [("xp0", [P, XP], F32), ("xp1", [P, XP], F32), ("acc", [P, NTOK], F32),
                          ("cvo", [P, KT, 27], F32), ("cvi", [P, KT, 24], F32)],
                         [("xs", [P, 512], F32), ("xdt", [P, 512], F32), ("xdd", [P, 512], F32),
                          ("ST", [P, 512], F32), ("zt", [P, 512], F32), 
                          ("sm", [P, 128], F32), ("yoT", [P, 512], F32)],
                         [("qkr0", [P, 2, 512], F32), ("qkr1", [P, 2, 512], F32), ("on", [P, 512], F32),
                          ("at_sm", [P, 64], F32)],
                         [("E01", [P, SEQ], F32), ("E11", [P, SEQ], F32), ("on_", [P, 512], F32), ("at_sm_", [P, 64], F32),
                          ("ATT1", [P, SEQ], F32), ("osq", [P, 512], F32)],
                         [("xm", [P, 32], F32), ("cV1", [P, 2, D], F32)],
                         [(f"sg{i}", [P, NC], F32) for i in range(2)] + [(f"hr{i}", [P, NC], F32) for i in range(2)]))
        dt_t = sb("dt_t", [P, NT, SH])
        ad_t = sb("ad_t", [P, NT, SH])
        row = sb("row", [P, R_END])
        g = T.__getitem__

        bank = [ctx.enter_context(nc.psum_tensor(f"bank{i}", [P, 1024], F32)) for i in range(4)]
        B = [bank[i // 2][:, 512 * (i % 2):512 * (i % 2) + 512] for i in range(8)]
        TT = nc.vector.tensor_tensor
        TS = nc.vector.tensor_scalar
        STT = nc.vector.scalar_tensor_tensor
        CP = nc.vector.tensor_copy
        act_f = nc.scalar.activation
        mm = nc.tensor.matmul
        ident = cst[:, C_ID:C_ID + P]

        ld = {n: sem("ld_" + n) for n in ("cst", "vec", "row", "mem", "x0", "x1", "x2", "wdt", "scv", "h0", "Hb0", "xr")}
        w_raw = [sem(f"w_raw_in{i}") for i in range(2)]
        w_hi = sem("w_hi_done")
        w_ready = sem("w_ready")
        w_used = sem("w_used")
        setup = sem("setup_done")
        n_sq, n_pc, n_std, n_t, n_hi, n_lo, n_res = (sem("norm_" + x) for x in
                                                     ("squares", "pieces", "std", "scaled", "high", "ready", "residual"))
        p_sq, p_add, p_sum, p_std, p_t = (sem("post_" + x) for x in ("squares", "added", "sums", "std", "scaled"))
        lin_mm, lin_ev = sem("lin_mm"), sem("lin_evac")
        xb_mm, xb_ev = sem("xbc_mm"), sem("xbc_evac")
        tm_mm, tm_ev = sem("tm_mm"), sem("tm_evac")
        st_out = [sem(f"stage_out{i}") for i in range(4)]
        mem_mm, mem_ev, mem_out = sem("mem_mm"), sem("mem_evac"), sem("mem_out")
        dve_c, act_c = sem("dve_chain"), sem("act_chain")
        out_s = sem("out_stores")

        chain = {"dve": 0, "act": 0}

        def dlink(eng, ins):
            chain["dve"] += 1
            ins.then_inc(dve_c, 1)
            eng.wait_ge(dve_c, chain["dve"])

        def alink(eng, ins):
            chain["act"] += 1
            ins.then_inc(act_c, 1)
            eng.wait_ge(act_c, chain["act"])

        def three(out, pairs, release=()):
            n = len(pairs)
            for i, (ah, al, bh, bl) in enumerate(pairs):
                m = mm(out, ah, bh, start=(i == 0), stop=False)
                if i in release:
                    m.then_inc(w_used, 1)
                mm(out, ah, bl, start=False, stop=False)
                m = mm(out, al, bh, start=False, stop=(i == n - 1))
            return m

        P_MIX, P_MEM, P_X, P_FF, P_END = 0, 3, 4, 7, 10
        SPLIT_Y, SPLIT_OX = 4, 10
        split_no = {0: 0, 1: 1, 2: 2, 3: 3, 4: 7, 5: 8, 6: 9, 7: 13, 8: 14, 9: 15}

        def pre_sq(act, p, i, src, w):
            r = 4 * p + i
            if r >= 2:
                act.wait_ge(n_pc, r - 1)
            act_f(g(f"sq{r % 2}")[:, :, 0:w], src[:, 2 * i:2 * i + 2, :], ACT.Square).then_inc(n_sq, 1)

        def pre_std(act, p, w):
            act.wait_ge(n_pc, 4 * p + 4)
            if p:
                act.wait_ge(n_t, p)
            act_f(g("rstd")[:, 0:w], B[7][:, 0:w], ACT.Sqrt, bias=eps6[:, :], scale=1.0 / D).then_inc(n_std, 1)

        def pre_pe(pe, p, w):
            for i in range(4):
                pe.wait_ge(n_sq, 4 * p + i + 1)
                if p and i == 0:
                    pe.wait_ge(n_std, p)
                for k in range(2):
                    m = mm(B[7][:, 0:w], ones[:, :], g(f"sq{i % 2}")[:, k, 0:w], start=(i == 0 and k == 0),
                           stop=(i == 3 and k == 1))
                m.then_inc(n_pc, 1)

        def pre_dve(dve, p, src, tmp, lo, hi, gain, w):
            dve.wait_ge(n_std, p + 1)
            dlink(dve, nc.vector.reciprocal(g("rstd")[:, 0:w], g("rstd")[:, 0:w]))
            for k in range(KT):
                m = STT(out=tmp[:, k, :], in0=src[:, k, :], scalar=vec[:, gain + k:gain + k + 1],
                        in1=g("rstd")[:, 0:w], op0=ALU.mult, op1=ALU.mult)
            m.then_inc(n_t, 1)
            dve.wait_ge(n_t, p + 1)
            split_dve(dve, split_no[p], tmp, hi, lo)

        def split_dve(dve, n, src, hi, lo):
            dve.wait_ge(n_hi, n + 1)
            TT(lo, src, hi.bitcast(F32), ALU.subtract).then_inc(n_lo, 1)

        def pre_hi(act, p, tmp, hi):
            act.wait_ge(n_t, p + 1)
            act_f(hi, tmp, ACT.Copy).then_inc(n_hi, 1)

        def post_pe(pe, z):
            pe.wait_ge(p_add, post_added(z))
            if z:
                pe.wait_ge(p_std, z)
            mm(B[6][:, 0:NC], ones[:, :], g("sqa")[:, z % CH, :], start=True, stop=True).then_inc(p_sum, 1)

        def post_added(z):
            return 24 * (z // CH) + 12 + 4 * (z % CH) + 4

        def post_std(act, z):
            act.wait_ge(p_sum, z + 1)
            if z:
                act.wait_ge(p_t, z)
            act_f(g("rstdp")[:], B[6][:, 0:NC], ACT.Sqrt, bias=eps6[:, :], scale=1.0 / D).then_inc(p_std, 1)

        def post_dve(dve, z, src, res):
            dve.wait_ge(p_std, z + 1)
            dlink(dve, nc.vector.reciprocal(g("rstdp")[:], g("rstdp")[:]))
            TT(src, src, g("rstdp")[:].unsqueeze(1).broadcast_to([P, KT, NC]), ALU.mult).then_inc(p_t, 1)
            dve.wait_ge(p_t, z + 1)
            TT(res, res, src, ALU.add).then_inc(n_res, 1)

        def cs(c):
            return slice(NC * c, NC * c + NC)

        def lin_unit(pe, base, turn, q, xh, xl):
            blk, c, s = q // 12, q % 12 // 4, q % 4
            if c == 0:
                pe.wait_ge(w_ready, base + 4 * blk + s + 1)
            pe.wait_ge(lin_ev, 24 * turn + q + 1)
            three(B[q % 4][:, 0:NC],
                  [(whi[s][:, P * k:P * k + P], wlo[s][:, P * k:P * k + P], xh[:, k, cs(c)], xl[:, k, cs(c)])
                   for k in range(KT)],
                  release=((0,) if (c == 0 and s == 0) or (c == CH - 1 and s) else ())).then_inc(lin_mm, 1)

        def lin_dst(dst, q):
            blk, c, s = q // 12, q % 12 // 4, q % 4
            return dst[:, 4 * blk + s, cs(c)]

        def lin_copy(act, turn, q, dst):
            act.wait_ge(lin_mm, 24 * turn + q + 1)
            act_f(lin_dst(dst, q), B[q % 4][:, 0:NC], ACT.Copy).then_inc(lin_ev, 1)

        def lin_post(act, turn, pair, q, dst, gain):
            act.wait_ge(lin_mm, 24 * turn + q + 1)
            n = 24 * pair + q
            if n:
                act.wait_ge(p_add, n)
            act_f(g("sqt")[:], B[q % 4][:, 0:NC], ACT.Square).then_inc(p_sq, 1)
            m = 4 * (q // 12) + q % 4
            act_f(lin_dst(dst, q), B[q % 4][:, 0:NC], ACT.Copy, scale=vec[:, gain + m:gain + m + 1]).then_inc(lin_ev, 1)

        def post_add(dve, pair, q):
            dve.wait_ge(p_sq, 24 * pair + q + 1)
            a = g("sqa")[:, q % 12 // 4, :]
            if q < 12 and q % 4 == 0:
                CP(a, g("sqt")[:]).then_inc(p_add, 1)
            else:
                dve.wait_ge(p_add, 24 * pair + q)
                TT(a, a, g("sqt")[:], ALU.add).then_inc(p_add, 1)

        def yA(t):
            return g("yA2")[:, t % 2, :]

        def tok(t):
            return slice(P * t, P * t + P)

        def bc(ap, shape):
            return ap.broadcast_to(shape)

        def tm_no(kind, jj, t):
            return 18 * kind + 9 * jj + t

        s_dt, s_dtm, s_dtu = sem("dt_ready"), sem("dt_mm"), sem("dt_act")
        s_wdt = sem("wdt_split")
        s_pad = sem("conv_pads")
        cv_done, xc_done, cv_out = sem("conv_done"), sem("xbc_ready"), sem("conv_out")
        (s_cbm, s_p1, s_cols, s_exps, s_D, s_E, s_xb, s_mt, s_xdt, s_xdd, s_off, s_yd, s_stm, s_stu, s_yA, s_ysq,
         s_y, s_yt, s_yte) = (sem("ssd_" + n) for n in
                              ("masked", "first", "cols", "exps", "diff", "decay", "copies", "mixed", "xdt", "xdd", "yoff",
                               "ydiag", "states", "state", "yraw", "yrms", "ynorm", "ytrans", "yout"))
        ld_z = [sem(f"ld_z{i}") for i in range(2)]
        s_yo1, s_yo2, s_xb8, s_nb = sem("ssd_yoff_t"), sem("ssd_yoff_copy"), sem("ssd_xddb"), sem("ssd_newstate")
        s_nbm = sem("ssd_newstate_mm")
        ld_qk = [sem(f"ld_qk{i}") for i in range(2)]
        ld_v = sem("ld_v")
        a_lo, a_oc = sem("att_qk_low"), sem("att_out")
        a_tr, a_tre, a_S, a_nb, a_exp, a_att, a_T, a_Te, a_pv, a_o, a_on, a_yt, a_yte = (
            sem("att_" + n) for n in ("qk_trans", "qk_copy", "scores", "max", "exp", "probs", "ptrans", "pcopy", "pv",
                                      "ocopy", "onorm", "otrans", "oout"))
        ld_kb = [sem(f"ld_kc{i}") for i in range(DB)]
        b_q, b_S, b_nb, b_exp, b_p, b_T, b_Te, b_pv, b_o, b_ot, b_ote = (
            sem("smp_" + n) for n in ("qbd", "scores", "max", "exp", "probs", "ptrans", "pcopy", "pv", "ocopy", "otrans",
                                      "otok"))
        ld_mkv, ld_cm = sem("ld_mem_kv"), [sem(f"ld_cache_mem{i}") for i in range(2)]
        x_S, x_nb, x_exp, x_p, x_T, x_Te, x_pv, x_o = (
            sem("x_" + n) for n in ("scores", "max", "exp", "probs", "ptrans", "pcopy", "pv", "out"))
        y_q, y_S, y_nb, y_exp, y_p, y_T, y_Te, y_pv, ys_o = (
            sem("xs_" + n) for n in ("qbd", "scores", "max", "exp", "probs", "ptrans", "pcopy", "pv", "out"))
        f_up, f_sg, f_hr, f_hh, f_hl, f_dn, f_de, f_acc = (
            sem("ffn_" + n) for n in ("up", "silu", "hidden", "high", "low", "down", "down_add", "acc_zero"))
        h_out, y_out = sem("h_store"), sem("y_store")
        rp_c, a_rs, ld_vs, y_z = sem("rope_chain"), sem("att_rms"), sem("ld_vs"), sem("xs_zero")

        block = ctx.enter_context(nc.Block())

        @block.sync
        def _(sp):
            sp.dma_start(vec[:], vecs).then_inc(ld["vec"], 16)
            sp.dma_start(g("H")[:, :, cs(0)], xT[:, :, cs(0)]).then_inc(ld["x0"], 16)
            for i in range(2):
                sp.dma_start(raw[i][:], wall[i]).then_inc(w_raw[i], 16)
            for c in range(1, CH):
                sp.dma_start(g("H")[:, :, cs(c)], xT[:, :, cs(c)]).then_inc(ld[f"x{c}"], 16)
            sp.dma_start(row[:], rows.partition_broadcast(P)).then_inc(ld["row"], 16)
            sp.dma_start(cst[:], consts).then_inc(ld["cst"], 16)

            def weights(n0, n1):
                with sp.Fori(n0 // 2, n1 // 2) as i:
                    for s in range(2):
                        sp.wait_ge(w_ready, 2 * i + s - 1)
                        sp.dma_start(raw[s][:], wall[2 * i + s]).then_inc(w_raw[s], 16)

            weights(2, I_WO + 2)
            sp.wait_ge(a_exp, 2 * H * (NT - 1))
            for b in range(6):
                sp.dma_start(g(f"Kb{b}")[:], kc[b]).then_inc(ld_kb[b], 16)
                sp.dma_start(g(f"Vb{b}")[:], vc[b].rearrange("(t p) c -> p t c", p=P)).then_inc(ld_kb[b], 16)
            sp.wait_ge(b_pv, 4)
            for c in range(CH):
                sp.dma_start(g("H")[:, :, cs(c)], xT[:, :, cs(c)]).then_inc(ld["xr"], 16)
            weights(I_WO + 2, I_WX + 2)
            sp.wait_ge(lin_mm, 48)
            sp.dma_start(g("mkT")[:], mk_o).then_inc(ld_mkv, 16)
            sp.dma_start(g("mvt")[:], mv_o.rearrange("(t p) c -> p t c", p=P)).then_inc(ld_mkv, 16)
            for b in range(DB):
                if b >= 2:
                    sp.wait_ge(y_pv, b - 1)
                sp.dma_start(g(f"cK{b % 2}")[:], cmk[b]).then_inc(ld_cm[b % 2], 16)
                sp.dma_start(g(f"cV{b % 2}")[:], cmv[b].rearrange("(t p) c -> p t c", p=P)).then_inc(ld_cm[b % 2], 16)
            weights(I_WX + 2, N_ITEMS)

        @block.gpsimd
        def _(pool):
            pool.memset(one[:], 1.0).then_inc(w_hi, 1)
            pool.wait_ge(w_hi, 1)

            def split(n, s, first):
                pool.wait_ge(w_raw[s % 2], 16 * (n // 2 + 1) if first else (n - s % 2) * 8 + 16)
                if not first:
                    pool.wait_ge(w_used, n - 3)
                pool.tensor_tensor(whi[s][:], raw[s % 2][:], bc(one[:, 0:1], [P, WI]), ALU.mult).then_inc(w_hi, 1)
                pool.wait_ge(w_hi, n + 2)
                pool.tensor_tensor(wlo[s][:], raw[s % 2][:], whi[s][:].bitcast(F32), ALU.subtract).then_inc(w_ready, 1)

            for n in range(4):
                split(n, n, True)
            with pool.Fori(1, N_ITEMS // 4) as i:
                for s in range(4):
                    split(4 * i + s, s, False)
            for n in range(N_ITEMS // 4 * 4, N_ITEMS):
                split(n, n % 4, False)

        @block.tensor
        def _(pe):
            pe.wait_ge(setup, 1)
            for c in range(CH):
                pre_pe(pe, P_MIX + c, NC)
            pe.wait_ge(n_lo, CH)

            def tm_chunk(kind, jj):
                s = 2 * jj
                pe.wait_ge(w_ready, I_TM + 8 * kind + 2 * jj + 2)
                for t in range(NT):
                    pe.wait_ge(tm_ev, tm_no(kind, jj, t) + 1)
                    three(B[(9 * jj + t) % 6][:, 0:256],
                          [(g("NH")[:, k, tok(t)], g("NL")[:, k, tok(t)],
                            whi[s + k // 4][:, 256 * (k % 4):256 * (k % 4) + 256],
                            wlo[s + k // 4][:, 256 * (k % 4):256 * (k % 4) + 256]) for k in range(KT)],
                          release=((0,) if t == 0 and kind + jj else (4,) if t == NT - 1 else ())).then_inc(tm_mm, 1)

            def mem_k(m):
                pe.wait_ge(w_ready, I_TM + 8 * (m // 4) + 4 + m % 4 + 1)
                if m >= 2:
                    pe.wait_ge(mem_ev, m - 1)
                three(B[6 + m % 2][:, 0:MEM], [(whi[m % 4][:, tok(k)], wlo[m % 4][:, tok(k)], g("mhi")[:, k, :],
                                                g("mlo")[:, k, :]) for k in range(KT)], release=(0,)).then_inc(mem_mm, 1)

            def mem_v(j):
                s = 2 * (j % 2)
                pe.wait_ge(w_ready, I_TM + 16 + 8 * (j // 2) + 4 + 2 * (j % 2) + 2)
                for t in range(2):
                    n = KT + 2 * j + t
                    pe.wait_ge(mem_ev, n - 1)
                    three(B[6 + n % 2][:, 0:256],
                          [(g("mhi")[:, k, tok(t)], g("mlo")[:, k, tok(t)],
                            whi[s + k // 4][:, 256 * (k % 4):256 * (k % 4) + 256],
                            wlo[s + k // 4][:, 256 * (k % 4):256 * (k % 4) + 256]) for k in range(KT)],
                          release=((0,) if t == 0 else (4,))).then_inc(mem_mm, 1)

            for kind in range(4):
                tm_chunk(kind, 0)
                if kind == 0:
                    pre_pe(pe, P_MEM, MEM)
                tm_chunk(kind, 1)
                if kind == 0:
                    pe.wait_ge(n_lo, P_MEM + 1)
                if kind == 3:
                    pe.wait_ge(s_dt, 1)
                for i in range(4):
                    if kind < 2:
                        mem_k(4 * kind + i)
                    elif i % 2:
                        mem_v(2 * (kind - 2) + i // 2)
                if kind == 2:
                    pe.wait_ge(s_wdt, 1)
                    pe.wait_ge(mem_ev, 12)
                    for t in range(NT):
                        m = three(B[6][:, SH * t:SH * t + SH],
                                  [(g("NH")[:, k, tok(t)], g("NL")[:, k, tok(t)], g("wdh")[:, k, :], g("wdl")[:, k, :])
                                   for k in range(KT)])
                    m.then_inc(s_dtm, 1)
            pe.wait_ge(tm_ev, 6 + 72)
            with pe.Fori(0, KT // 4) as i:
                for s in range(4):
                    pe.wait_ge(w_ready, I_XB + s + 1 + 4 * i)
                    for c in range(CH):
                        pe.wait_ge(xb_ev, 3 * s + c + 1 + 12 * i)
                        three(B[3 * (s % 2) + c][:, 0:NC],
                              [(whi[s][:, P * k:P * k + P], wlo[s][:, P * k:P * k + P], g("NH")[:, k, cs(c)],
                                g("NL")[:, k, cs(c)]) for k in range(KT)],
                              release=((0,) if c == 0 else ())).then_inc(xb_mm, 1)

            pe.wait_ge(xc_done, KT)
            pe.wait_ge(s_dt, 1)
            XC = g("XC")

            def first_sums(t):
                tri = cst[:, C_TS:C_TS + P] if t == NT - 1 else cst[:, C_TP:C_TP + P]
                if t:
                    pe.wait_ge(s_D, t)
                for h in range(SH):
                    mm(B[h // 4][:, tok(h % 4)], bc(ad_t[:, t, h:h + 1], [P, P]), tri, start=True, stop=True)

            def first(t):
                smp = t == NT - 1
                tri = cst[:, C_TS:C_TS + P] if smp else cst[:, C_TP:C_TP + P]
                blk = cst[:, C_BS:C_BS + P] if smp else ones[:, :]
                if t:
                    pe.wait_ge(s_mt, t)
                    pe.wait_ge(s_xb, t)
                mm(B[2][:, 256:264], tri, ad_t[:, t, :], start=True, stop=True)
                mm(B[2][:, 264:272], blk, ad_t[:, t, :], start=True, stop=True)
                if smp:
                    for b in range(DB):
                        mm(B[2][:, 272 + 8 * b:280 + 8 * b], bc(cst[:, C_BB + b:C_BB + b + 1], [P, P]), ad_t[:, t, :],
                           start=True, stop=True)
                for gr in range(2):
                    mm(B[2][:, tok(gr)], XC[:, 4 + gr, tok(t)], XC[:, 6 + gr, tok(t)], start=True, stop=True)
                for j in range(4):
                    nc.tensor.transpose(B[3][:, tok(j)], XC[:, j, tok(t)], ident)
                if t >= 2:
                    pe.wait_ge(s_yte, t - 1)
                for j in range(2):
                    m = nc.tensor.transpose(B[4][:, tok(j)], XC[:, 4 + j, tok(t)], ident)
                m.then_inc(s_p1, 1)

            def from_state(t):
                if t:
                    pe.wait_ge(s_yA, t)
                if t < NT - 1:
                    pe.wait_ge(s_stu, t + 1)
                    for gr in range(2):
                        m = mm(B[5][:, 256 * gr:256 * gr + 256], XC[:, 6 + gr, tok(t)], g("ST")[:, 256 * gr:256 * gr + 256],
                               start=True, stop=True)
                    m.then_inc(s_off, 1)
                else:
                    pe.wait_ge(ld["h0"], 16)
                    for b in range(DB):
                        for j in range(4):
                            lo = P * t + DS * b
                            m = mm(B[5][:, P * j + DS * b:P * j + DS * b + DS], g("h0t")[:, b, tok(j)],
                                   XC[:, 6 + j // 2, lo:lo + DS], start=True, stop=True)
                    m.then_inc(s_yo1, 1)
                    pe.wait_ge(s_yo2, 1)
                    for j in range(4):
                        m = nc.tensor.transpose(B[5][:, tok(j)], g("yoT")[:, tok(j)], ident)
                    m.then_inc(s_off, 1)

            def y_turn(t):
                pe.wait_ge(s_y, t + 1)
                for j in range(4):
                    m = nc.tensor.transpose(B[4][:, tok(j)], yA(t)[:, tok(j)], ident)
                m.then_inc(s_yt, 1)

            first_sums(0)
            first(0)
            for t in range(NT):
                from_state(t)
                if t + 1 < NT:
                    first_sums(t + 1)
                pe.wait_ge(s_mt, t + 1)
                pe.wait_ge(s_xdt, t + 1)
                for h in range(SH):
                    m = mm(B[6][:, SP_ * h:SP_ * h + SP_], g("MT")[:, h, :], g("xdt")[:, SP_ * h:SP_ * h + SP_],
                           start=True, stop=True)
                m.then_inc(s_yd, 1)
                pe.wait_ge(s_xdd, t + 1)
                pe.wait_ge(s_xb, t + 1)
                if t < NT - 1:
                    for gr in range(2):
                        m = mm(B[7][:, 256 * gr:256 * gr + 256], g("Btm")[:, gr, :], g("xdd")[:, 256 * gr:256 * gr + 256],
                               start=True, stop=True)
                    m.then_inc(s_stm, 1)
                if t:
                    y_turn(t - 1)
                if t + 1 < NT:
                    first(t + 1)
            pe.wait_ge(s_yte, NT - 1)
            y_turn(NT - 1)
            for b in range(DB):
                pe.wait_ge(s_xb8, b + 1)
                if b >= 2:
                    pe.wait_ge(s_nb, b - 1)
                for gr in range(2):
                    m = mm(B[7 if b % 2 else 0][:, 256 * gr:256 * gr + 256], g("Btm")[:, gr, :],
                           yA(b)[:, 256 * gr:256 * gr + 256], start=True, stop=True)
                m.then_inc(s_nbm, 1)

            for t in range(NT):
                for w in range(2):
                    n = 2 * t + w
                    pe.wait_ge(ld_qk[t % 2], 32 * (t // 2 + 1))
                    if n >= 2:
                        pe.wait_ge(a_tre, n - 1)
                        pe.wait_ge(a_lo, n - 1)
                    else:
                        pe.wait_ge(s_yA, NT)
                    for h in range(H):
                        m = nc.tensor.transpose(B[6 + w][:, tok(h)], g(f"qkr{t % 2}")[:, w, tok(h)], ident)
                    m.then_inc(a_tr, 1)
            pe.wait_ge(a_tre, 2 * NT)
            pe.wait_ge(a_lo, 2 * NT - 2)
            pe.wait_ge(ld_v, 16)
            pe.wait_ge(s_nb, DB)
            pe.wait_ge(s_yte, NT)

            def scores(u):
                t, h = divmod(u, H)
                W = P * (t + 1)
                for c in range(2):
                    if u:
                        pe.wait_ge(a_exp, 2 * (u - 1) + c + 1)
                    r = slice(64 * c, 64 * c + 64)
                    for w0 in range(0, W, 512):
                        w1 = min(W, w0 + 512)
                        o = bank[c][:, w0:w1]
                        qh, ql, kh, kl = g("QTt")[r, h, tok(t)], g("QL")[r, h, tok(t)], g("KTt")[r, h, w0:w1], g("KL")[r, h, w0:w1]
                        mm(o, qh, kh, start=True, stop=False)
                        mm(o, qh, kl, start=False, stop=False)
                        m = mm(o, ql, kh, start=False, stop=True)
                    m.then_inc(a_S, 1)

            def probs_turn(u):
                pe.wait_ge(a_att, u + 1)
                if u:
                    pe.wait_ge(a_Te, u)
                for k in range(u // H + 1):
                    m = nc.tensor.transpose(B[4 + k // 4][:, tok(k % 4)], g(f"ATT{u % 2}")[:, tok(k)], ident)
                m.then_inc(a_T, 1)

            def values(u):
                t, h = divmod(u, H)
                pe.wait_ge(a_Te, u + 1)
                if h == 0 and t:
                    pe.wait_ge(a_oc, t)
                for k in range(t + 1):
                    m = mm(B[6][:, tok(h)], g("PTs")[:, tok(k)], g("V")[:, k, tok(h)], start=(k == 0), stop=(k == t))
                m.then_inc(a_pv, 1)

            def o_trans(t):
                pe.wait_ge(a_on, t + 1)
                if t:
                    pe.wait_ge(a_yte, t)
                for h in range(H):
                    m = nc.tensor.transpose(B[7][:, tok(h)], g("on")[:, tok(h)], ident)
                m.then_inc(a_yt, 1)

            U = H * (NT - 1)
            scores(0)
            for u in range(U):
                if u + 1 < U:
                    scores(u + 1)
                probs_turn(u)
                if u:
                    values(u - 1)
                if u % H == 2 and u > H:
                    o_trans(u // H - 1)
            values(U - 1)

            def s_scores(b):
                sl = b % 2
                pe.wait_ge(ld_kb[b], 32)
                if b >= 2:
                    pe.wait_ge(b_exp, b - 1)
                for h in range(H):
                    mm(B[sl][:, 0:PAST], g("Qbd")[:, b, h, :], g(f"Kb{b}")[:, h, :], start=(h == 0), stop=(h == H - 1))
                for h in range(H):
                    m = mm(B[sl][:, PAST:PAST + DS], g("Qbd")[:, b, h, :], g("KTs")[:, h, DS * b:DS * b + DS],
                           start=(h == 0), stop=(h == H - 1))
                m.then_inc(b_S, 1)

            pe.wait_ge(b_q, 1)
            pe.wait_ge(a_exp, 2 * U)
            s_scores(0)
            for b in range(DB):
                sl = b % 2
                if b + 1 < DB:
                    s_scores(b + 1)
                if b == 0:
                    o_trans(NT - 2)
                pe.wait_ge(b_p, b + 1)
                if b >= 2:
                    pe.wait_ge(b_Te, b - 1)
                for k in range(2):
                    nc.tensor.transpose(B[2 + sl][:, tok(k)], g("Pp")[:, sl, tok(k)], ident)
                nc.tensor.transpose(B[2 + sl][:, tok(2)], g("Pn")[:, b, :], ident).then_inc(b_T, 1)
                pe.wait_ge(b_Te, b + 1)
                for h in range(H):
                    o = B[4 + b // 4][:, P * (b % 4) + 32 * h:P * (b % 4) + 32 * h + 32]
                    for k in range(2):
                        mm(o, g(f"Vb{b}")[:, k, tok(h)], g("PTb")[:, sl, P * k + 32 * h:P * k + 32 * h + 32], start=(k == 0),
                           stop=False)
                    m = mm(o, g("Vs")[:, tok(h)], g("PTb")[:, sl, 2 * P + 32 * h:2 * P + 32 * h + 32], start=False, stop=True)
                m.then_inc(b_pv, 1)
            pe.wait_ge(b_o, 1)
            pe.wait_ge(a_oc, NT - 1)
            for h in range(H):
                m = nc.tensor.transpose(B[6][:, tok(h)], g("oTs")[:, h, :], ident)
            m.then_inc(a_pv, 1)
            o_trans(NT - 1)

            YH, NH, NL = g("YH"), g("NH"), g("NL")

            def first(q):
                lin_unit(pe, I_WO, 0, q, YH, NL)

            def second(q):
                if q % 4 == 0 and q < 12:
                    pe.wait_ge(n_lo, 7 + q // 4 + 1)
                lin_unit(pe, I_WQ, 1, q, NH, NL)

            def joined_pe(first, second, z0, p0, n_first, n_second):
                for q in range(n_first):
                    first(q)
                    if q == n_first - 8:
                        post_pe(pe, z0)
                    if q == n_first - 4:
                        post_pe(pe, z0 + 1)
                        pre_pe(pe, p0, NC)
                pre_pe(pe, p0 + 1, NC)
                for q in range(n_second):
                    second(q)
                    if q == 0:
                        post_pe(pe, z0 + 2)
                    if q == 3:
                        pre_pe(pe, p0 + 2, NC)

            pe.wait_ge(n_lo, SPLIT_Y + CH)
            joined_pe(first, second, 0, P_X, 24, 24)

            pe.wait_ge(lin_ev, 4 + 48)
            pe.wait_ge(ld_mkv, 32)
            pe.wait_ge(y_q, 1)
            QX = g("QX")

            def x_scores(t):
                if t:
                    pe.wait_ge(x_exp, H * t)
                for h in range(H):
                    o = B[h // 2][:, MEM * (h % 2):MEM * (h % 2) + MEM]
                    for k in range(2):
                        m = mm(o, QX[:, 2 * h + k, tok(t)], g("mkT")[:, 2 * h + k, :], start=(k == 0), stop=(k == 1))
                m.then_inc(x_S, 1)

            def y_scores(b):
                pe.wait_ge(ld_cm[b % 2], 32 * (b // 2 + 1))
                if b:
                    pe.wait_ge(y_exp, b)
                for k in range(KT):
                    m = mm(B[6][0:64, 0:MEM], g("xQbd")[:, b, k, :], g(f"cK{b % 2}")[:, k, :], start=(k == 0),
                           stop=(k == KT - 1))
                m.then_inc(y_S, 1)

            def x_trans(t):
                pe.wait_ge(x_p, t + 1)
                if t:
                    pe.wait_ge(x_Te, t)
                for h in range(H):
                    for k in range(2):
                        m = nc.tensor.transpose(B[2 + h // 2][:, tok(2 * (h % 2) + k)], g(f"xE{t % 2}")[:, h, tok(k)], ident)
                m.then_inc(x_T, 1)

            def y_trans(b):
                pe.wait_ge(y_p, b + 1)
                if b:
                    pe.wait_ge(ys_o, b)
                for k in range(2):
                    m = nc.tensor.transpose(B[7][:, 64 * k:64 * k + 64], g(f"sE{b % 2}")[:, tok(k)], ident[0:64, 0:64])
                m.then_inc(y_T, 1)

            def x_values(t):
                pe.wait_ge(x_Te, t + 1)
                if t:
                    pe.wait_ge(x_o, t)
                for h in range(H):
                    for e in range(2):
                        for k in range(2):
                            m = mm(B[4 + h // 2][:, tok(2 * (h % 2) + e)], g("mvt")[:, k, tok(2 * h + e)],
                                   g("xPT")[:, tok(2 * h + k)], start=(k == 0), stop=(k == 1))
                m.then_inc(x_pv, 1)

            def y_values(b):
                pe.wait_ge(y_Te, b + 1)
                for h in range(H):
                    for e in range(2):
                        o = B[7][:, P + DS * (2 * h + e):P + DS * (2 * h + e) + DS]
                        for k in range(2):
                            m = mm(o, g(f"cV{b % 2}")[:, k, tok(2 * h + e)], g("sPT")[:, k, DS * h:DS * h + DS],
                                   start=(k == 0), stop=(k == 1))
                m.then_inc(y_pv, 1)

            x_scores(0)
            y_scores(0)
            for i in range(DB):
                if i + 1 < DB:
                    x_scores(i + 1)
                    y_scores(i + 1)
                x_trans(i)
                y_trans(i)
                x_values(i)
                y_values(i)

            def up_unit(q, p0, s0, ready):
                c, s = q // 4, q % 4
                if c == 0:
                    pe.wait_ge(w_ready, ready + s)
                if s % 2 == 0:
                    pe.wait_ge(f_hr, p0 + q // 2 + 1)
                w = (s0 + s) % 4
                three(B[2 * (q // 2 % 3) + q % 2][:, 0:NC],
                      [(whi[w][:, tok(k)], wlo[w][:, tok(k)], NH[:, k, cs(c)], NL[:, k, cs(c)]) for k in range(KT)],
                      release=((0,) if (c == 0 and s == 0) or (c == CH - 1 and s) else ())).then_inc(f_up, 1)

            def down(par, n0, s0, ready, hid, between=None):
                pe.wait_ge(w_ready, ready)
                pe.wait_ge(f_hl, hid)
                for q in range(3 * KT):
                    c, m_ = q // KT, q % KT
                    pe.wait_ge(f_de, n0 + q + 1)
                    three(B[6 + q % 2][:, 0:NC],
                          [(whi[(s0 + f) % 4][:, tok(m_)], wlo[(s0 + f) % 4][:, tok(m_)],
                            g(f"hid_h{par}{f}")[:, cs(c)], g(f"hid_l{par}{f}")[:, cs(c)]) for f in range(2)],
                          release=((0,) if q == 0 else (1,) if q == 3 * KT - 1 else ())).then_inc(f_dn, 1)

            def third(q):
                if q % 4 == 0 and q < 12:
                    pe.wait_ge(n_lo, SPLIT_OX + q // 4 + 1)
                lin_unit(pe, I_WX, 2, q, NH, NL)

            def fourth(q):
                if q % 4 == 0:
                    pe.wait_ge(n_lo, 13 + q // 4 + 1)
                up_unit(q, 0, 0, I_FF + 1)

            joined_pe(third, fourth, 3, P_FF, 24, 12)
            with pe.Fori(0, (NG - 1) // 2) as i:
                for x in range(2):
                    for q in range(12):
                        up_unit(q, 6 * (1 + x) + 12 * i, 2 * x, I_FF + 5 + 6 * x + 12 * i)
                    down(x, 24 * x + 48 * i, 2 * x, I_FF + 10 + 6 * x + 12 * i, 6 + 6 * x + 12 * i)
            down(0, 24 * (NG - 1), 0, N_ITEMS, 6 * NG)
            pe.wait_ge(f_de, 2 + 24 * NG)
            for c in range(CH):
                pre_pe(pe, P_END + c, NC)

        @block.scalar
        def _(act):
            H_, NH, NLf = g("H"), g("NH"), g("NLf")
            act.wait_ge(setup, 1)
            act.wait_ge(ld["vec"], 16)

            def pre_act(p, src, tmp, hi, w):
                for i in range(4):
                    pre_sq(act, p, i, src, w)
                pre_std(act, p, w)
                pre_hi(act, p, tmp, hi)

            for c in range(CH):
                act.wait_ge(ld[f"x{c}"], 16)
                pre_act(P_MIX + c, H_[:, :, cs(c)], NLf[:, :, cs(c)], NH[:, :, cs(c)], NC)
            act.dma_start(g("mraw")[:], memT).then_inc(ld["mem"], 16)

            dram = [zs_d, q_d, k_o, v_o]

            def store(kind, jj):
                j = 2 * kind + jj
                act.wait_ge(tm_ev, 6 + 9 * (j + 1))
                act.dma_start(dram[kind].rearrange("(t p) c -> p t c", p=P)[:, :, 256 * jj:256 * jj + 256],
                              g(f"stg{j % 4}")[:]).then_inc(st_out[j % 4], 16)

            def tm_out(kind, jj, f):
                j = 2 * kind + jj
                if j >= 4:
                    act.wait_ge(st_out[j % 4], 16)
                for t in range(NT):
                    n = tm_no(kind, jj, t)
                    act.wait_ge(tm_mm, n + 1)
                    act_f(g(f"stg{j % 4}")[:, t, :], B[(9 * jj + t) % 6][:, 0:256], f).then_inc(tm_ev, 1)
                store(kind, jj)

            def mem_k_out(m):
                act.wait_ge(mem_mm, m + 1)
                act_f(g("mraw")[:, m, :], B[6 + m % 2][:, 0:MEM], ACT.Copy).then_inc(mem_ev, 1)

            def mem_v_out(j):
                for t in range(2):
                    n = KT + 2 * j + t
                    act.wait_ge(mem_mm, n + 1)
                    act_f(g("mvs")[:, t, 256 * j:256 * j + 256], B[6 + n % 2][:, 0:256], ACT.Copy).then_inc(mem_ev, 1)

            tm_out(0, 0, ACT.Silu)
            act.wait_ge(ld["mem"], 16)
            pre_act(P_MEM, g("mraw")[:], g("mraw")[:], g("mhi")[:], MEM)
            tm_out(0, 1, ACT.Silu)
            act.wait_ge(n_lo, P_MEM + 1)
            act.dma_start(g("wdr")[:], wdt).then_inc(ld["wdt"], 16)
            for m in range(4):
                mem_k_out(m)
            act.wait_ge(setup, 2)
            act_f(row[:, R_LAM:R_LAM + 2], row[:, R_LAM:R_LAM + 2], ACT.Exp).then_inc(s_dtu, 1)
            act_f(row[:, R_ALOG:R_ALOG + SH], row[:, R_ALOG:R_ALOG + SH], ACT.Exp).then_inc(s_dtu, 1)
            act.wait_ge(ld["wdt"], 16)
            act_f(g("wdh")[:], g("wdr")[:], ACT.Copy).then_inc(s_dtu, 1)
            store(1, 0)
            store(1, 1)
            for m in range(4, KT):
                mem_k_out(m)
            act.wait_ge(mem_ev, KT)
            act.dma_start(mk_o, g("mraw")[:]).then_inc(mem_out, 16)
            store(2, 0)
            store(2, 1)
            for j in range(2):
                mem_v_out(j)
            D6 = g("dts")
            act.wait_ge(s_dt, 1)
            act_f(D6[:, :, 1], D6[:, :, 0], ACT.Abs).then_inc(s_dtu, 1)
            act.wait_ge(s_dtu, 4)
            act_f(D6[:, :, 2], D6[:, :, 1], ACT.Exp, scale=-1.0).then_inc(s_dtu, 1)
            act.wait_ge(s_dtu, 5)
            act_f(D6[:, :, 3], D6[:, :, 2], ACT.Ln, bias=1.0).then_inc(s_dtu, 1)
            tm_out(3, 0, ACT.Copy)
            tm_out(3, 1, ACT.Copy)
            for j in range(2, 4):
                mem_v_out(j)
            act.wait_ge(mem_ev, 2 * KT)
            act.dma_start(mv_o.rearrange("(t p) c -> p t c", p=P), g("mvs")[:]).then_inc(mem_out, 16)
            act.wait_ge(s_dt, 2)
            act.dma_start(g("cvi")[:], sconv).then_inc(ld["scv"], 16)
            act.wait_ge(ld["scv"], 16)

            def xp_s(m):
                return g(f"xp{m % 2}")[:, 3 + SEQ:XP].rearrange("p (b s) -> p b s", b=DB)

            def silu(m):
                act.wait_ge(cv_done, m + 1)
                if m == 0:
                    for i in range(4):
                        act.wait_ge(st_out[i], 32)
                act_f(g("XC")[:, m, :], g("acc")[:], ACT.Silu).then_inc(xc_done, 1)

            for m in range(KT):
                if m >= 2:
                    act.wait_ge(cv_done, m - 1)
                act_f(xp_s(m)[:, :, 0:3], g("cvi")[:, m, :].rearrange("p (b s) -> p b s", b=DB), ACT.Copy)
                for c in range(CH):
                    act.wait_ge(xb_mm, 3 * m + c + 1)
                    src = B[3 * (m % 2) + c]
                    if c < 2:
                        act_f(g(f"xp{m % 2}")[:, 3 + NC * c:3 + NC * c + NC], src[:, 0:NC], ACT.Copy).then_inc(xb_ev, 1)
                    else:
                        w = SEQ - NC * c
                        act_f(g(f"xp{m % 2}")[:, 3 + NC * c:3 + SEQ], src[:, 0:w], ACT.Copy)
                        act_f(xp_s(m)[:, :, 3:], src[:, w:NC].rearrange("p (b s) -> p b s", b=DB), ACT.Copy).then_inc(xb_ev, 1)
                if m:
                    silu(m - 1)
            silu(KT - 1)
            act.dma_start(conv_o, g("cvo")[:]).then_inc(cv_out, 16)
            act.dma_start(g("h0t")[:], h0).then_inc(ld["h0"], 16)
            act.wait_ge(cv_out, 16)
            act.wait_ge(xc_done, KT)

            sm = g("sm")

            def y_rms(t):
                act.wait_ge(s_yA, t + 1)
                if t:
                    act.wait_ge(s_y, t)
                for gr in range(2):
                    x = act_f(g("sqs")[:, 256 * gr:256 * gr + 256], yA(t)[:, 256 * gr:256 * gr + 256], ACT.Square,
                              accum_out=sm[:, 112 + gr:113 + gr])
                alink(act, x)
                alink(act, act_f(sm[:, 114:116], sm[:, 112:114], ACT.Ln, bias=eps5[:, :], scale=1.0 / 256))
                act_f(sm[:, 116:118], sm[:, 114:116], ACT.Exp, scale=-0.5).then_inc(s_ysq, 1)

            def y_evac(t):
                act.wait_ge(s_yt, t + 1)
                for j in range(4):
                    x = act_f(g("YT")[:, j, tok(t)], B[4][:, tok(j)], ACT.Copy, scale=vec[:, V_SSM + j:V_SSM + j + 1])
                x.then_inc(s_yte, 1)

            for t in range(NT):
                smp = t == NT - 1
                if t:
                    act.wait_ge(s_yA, t)
                act.dma_start(g("zt")[:], zs_d[P * t:P * t + P, :]).then_inc(ld_z[0], 16)
                if smp:
                    act.dma_start(ssm_o[0], g("ST")[:]).then_inc(out_s, 16)
                act.wait_ge(s_p1, t + 1)
                if t:
                    act.wait_ge(s_stm, t)
                act_f(g("Btm")[:].rearrange("p a n -> p (a n)"), B[4][:, 0:256], ACT.Copy)
                act_f(g("xs")[:], B[3][:, :], ACT.Copy).then_inc(s_xb, 1)
                act.wait_ge(s_cols, t + 1)
                if smp:
                    act_f(sm[:, 48:112], sm[:, 48:112], ACT.Exp)
                act_f(sm[:, 24:48], sm[:, 0:24], ACT.Exp).then_inc(s_exps, 1)
                act.wait_ge(s_D, t + 1)
                act_f(g("E")[:], g("E")[:], ACT.Exp).then_inc(s_E, 1)
                if smp:
                    act.wait_ge(s_yo1, 1)
                    act_f(g("yoT")[:], B[5][:, :], ACT.Copy).then_inc(s_yo2, 1)
                if t:
                    y_rms(t - 1)
                    y_evac(t - 1)
            y_rms(NT - 1)
            y_evac(NT - 1)
            act.wait_ge(s_nb, DB)
            act.dma_start(ssm_o[1:1 + DB].rearrange("b n q -> n b q"), g("h0t")[:]).then_inc(out_s, 16)
            act.wait_ge(out_s, 32)

            def load_qk(t):
                if t >= 2:
                    act.wait_ge(a_tr, 2 * t - 2)
                act.dma_start(g(f"qkr{t % 2}")[:, 0, :], q_d[P * t:P * t + P, :]).then_inc(ld_qk[t % 2], 16)
                act.dma_start(g(f"qkr{t % 2}")[:, 1, :], k_o[P * t:P * t + P, :]).then_inc(ld_qk[t % 2], 16)

            act.dma_start(g("V")[:], v_o.rearrange("(t p) c -> p t c", p=P)).then_inc(ld_v, 16)
            load_qk(0)
            load_qk(1)
            act.wait_ge(mem_out, 32)
            for t in range(NT):
                for w in range(2):
                    n = 2 * t + w
                    act.wait_ge(a_tr, n + 1)
                    if t < NT - 1:
                        dst = g("QTt" if w == 0 else "KTt")[:, :, tok(t)]
                    else:
                        dst = g("QTs" if w == 0 else "KTs")[:]
                    act_f(dst, B[6 + w][:, :].rearrange("p (h q) -> p h q", h=H), ACT.Copy).then_inc(a_tre, 1)
                if t + 2 < NT:
                    load_qk(t + 2)
            act.wait_ge(a_tr, 2 * NT)
            asm = g("at_sm")

            def exps(u):
                t, h = divmod(u, H)
                W = P * (t + 1)
                a = 8 * (u % 2)
                for c in range(2):
                    act.wait_ge(a_nb, 2 * u + c + 1)
                    if u >= 2:
                        act.wait_ge(a_att, u - 1)
                    act_f(g(f"E{c}{u % 2}")[:, 0:W], bank[c][:, 0:W], ACT.Exp, bias=asm[:, a + c:a + c + 1], scale=0.125,
                          accum_out=asm[:, a + 2 + c:a + 3 + c]).then_inc(a_exp, 1)

            def copy_pt(u):
                act.wait_ge(a_T, u + 1)
                if u:
                    act.wait_ge(a_pv, u)
                W = P * (u // H + 1)
                for w0 in range(0, W, 512):
                    w1 = min(W, w0 + 512)
                    x = act_f(g("PTs")[:, w0:w1], B[4 + w0 // 512][:, 0:w1 - w0], ACT.Copy)
                x.then_inc(a_Te, 1)

            def o_norm(t):
                act.wait_ge(a_oc, t + 1)
                if t:
                    act.wait_ge(a_on, t)
                for h in range(H):
                    x = act_f(g("osq")[:, tok(h)], g("on")[:, tok(h)], ACT.Square, accum_out=asm[:, 40 + h:41 + h])
                alink(act, x)
                alink(act, act_f(asm[:, 44:48], asm[:, 40:44], ACT.Ln, bias=eps5[:, :], scale=1.0 / DH))
                act_f(asm[:, 48:52], asm[:, 44:48], ACT.Exp, scale=-0.5).then_inc(a_rs, 1)

            def o_evac(t):
                act.wait_ge(a_yt, t + 1)
                act_f(g("YT")[:, 4:8, tok(t)], B[7][:, :].rearrange("p (h q) -> p h q", h=H), ACT.Copy,
                      scale=vec[:, V_SUB:V_SUB + 1]).then_inc(a_yte, 1)

            U = H * (NT - 1)
            exps(0)
            for u in range(U):
                if u + 1 < U:
                    exps(u + 1)
                copy_pt(u)
                if u % H == 1 and u > H:
                    o_norm(u // H - 1)
                if u % H == 3 and u > H:
                    o_evac(u // H - 1)

            def load_kb(b):
                act.dma_start(g(f"Kb{b}")[:], kc[b]).then_inc(ld_kb[b], 16)
                act.dma_start(g(f"Vb{b}")[:], vc[b].rearrange("(t p) c -> p t c", p=P)).then_inc(ld_kb[b], 16)

            act.wait_ge(a_pv, U)
            act.dma_start(g("Vs")[:], v_o[SEQ:NTOK, :]).then_inc(ld_vs, 16)
            for b in (6, 7):
                load_kb(b)
            o_norm(NT - 2)
            o_evac(NT - 2)
            act.wait_ge(ld_vs, 16)

            def s_exp(b):
                a = 8 * (b % 2)
                act.wait_ge(b_nb, b + 1)
                act_f(g("Es")[:, b % 2, :], B[b % 2][:, 0:PAST + DS], ACT.Exp, bias=asm[:, a:a + 1], scale=0.125,
                      accum_out=asm[:, a + 2:a + 3]).then_inc(b_exp, 1)

            s_exp(0)
            for b in range(DB):
                if b + 1 < DB:
                    s_exp(b + 1)
                act.wait_ge(b_T, b + 1)
                act_f(g("PTb")[:, b % 2, :], B[2 + b % 2][:, 0:384], ACT.Copy).then_inc(b_Te, 1)
            o_norm(NT - 1)
            o_evac(NT - 1)

            act.wait_ge(a_yte, NT)
            act.wait_ge(s_yte, NT)
            for c in range(CH):
                act_f(g("YH")[:, :, cs(c)], g("YT")[:, :, cs(c)], ACT.Copy).then_inc(n_hi, 1)

            def squares(p, c, i0, i1):
                for i in range(i0, i1):
                    pre_sq(act, p + c, i, H_[:, :, cs(c)], NC)

            def joined_act(first, second, z0, p0, n_second, keep=None):
                for q in range(24):
                    if q == 20:
                        act.wait_ge(n_res, z0 + 1)
                        squares(p0, 0, 0, 2)
                        if keep:
                            keep(0)
                    if q == 23:
                        pre_hi(act, p0, NLf[:, :, cs(0)], NH[:, :, cs(0)])
                        act.wait_ge(n_res, z0 + 2)
                        squares(p0, 1, 0, 2)
                        if keep:
                            keep(1)
                    first(q)
                    if q == 16:
                        post_std(act, z0)
                    if q == 20:
                        post_std(act, z0 + 1)
                        squares(p0, 0, 2, 4)
                        pre_std(act, p0, NC)
                squares(p0, 1, 2, 4)
                pre_std(act, p0 + 1, NC)
                for q in range(n_second):
                    second(q)
                    if q == 0:
                        post_std(act, z0 + 2)
                        pre_hi(act, p0 + 1, NLf[:, :, cs(1)], NH[:, :, cs(1)])
                    if q == 2:
                        act.wait_ge(n_res, z0 + 3)
                        squares(p0, 2, 0, 2)
                        if keep:
                            keep(2)
                    if q == 3:
                        squares(p0, 2, 2, 4)
                        pre_std(act, p0 + 2, NC)
                        pre_hi(act, p0 + 2, NLf[:, :, cs(2)], NH[:, :, cs(2)])

            joined_act(lambda q: lin_post(act, 0, 0, q, g("MIX"), G_POSTMIX),
                       lambda q: lin_copy(act, 1, q, g("QX")), 0, P_X, 24)

            xm = g("xm")

            def x_exps(t):
                act.wait_ge(x_nb, t + 1)
                if t >= 2:
                    act.wait_ge(x_T, t - 1)
                for h in range(H):
                    act_f(g(f"xE{t % 2}")[:, h, :], B[h // 2][:, MEM * (h % 2):MEM * (h % 2) + MEM], ACT.Exp,
                          bias=xm[:, 4 + h:5 + h], scale=1.0 / 16, accum_out=xm[:, 8 + h:9 + h]).then_inc(x_exp, 1)

            def y_exps(b):
                act.wait_ge(y_nb, b + 1)
                if b >= 2:
                    act.wait_ge(y_T, b - 1)
                act_f(g(f"sE{b % 2}")[:, :], B[6][0:64, 0:MEM], ACT.Exp, bias=xm[0:64, 17:18], scale=1.0 / 16,
                      accum_out=xm[0:64, 18:19]).then_inc(y_exp, 1)

            def x_copy(t):
                act.wait_ge(x_T, t + 1)
                if t:
                    act.wait_ge(x_pv, t)
                for j in range(2):
                    x = act_f(g("xPT")[:, 512 * j:512 * j + 512], B[2 + j][:, :], ACT.Copy)
                x.then_inc(x_Te, 1)

            def y_copy(b):
                act.wait_ge(y_T, b + 1)
                if b:
                    act.wait_ge(y_pv, b)
                act_f(g("sPT")[:].rearrange("p a n -> p (a n)"), B[7][:, 0:128], ACT.Copy).then_inc(y_Te, 1)

            x_exps(0)
            y_exps(0)
            for i in range(DB):
                if i + 1 < DB:
                    x_exps(i + 1)
                    y_exps(i + 1)
                x_copy(i)
                y_copy(i)
            act.wait_ge(ys_o, DB)
            act.wait_ge(x_o, NT - 1)
            for c in range(CH):
                act_f(NH[:, :, cs(c)], g("QX")[:, :, cs(c)], ACT.Copy).then_inc(n_hi, 1)

            def keep(c):
                act.dma_start(h_d[:, :, cs(c)], H_[:, :, cs(c)]).then_inc(h_out, 16)

            def gate(n):
                act.wait_ge(f_up, 2 * n + 1)
                if n >= 2:
                    act.wait_ge(f_hr, 3 + n - 1)
                act_f(g(f"sg{n % 2}")[:], B[2 * (n % 3)][:, 0:NC], ACT.Silu).then_inc(f_sg, 1)

            def hid_high(n):
                gi, c, f = n // 6, n % 6 // 2, n % 2
                act.wait_ge(f_hr, 3 + n + 1)
                if n == 0:
                    act.wait_ge(h_out, 16 * CH)
                if n % 6 == 0 and gi >= 2:
                    act.wait_ge(f_dn, 24 * (gi - 1))
                act_f(g(f"hid_h{gi % 2}{f}")[:, cs(c)], g(f"hr{n % 2}")[:], ACT.Copy).then_inc(f_hh, 1)

            joined_act(lambda q: lin_post(act, 2, 1, q, g("QX"), G_POSTX), lambda q: None, 3, P_FF, 4, keep)
            for n in range(6 * NG):
                gate(n)
                hid_high(n)
            act.wait_ge(f_dn, 24 * NG)
            act.dma_start(g("Hback")[:], h_d).then_inc(ld["Hb0"], 16)
            for c in range(CH):
                act.wait_ge(f_de, 2 + 24 * (NG - 1) + KT * (c + 1))
                for i in range(4):
                    pre_sq(act, P_END + c, i, g("ACC")[:, :, cs(c)], NC)
                pre_std(act, P_END + c, NC)
            for c in range(CH):
                act.wait_ge(n_res, 2 * CH + c + 1)
                act.dma_start(y_o[:, :, cs(c)], g("Hback")[:, :, cs(c)]).then_inc(y_out, 16)
            act.wait_ge(y_out, 16 * CH)

        @block.vector
        def _(dve):
            link = lambda ins: dlink(dve, ins)
            H_, NH, NL, NLf = g("H"), g("NH"), g("NL"), g("NLf")
            nc.vector.memset(ones[:], 1.0)
            nc.vector.memset(eps6[:], 1e-6)
            nc.vector.memset(eps5[:], 1e-5).then_inc(setup, 1)
            nc.vector.memset(cred[:, 0:1], 0.0).then_inc(lin_ev, 4)
            nc.vector.memset(cred[:, 1:2], 0.0).then_inc(tm_ev, 6)
            nc.vector.memset(cred[:, 2:3], 0.0).then_inc(f_hr, 3)
            nc.vector.memset(cred[:, 3:4], 0.0).then_inc(f_de, 2)
            nc.vector.memset(cred[:, 4:5], 0.0).then_inc(xb_ev, 6)
            dve.wait_ge(ld["vec"], 16)
            for c in range(CH):
                pre_dve(dve, P_MIX + c, H_[:, :, cs(c)], NLf[:, :, cs(c)], NL[:, :, cs(c)], NH[:, :, cs(c)], G_PREMIX, NC)
            pre_dve(dve, P_MEM, g("mraw"), g("mraw")[:], g("mlo")[:], g("mhi")[:], G_MEM, MEM)
            dve.wait_ge(ld["row"], 16)
            lq = row[:, R_LAM:R_LAM + 256].rearrange("p (a b d) -> p a b d", a=2, b=2)
            link(TT(lq[:, :, 0, :], lq[:, :, 0, :], lq[:, :, 1, :], ALU.mult))
            link(nc.vector.tensor_reduce(lams[:], lq[:, :, 0, :], AX, ALU.add))
            CP(row[:, R_LAM:R_LAM + 2], lams[:]).then_inc(setup, 1)
            dve.wait_ge(s_dtu, 3)
            TT(g("wdl")[:], g("wdr")[:], g("wdh")[:].bitcast(F32), ALU.subtract).then_inc(s_wdt, 1)
            link(TT(nlam[:], row[:, R_LAM + 1:R_LAM + 2], row[:, R_LAM:R_LAM + 1], ALU.subtract))
            link(TS(nlam[:], nlam[:], -0.2, None, ALU.add))
            link(TS(row[:, R_ALOG:R_ALOG + SH], row[:, R_ALOG:R_ALOG + SH], -1.0, None, ALU.mult))
            dve.wait_ge(ld["cst"], 16)
            link(TT(coef[:], cst[:, C_C1:C_C1 + 1], nlam[:], ALU.mult))
            link(TT(coef[:], coef[:], cst[:, C_C0:C_C0 + 1], ALU.add))
            link(TS(vec[:, V_SUB:V_SUB + 1], vec[:, V_SUB:V_SUB + 1], 0.8, None, ALU.mult))
            for kind in (1, 2):
                for jj in range(2):
                    j = 2 * kind + jj
                    dve.wait_ge(tm_ev, 6 + 9 * j)
                    if j >= 4:
                        dve.wait_ge(st_out[j % 4], 16)
                    for t in range(NT):
                        n = tm_no(kind, jj, t)
                        dve.wait_ge(tm_mm, n + 1)
                        X = B[(9 * jj + t) % 6][:, 0:256].rearrange("p (g d) -> p g d", d=32)
                        cos = bc(cst[:, C_COS + 32 * t:C_COS + 32 * t + 32].unsqueeze(1), [P, 8, 32])
                        sin = bc(cst[:, C_SIN + 32 * t:C_SIN + 32 * t + 32].unsqueeze(1), [P, 8, 32])
                        A = g("rpA")[:].rearrange("p (g d) -> p g d", d=32)
                        R = g("rpB")[:].rearrange("p (g d) -> p g d", d=32)
                        TT(A, X, cos, ALU.mult)
                        TT(R, X, sin, ALU.mult).then_inc(rp_c, 1)
                        dve.wait_ge(rp_c, 2 * (n - 18) + 1)
                        A4 = g("rpA")[:].rearrange("p (g x d) -> p g x d", x=2, d=32)
                        R4 = g("rpB")[:].rearrange("p (g x d) -> p g x d", x=2, d=32)
                        O4 = g(f"stg{j % 4}")[:, t, :].rearrange("p (g x d) -> p g x d", x=2, d=32)
                        TT(O4[:, :, 0, :], A4[:, :, 0, :], R4[:, :, 1, :], ALU.subtract).then_inc(rp_c, 1)
                        TT(O4[:, :, 1, :], A4[:, :, 1, :], R4[:, :, 0, :], ALU.add).then_inc(tm_ev, 1)
                        dve.wait_ge(tm_ev, 6 + n + 1)
            D6 = g("dts")
            dve.wait_ge(s_dtm, 1)
            TT(D6[:, :, 0].rearrange("p (t h) -> p t h", h=SH), B[6][:, 0:72].rearrange("p (t h) -> p t h", h=SH),
               bc(row[:, R_DTB:R_DTB + SH].unsqueeze(1), [P, NT, SH]), ALU.add).then_inc(s_dt, 1)
            dve.wait_ge(s_dtu, 6)
            u, e, ln = D6[:, :, 0], D6[:, :, 2], D6[:, :, 3]
            t1, t2 = D6[:, :, 4], D6[:, :, 5]
            link(TS(t1, e, 1.0, None, ALU.add))
            link(TS(t1, t1, -1.0, 1e-30, ALU.add, ALU.max))
            link(nc.vector.reciprocal(t2, t1))
            link(TT(t2, t2, e, ALU.mult))
            link(TT(t2, t2, ln, ALU.mult))
            link(TS(t1, e, 5.9e-8, None, ALU.min))
            link(TT(t2, t2, t1, ALU.max))
            link(TS(t1, u, 0.0, None, ALU.max))
            link(TT(dt_t[:].rearrange("p t h -> p (t h)"), t1, t2, ALU.add))
            TT(ad_t[:], dt_t[:], bc(row[:, R_ALOG:R_ALOG + SH].unsqueeze(1), [P, NT, SH]), ALU.mult).then_inc(s_dt, 1)
            dve.wait_ge(s_dt, 2)
            for i in range(2):
                link(nc.vector.memset(g(f"xp{i}")[:, 0:3], 0.0))
            acc = g("acc")
            accs = acc[:, SEQ:NTOK].rearrange("p (b s) -> p b s", b=DB)
            for m in range(KT):
                x = g(f"xp{m % 2}")
                xs_ = x[:, 3 + SEQ:XP].rearrange("p (b s) -> p b s", b=DB)
                dve.wait_ge(xb_ev, 6 + 3 * (m + 1))
                if m:
                    dve.wait_ge(xc_done, m)
                w = [vec[:, V_CW + 4 * m + j:V_CW + 4 * m + j + 1] for j in range(4)]
                cb = vec[:, V_CB + m:V_CB + m + 1]
                TS(acc[:, 0:SEQ], x[:, 0:SEQ], w[0], cb, ALU.mult, ALU.add)
                link(TS(accs, xs_[:, :, 0:DS], w[0], cb, ALU.mult, ALU.add))
                for j in range(1, 4):
                    STT(out=acc[:, 0:SEQ], in0=x[:, j:j + SEQ], scalar=w[j], in1=acc[:, 0:SEQ], op0=ALU.mult, op1=ALU.add)
                    if j < 3:
                        link(STT(out=accs, in0=xs_[:, :, j:j + DS], scalar=w[j], in1=accs, op0=ALU.mult, op1=ALU.add))
                    else:
                        STT(out=accs, in0=xs_[:, :, j:j + DS], scalar=w[j], in1=accs, op0=ALU.mult, op1=ALU.add)
                CP(g("cvo")[:, m, 0:3], x[:, SEQ:SEQ + 3])
                CP(g("cvo")[:, m, 3:27].rearrange("p (b s) -> p b s", b=DB), xs_[:, :, DS:DS + 3]).then_inc(cv_done, 1)

            dve.wait_ge(xc_done, KT)
            dve.wait_ge(cv_out, 16)
            sm, E, MT, xs, xdt, xdd, ST = (g(n) for n in ("sm", "E", "MT", "xs", "xdt", "xdd", "ST"))

            def heads(ap):
                return ap.rearrange("p (h q) -> p h q", h=SH)

            def y_scale(t):
                dve.wait_ge(s_ysq, t + 1)
                y = yA(t).rearrange("p (a q) -> p a q", a=2)
                TT(y, y, bc(sm[:, 116:118].unsqueeze(2), [P, 2, 256]), ALU.mult).then_inc(s_y, 1)

            nc.vector.memset(ST[:], 0.0).then_inc(s_stu, 1)
            for t in range(NT):
                smp = t == NT - 1
                tri = cst[:, C_TS:C_TS + P] if smp else cst[:, C_TP:C_TP + P]
                y = yA(t)
                dve.wait_ge(s_p1, t + 1)
                if t:
                    dve.wait_ge(s_mt, t)
                if smp:
                    CP(sm[:, 48:112], B[2][:, 272:336])
                link(CP(sm[:, 0:16], B[2][:, 256:272]))
                TT(sm[:, 16:24], sm[:, 8:16], sm[:, 0:8], ALU.subtract).then_inc(s_cols, 1)
                for h in range(SH):
                    m = TS(E[:, h, :], B[h // 4][:, tok(h % 4)], sm[:, h:h + 1], 0.0, ALU.subtract, ALU.min)
                m.then_inc(s_D, 1)
                dve.wait_ge(s_xb, t + 1)
                TT(heads(xdt[:]), heads(xs[:]), bc(dt_t[:, t, :].unsqueeze(2), [P, SH, SP_]), ALU.mult).then_inc(s_xdt, 1)
                TT(g("cbm")[:], B[2][:, 0:256].rearrange("p (a l) -> p a l", a=2), bc(tri.unsqueeze(1), [P, 2, P]),
                   ALU.mult).then_inc(s_cbm, 1)
                dve.wait_ge(s_xdt, t + 1)
                dve.wait_ge(s_exps, t + 1)
                TT(heads(xdd[:]), heads(xdt[:]), bc(sm[:, 40:48].unsqueeze(2), [P, SH, SP_]), ALU.mult).then_inc(s_xdd, 1)
                dve.wait_ge(s_cbm, t + 1)
                dve.wait_ge(s_E, t + 1)
                TT(MT[:].rearrange("p (a r) l -> p a r l", a=2), E[:].rearrange("p (a r) l -> p a r l", a=2),
                   bc(g("cbm")[:].unsqueeze(2), [P, 2, 4, P]), ALU.mult).then_inc(s_mt, 1)
                dve.wait_ge(s_off, t + 1)
                if t >= 2:
                    dve.wait_ge(s_yt, t - 1)
                m = TT(heads(y), heads(B[5][:, :]), bc(sm[:, 24:32].unsqueeze(2), [P, SH, SP_]), ALU.mult)
                if not smp:
                    m = TT(heads(ST[:]), heads(ST[:]), bc(sm[:, 32:40].unsqueeze(2), [P, SH, SP_]), ALU.mult)
                link(TT(heads(xs[:]), heads(xs[:]), bc(row[:, R_DSK:R_DSK + SH].unsqueeze(2), [P, SH, SP_]), ALU.mult))
                link(TT(y, y, xs[:], ALU.add))
                if t:
                    y_scale(t - 1)
                dve.wait_ge(s_yd, t + 1)
                link(TT(y, y, B[6][:, :], ALU.add))
                if not smp:
                    dve.wait_ge(s_stm, t + 1)
                    TT(ST[:], ST[:], B[7][:, :], ALU.add).then_inc(s_stu, 1)
                dve.wait_ge(ld_z[0], 16 * (t + 1))
                TT(y, y, g("zt")[:], ALU.mult).then_inc(s_yA, 1)
            dve.wait_ge(s_yA, NT)
            y_scale(NT - 1)
            dve.wait_ge(s_yt, NT)

            def part(b):
                if b >= 2:
                    dve.wait_ge(s_nbm, b - 1)
                TS(yA(b), xdd[:], cst[:, C_BB + b:C_BB + b + 1], None, ALU.mult).then_inc(s_xb8, 1)

            part(0)
            for b in range(DB):
                if b + 1 < DB:
                    part(b + 1)
                hb = g("h0t")[:, b, :]
                link(TT(heads(hb), heads(hb), bc(sm[:, 48 + 8 * b:56 + 8 * b].unsqueeze(2), [P, SH, SP_]), ALU.mult))
                dve.wait_ge(s_nbm, b + 1)
                TT(hb, hb, B[7 if b % 2 else 0][:, :], ALU.add).then_inc(s_nb, 1)

            asm = g("at_sm")
            dve.wait_ge(mem_out, 32)
            for t in range(NT - 1):
                for w in range(2):
                    dve.wait_ge(a_tre, 2 * t + w + 1)
                    hi = g("QTt" if w == 0 else "KTt")[:, :, tok(t)]
                    TT(g("QL" if w == 0 else "KL")[:, :, tok(t)], B[6 + w][:, :].rearrange("p (h q) -> p h q", h=H),
                       hi.bitcast(F32), ALU.subtract).then_inc(a_lo, 1)

            def maxes(u):
                t, h = divmod(u, H)
                W = P * (t + 1)
                a = 8 * (u % 2)
                for c in range(2):
                    dve.wait_ge(a_S, 2 * u + c + 1)
                    link(nc.vector.memset(bank[c][0:64, W - 64:W], BIG))
                    link(nc.vector.tensor_reduce(asm[:, a + 4 + c:a + 5 + c], bank[c][:, 0:W], AX, ALU.max))
                    TS(asm[:, a + c:a + c + 1], asm[:, a + 4 + c:a + 5 + c], -0.125, None, ALU.mult).then_inc(a_nb, 1)

            def r0(t):
                return asm[:, 32 + 4 * (t % 2):36 + 4 * (t % 2)]

            def probs(u):
                t, h = divmod(u, H)
                W = P * (t + 1)
                a = 8 * (u % 2)
                dve.wait_ge(a_exp, 2 * u + 2)
                nc.vector.reciprocal(r0(t)[:, h:h + 1], asm[:, a + 2:a + 3])
                link(nc.vector.reciprocal(asm[:, a + 7:a + 8], asm[:, a + 3:a + 4]))
                link(TT(asm[:, a + 7:a + 8], asm[:, a + 7:a + 8], nlam[:, :], ALU.mult))
                link(TT(asm[:, a + 7:a + 8], asm[:, a + 7:a + 8], asm[:, a + 2:a + 3], ALU.mult))
                if u >= 2:
                    dve.wait_ge(a_T, u - 1)
                STT(out=g(f"ATT{u % 2}")[:, 0:W], in0=g(f"E1{u % 2}")[:, 0:W], scalar=asm[:, a + 7:a + 8],
                    in1=g(f"E0{u % 2}")[:, 0:W], op0=ALU.mult, op1=ALU.add).then_inc(a_att, 1)

            on = g("on")[:].rearrange("p (h e) -> p h e", h=H)

            def o_copy(t):
                dve.wait_ge(a_pv, H * (t + 1) if t < NT - 1 else U + 1)
                if t:
                    dve.wait_ge(a_yt, t)
                b6 = B[6][:, :].rearrange("p (h e) -> p h e", h=H)
                if t < NT - 1:
                    TT(on, b6, bc(r0(t).unsqueeze(2), [P, H, DH]), ALU.mult).then_inc(a_oc, 1)
                else:
                    CP(on, b6).then_inc(a_oc, 1)

            def o_scale(t):
                dve.wait_ge(a_rs, t + 1)
                TT(on, on, bc(asm[:, 48:52].unsqueeze(2), [P, H, DH]), ALU.mult).then_inc(a_on, 1)

            U = H * (NT - 1)
            dve.wait_ge(out_s, 32)
            dve.wait_ge(a_tre, 2 * NT)
            maxes(0)
            for u in range(U):
                probs(u)
                if u % H == 1 and u > H:
                    o_copy(u // H - 1)
                if u % H == 2 and u > H:
                    o_scale(u // H - 1)
                if u + 1 < U:
                    maxes(u + 1)

            link(nc.vector.memset(g("Qbd")[:], 0.0))
            for h in range(H):
                for c in range(2):
                    r = slice(64 * c, 64 * c + 64)
                    m = CP(g("Qbd")[r, :, h, 32 * h + 16 * c:32 * h + 16 * c + 16],
                           g("QTs")[r, h, :].rearrange("p (b q) -> p b q", b=DB))
            m.then_inc(b_q, 1)
            dve.wait_ge(a_pv, U)
            o_copy(NT - 2)
            link(nc.vector.memset(g("Pn")[:], 0.0))
            o_scale(NT - 2)

            def s_max(b):
                a = 8 * (b % 2)
                dve.wait_ge(b_S, b + 1)
                link(nc.vector.tensor_reduce(asm[:, a + 4:a + 5], B[b % 2][:, 0:PAST + DS], AX, ALU.max))
                TS(asm[:, a:a + 1], asm[:, a + 4:a + 5], -0.125, None, ALU.mult).then_inc(b_nb, 1)

            s_max(0)
            for b in range(DB):
                a = 8 * (b % 2)
                if b + 1 < DB:
                    s_max(b + 1)
                dve.wait_ge(b_exp, b + 1)
                if b >= 2:
                    dve.wait_ge(b_T, b - 1)
                link(nc.vector.reciprocal(asm[:, a + 6:a + 7], asm[:, a + 2:a + 3]))
                link(TT(asm[:, a + 6:a + 7], asm[:, a + 6:a + 7], coef[:, :], ALU.mult))
                TS(g("Pp")[:, b % 2, :], g("Es")[:, b % 2, 0:PAST], asm[:, a + 6:a + 7], None, ALU.mult)
                TS(g("Pn")[:, b, DS * b:DS * b + DS], g("Es")[:, b % 2, PAST:PAST + DS], asm[:, a + 6:a + 7], None,
                   ALU.mult).then_inc(b_p, 1)
            dve.wait_ge(b_pv, DB)
            for i in range(2):
                o5 = B[4 + i][:, :].rearrange("p (b h c q) -> p b h c q", b=4, h=H, c=2)
                ot = g("oTs")[:, :, 64 * i:64 * i + 64].rearrange("p h (b q) -> p b h q", b=4)
                link(CP(ot, o5[:, :, :, 0, :]))
                m = TT(ot, ot, o5[:, :, :, 1, :], ALU.add)
                if i:
                    m.then_inc(b_o, 1)
            o_copy(NT - 1)
            o_scale(NT - 1)

            for c in range(CH):
                split_dve(dve, SPLIT_Y + c, g("YT")[:, :, cs(c)], g("YH")[:, :, cs(c)], NL[:, :, cs(c)])
            dve.wait_ge(ld["xr"], 16 * CH)

            def joined_dve(pair, src, gain):
                z0, p0 = CH * pair, P_X if pair == 0 else P_FF

                def post(c):
                    post_dve(dve, z0 + c, src[:, :, cs(c)], H_[:, :, cs(c)])

                def pre(c):
                    dve.wait_ge(n_res, z0 + c + 1)
                    pre_dve(dve, p0 + c, H_[:, :, cs(c)], NLf[:, :, cs(c)], NL[:, :, cs(c)], NH[:, :, cs(c)], gain, NC)

                for q in range(24):
                    post_add(dve, pair, q)
                    if q == 16:
                        post(0)
                    if q == 20:
                        post(1)
                    if q == 21:
                        pre(0)
                pre(1)
                post(2)
                pre(2)

            joined_dve(0, g("MIX"), G_PREX)

            xm = g("xm")
            QX = g("QX")
            dve.wait_ge(lin_ev, 4 + 48)
            nc.vector.memset(g("xQbd")[:], 0.0).then_inc(y_z, 1)
            dve.wait_ge(y_z, 1)
            for h in range(H):
                for k in range(2):
                    m = CP(g("xQbd")[:, :, 2 * h + k, DS * h:DS * h + DS],
                           QX[:, 2 * h + k, SEQ:NTOK].rearrange("p (b q) -> p b q", b=DB))
            m.then_inc(y_q, 1)

            def x_max(t):
                dve.wait_ge(x_S, t + 1)
                for j in range(2):
                    m = nc.vector.tensor_reduce(xm[:, 2 * j:2 * j + 2], B[j][:, :].rearrange("p (a n) -> p a n", a=2), AX, ALU.max)
                link(m)
                TS(xm[:, 4:8], xm[:, 0:4], -1.0 / 16, None, ALU.mult).then_inc(x_nb, 1)

            def y_max(b):
                dve.wait_ge(y_S, b + 1)
                link(nc.vector.tensor_reduce(xm[0:64, 16:17], B[6][0:64, 0:MEM], AX, ALU.max))
                TS(xm[0:64, 17:18], xm[0:64, 16:17], -1.0 / 16, None, ALU.mult).then_inc(y_nb, 1)

            def x_probs(t):
                dve.wait_ge(x_exp, H * (t + 1))
                link(nc.vector.reciprocal(xm[:, 12:16], xm[:, 8:12]))
                e = g(f"xE{t % 2}")[:]
                TT(e, e, bc(xm[:, 12:16].unsqueeze(2), [P, H, MEM]), ALU.mult).then_inc(x_p, 1)

            def y_probs(b):
                dve.wait_ge(y_exp, b + 1)
                link(nc.vector.reciprocal(xm[0:64, 19:20], xm[0:64, 18:19]))
                e = g(f"sE{b % 2}")[:]
                TS(e, e, xm[0:64, 19:20], None, ALU.mult).then_inc(y_p, 1)

            def x_out(t):
                dve.wait_ge(x_pv, t + 1)
                for j in range(2):
                    m = CP(QX[:, 4 * j:4 * j + 4, tok(t)], B[4 + j][:, :].rearrange("p (a q) -> p a q", a=4))
                m.then_inc(x_o, 1)

            def y_out_(b):
                dve.wait_ge(y_pv, b + 1)
                CP(QX[:, :, SEQ + DS * b:SEQ + DS * b + DS], B[7][:, P:2 * P].rearrange("p (a q) -> p a q", a=KT)).then_inc(ys_o, 1)

            x_max(0)
            y_max(0)
            x_probs(0)
            y_probs(0)
            for i in range(DB):
                if i + 1 < DB:
                    x_max(i + 1)
                    y_max(i + 1)
                    x_probs(i + 1)
                    y_probs(i + 1)
                x_out(i)
                y_out_(i)

            for c in range(CH):
                split_dve(dve, SPLIT_OX + c, QX[:, :, cs(c)], NH[:, :, cs(c)], NL[:, :, cs(c)])
            joined_dve(1, QX, G_PREF)
            ACC = g("ACC")
            nc.vector.memset(ACC[:], 0.0).then_inc(f_acc, 1)
            dve.wait_ge(f_acc, 1)

            def hidden(gi):
                for n in range(6 * gi, 6 * gi + 6):
                    c, f = n % 6 // 2, n % 2
                    dve.wait_ge(f_sg, n + 1)
                    dve.wait_ge(f_up, 2 * n + 2)
                    if n >= 2:
                        dve.wait_ge(f_hh, n - 1)
                    TT(g(f"hr{n % 2}")[:], g(f"sg{n % 2}")[:], B[2 * (n % 3) + 1][:, 0:NC], ALU.mult).then_inc(f_hr, 1)
                    dve.wait_ge(f_hh, n + 1)
                    TT(g(f"hid_l{gi % 2}{f}")[:, cs(c)], g(f"hr{n % 2}")[:],
                       g(f"hid_h{gi % 2}{f}")[:, cs(c)].bitcast(F32), ALU.subtract).then_inc(f_hl, 1)

            def add_down(gi):
                for q in range(3 * KT):
                    dve.wait_ge(f_dn, 24 * gi + q + 1)
                    a = ACC[:, q % KT, cs(q // KT)]
                    TT(a, a, B[6 + q % 2][:, 0:NC], ALU.add).then_inc(f_de, 1)

            hidden(0)
            for gi in range(1, NG):
                hidden(gi)
                add_down(gi - 1)
            add_down(NG - 1)
            dve.wait_ge(ld["Hb0"], 16)
            for c in range(CH):
                dve.wait_ge(n_std, P_END + c + 1)
                link(nc.vector.reciprocal(g("rstd")[:], g("rstd")[:]))
                a = ACC[:, :, cs(c)]
                for k in range(KT):
                    m = STT(out=a[:, k, :], in0=a[:, k, :], scalar=vec[:, G_POSTF + k:G_POSTF + k + 1], in1=g("rstd")[:],
                            op0=ALU.mult, op1=ALU.mult)
                m.then_inc(n_t, 1)
                dve.wait_ge(n_t, P_END + c + 1)
                hb = g("Hback")[:, :, cs(c)]
                TT(hb, hb, a, ALU.add).then_inc(n_res, 1)


def _consts():
    p = np.arange(P)
    c = np.zeros((P, C_END), np.float32)
    c[:, C_ID:C_ID + P] = np.eye(P)
    c[:, C_TP:C_TP + P] = p[:, None] <= p[None, :]
    same = p[:, None] // DS == p[None, :] // DS
    c[:, C_TS:C_TS + P] = same & (p[:, None] <= p[None, :])
    c[:, C_BS:C_BS + P] = same
    c[:, C_BB:C_BB + DB] = p[:, None] // DS == np.arange(DB)
    c[:, C_C1] = p // DS % 2
    c[:, C_C0] = 1 - c[:, C_C1]
    pos = np.concatenate([np.arange(SEQ), PAST + np.arange(NS) % DS]).astype(np.float32)
    inv = np.power(np.float32(10000.0), -np.arange(0, 64, 2, dtype=np.float32) / np.float32(64))
    ang = (pos[:, None] * inv[None, :]).astype(np.float32).reshape(NT, P, 32).transpose(1, 0, 2).reshape(P, -1)
    c[:, C_COS:C_COS + 288] = np.cos(ang.astype(np.float64))
    c[:, C_SIN:C_SIN + 288] = np.sin(ang.astype(np.float64))
    return c


def kernel(x_prompt, x_sample, cache_attn_k, cache_attn_v, state_ssm, state_conv, cache_mem_k, cache_mem_v,
           mem_prompt, w_in, conv_w, conv_b, dt_bias, a_log, d_skip, ssm_norm_w,
           lam_q1, lam_k1, lam_q2, lam_k2, subln_w, w_out, g_mem, wq_x, wk_x, wv_x, wo_x,
           g_pre_mix, g_post_mix, g_pre_x, g_post_x, g_pre_ffn, g_post_ffn, w_gate, w_up, w_down):
    import concourse.bacc as _bacc
    from concourse.bass_utils import run_bass_kernel_spmd as _run

    A = np.asarray

    def feat(x):
        x = A(x)
        return x.T.reshape(-1, P, x.shape[0]).transpose(1, 0, 2)

    def fm(w):
        w = A(w)
        return w.reshape(w.shape[0] // P, P, -1, P).transpose(2, 1, 0, 3).reshape(-1, P, WI)

    def tm(w):
        w = A(w)
        return w.reshape(2, 4, P, -1, 256).transpose(3, 0, 2, 1, 4).reshape(-1, P, WI)

    x = np.concatenate([A(x_prompt)[0], A(x_sample).reshape(NS, D)])
    wi = A(w_in)[0]
    q0 = 512 + 1024 + 8
    gate, upw, down = fm(A(w_gate)[0]), fm(A(w_up)[0]), A(w_down)[0].reshape(FT, P, D)
    ups = [np.stack([gate[2 * g], upw[2 * g], gate[2 * g + 1], upw[2 * g + 1]]) for g in range(NG)]
    downs = [down[2 * g:2 * g + 2] for g in range(NG)]
    ff = [ups[0]]
    for g in range(1, NG):
        ff += [ups[g], downs[g - 1]]
    ff.append(downs[-1])
    mix, wk, wv = tm(np.concatenate([wi[:, 0:512], wi[:, q0:]], axis=1)), fm(A(wk_x)[0]), tm(A(wv_x)[0])
    wall = np.concatenate([mix[0:4], wk[0:4], mix[4:8], wk[4:8], mix[8:12], wv[0:4], mix[12:16], wv[4:8],
                           fm(wi[:, 512:1536]), fm(A(w_out)[0]), fm(A(wq_x)[0]), fm(A(wo_x)[0])] + ff)
    gains = [A(v)[0].reshape(KT, P).T for v in (g_mem, g_pre_mix, g_post_mix, g_pre_x, g_post_x, g_pre_ffn, g_post_ffn)]
    vecs = np.concatenate(gains + [A(conv_w)[0].T.reshape(KT, P, 4).transpose(1, 0, 2).reshape(P, 32),
                                   A(conv_b)[0].reshape(KT, P).T, A(ssm_norm_w)[0].reshape(4, P).T,
                                   A(subln_w)[0].reshape(P, 1)], axis=1)
    rows = np.concatenate([A(v)[0] for v in (dt_bias, a_log, d_skip, lam_q1, lam_k1, lam_q2, lam_k2)])
    arrays = {
        "xT": feat(x),
        "memT": feat(A(mem_prompt)[0]),
        "wall": wall,
        "wdt": wi[:, 1536:1544].reshape(KT, P, 8).transpose(1, 0, 2),
        "consts": _consts(),
        "vecs": vecs,
        "rows": rows,
        "kc": A(cache_attn_k)[0].reshape(DB, PAST, H, DH).transpose(0, 3, 2, 1),
        "vc": A(cache_attn_v)[0].reshape(DB, PAST, 512),
        "h0": A(state_ssm)[0].reshape(DB, 512, P).transpose(2, 0, 1),
        "sconv": A(state_conv)[0].reshape(DB, 3, KT, P).transpose(3, 2, 0, 1).reshape(P, KT, 24),
        "cmk": A(cache_mem_k)[0].reshape(DB, MEM, KT, P).transpose(0, 3, 2, 1),
        "cmv": A(cache_mem_v)[0].reshape(DB, MEM, D),
    }
    arrays = {k: np.ascontiguousarray(v) for k, v in arrays.items()}
    outs = {"y": (P, KT, NTOK), "k": (NTOK, 512), "v": (NTOK, 512), "ssm": (1 + DB, P, 512), "conv": (P, KT, 27),
            "mk": (P, KT, MEM), "mv": (MEM, D)}
    scratch = {"zs": (NTOK, 512), "q": (NTOK, 512), "h": (P, KT, NTOK)}
    nc = _bacc.Bacc("TRN2", target_bir_lowering=False, num_devices=1)
    args = [nc.dram_tensor("in_" + k, a.shape, mybir.dt.from_np(a.dtype), kind="ExternalInput").ap()
            for k, a in arrays.items()]
    args += [nc.dram_tensor("out_" + k, s, F32, kind="ExternalOutput").ap() for k, s in outs.items()]
    args += [nc.dram_tensor("scratch_" + k, s, F32, kind="Internal").ap() for k, s in scratch.items()]
    build(nc, *args)
    r = _run(nc, [{"in_" + k: a for k, a in arrays.items()}], core_ids=[0]).results[0]
    o = {k: r["out_" + k] for k in outs}
    y = o["y"].transpose(2, 1, 0).reshape(NTOK, D)
    conv = o["conv"].transpose(2, 1, 0).reshape(27, D)
    ssm = o["ssm"].transpose(0, 2, 1).reshape(1 + DB, SH, SP_, P)
    return (y[:SEQ][None], y[SEQ:].reshape(DB, DS, D),
            o["k"][:SEQ].reshape(1, 1, SEQ, 4, 2, 64), o["v"][:SEQ].reshape(1, 1, SEQ, 4, 128),
            ssm[:1][None], conv[:3].reshape(1, 1, 3, D),
            o["mk"].transpose(2, 1, 0).reshape(1, 1, MEM, 4, 256), o["mv"].reshape(1, 1, MEM, 4, 256),
            o["k"][SEQ:].reshape(1, DB, DS, 4, 2, 64), o["v"][SEQ:].reshape(1, DB, DS, 4, 128),
            ssm[1:][None], conv[3:].reshape(1, DB, 3, D))
```

```python
from contextlib import ExitStack

import numpy as np

import concourse.bass as bass
from concourse import mybir

P = 128
D = 1024
KT = D // P
SEQ, DB, DS, PAST, MEM = 1024, 8, 16, 256, 256
NS = DB * DS
NTOK = SEQ + NS
NT = NTOK // P
NC = 384
CH = NTOK // NC
FT = 2816 // P
NG = FT // 2
H, DH = 4, 128
SH, SP_ = 8, 64
XP = 3 + SEQ + DB * (3 + DS)
WI = 1024
BIG = -1e30
QB = 2 * 64 + DS

F32 = mybir.dt.float32
F32R = mybir.dt.float32r
ALU = mybir.AluOpType
ACT = mybir.ActivationFunctionType
AX = mybir.AxisListType.X

I_TM, I_XB, I_WO, I_WQ, I_WX, I_FF = 0, 32, 40, 48, 56, 64
N_ITEMS = I_FF + 6 * NG

C_ID, C_TP, C_TS, C_BS, C_BB, C_COS, C_SIN = 0, 128, 256, 384, 512, 520, 808
C_C0, C_C1 = 1096, 1097
C_END = 1098
G_MEM, G_PREMIX, G_POSTMIX, G_PREX, G_POSTX, G_PREF, G_POSTF = (8 * i for i in range(7))
V_CW = 56
V_CB = 88
V_SSM = 96
V_SUB = 100
V_END = 101
R_DTB, R_ALOG, R_DSK, R_LAM = 0, 8, 16, 24
R_END = 280


def build(nc, xT, memT, wall, wdt, consts, vecs, rows, kc, vc, h0, sconv, cmk, cmv,
          y_o, k_o, v_o, ssm_o, conv_o, mk_o, mv_o, zs_d, q_d, h_d):
    with ExitStack() as ctx:
        def sb(name, shape, dt=F32):
            return ctx.enter_context(nc.sbuf_tensor(name, shape, dt))

        def sem(name):
            return ctx.enter_context(nc.semaphore(name))

        raw = [sb(f"w_raw{i}", [P, WI]) for i in range(2)]
        whi = [sb(f"w_hi{i}", [P, WI], F32R) for i in range(4)]
        wlo = [sb(f"w_lo{i}", [P, WI], F32R) for i in range(4)]
        one = sb("one", [P, 1])
        cst = sb("cst", [P, C_END])
        vec = sb("vec", [P, V_END])
        ones = sb("ones", [P, P])
        eps6 = sb("eps6", [P, 1])
        eps5 = sb("eps5", [P, 1])
        nlam = sb("nlam", [P, 1])
        lams = sb("lams", [P, 2])
        coef = sb("coef", [P, 1])
        cred = sb("cred", [P, 5])

        def overlay(*groups):
            made, sizes = {}, []
            for group in groups:
                with ExitStack() as inner:
                    total = 0
                    for name, shape, dt in group:
                        made[name] = inner.enter_context(nc.sbuf_tensor(name, shape, dt))
                        total += -(-4 * int(np.prod(shape[1:])) // 64) * 64
                    sizes.append(total)
            sb(f"hold_{groups[0][0][0]}", [P, max(sizes) // 4])
            return made

        T = {}
        T.update(overlay([("H", [P, KT, NTOK], F32)],
                         [("mraw", [P, KT, MEM], F32), ("mhi", [P, KT, MEM], F32R), ("mlo", [P, KT, MEM], F32R),
                          ("mvs", [P, 2, D], F32)],
                         [("QL", [P, H, SEQ], F32R), ("KL", [P, H, SEQ], F32R)],
                         [x for b in range(4) for x in ((f"Kb{b}", [P, H, PAST + DS], F32), (f"Vb{b}", [P, 2, 512], F32))],
                         [(f"hid_{a}{g}{f}", [P, NTOK], F32R) for g in range(2) for f in range(2) for a in "hl"]))
        T.update(overlay([("NH", [P, KT, NTOK], F32R)],
                         [("YT", [P, KT, NTOK], F32)],
                         [("MIX", [P, KT, NTOK], F32)],
                         [("xQbd", [P, 2, H * QB], F32), ("mkh", [P, KT, MEM], F32R), ("xE0", [P, H, MEM], F32), ("xE1", [P, H, MEM], F32),
                          ("xPT", [P, 2 * H * P], F32), ("cK1", [P, KT, MEM], F32)],
                         [("Hback", [P, KT, NTOK], F32)]))
        T.update(overlay([("NL", [P, KT, NTOK], F32R)],
                         [("NLf", [P, KT, NTOK], F32)],
                         [("yA2", [P, 2, 512], F32), ("E", [P, SH, P], F32), ("MT", [P, SH, P], F32),
                          ("cbm", [P, 2, P], F32), ("Btm", [P, 2, P], F32), ("sqs", [P, 512], F32),
                          ("under_V", [P, 512], F32), ("h0t", [P, DB, 512], F32)],
                         [("V", [P, NT, 512], F32), ("E00", [P, SEQ], F32), ("E10", [P, SEQ], F32),
                          ("ATT0", [P, SEQ], F32), ("PTs", [P, SEQ], F32)],
                         [("Kb6", [P, H, PAST + DS], F32), ("Kb7", [P, H, PAST + DS], F32), ("Vb6", [P, 2, 512], F32),
                          ("Vb7", [P, 2, 512], F32), ("Vs", [P, 512], F32), ("Es", [P, 2, PAST + DS], F32),
                          ("Pn", [P, DB, P], F32), ("Pp", [P, 2, PAST], F32), ("PTb", [P, 2, 2 * P], F32), ("PTn", [P, DB, P], F32),
                          ("oTs", [P, H, P], F32)],
                         [("mkl", [P, KT, MEM], F32R), ("mvt", [P, 2, D], F32), ("cK0", [P, KT, MEM], F32),
                          ("cV0", [P, 2, D], F32), ("sE0", [64, MEM], F32), ("sE1", [64, MEM], F32),
                          ("sPT", [P, 2, 64], F32)]))
        T.update(overlay([("XC", [P, KT, NTOK], F32)],
                         [(f"stg{i}", [P, NT, 256], F32) for i in range(4)],
                         [("KTt", [P, H, SEQ], F32R), ("QTt", [P, H, SEQ], F32R), ("QTs", [P, H, P], F32),
                          ("KTs", [P, H, P], F32)],
                         [("Qbd", [P, DB, H, P], F32), ("Kb4", [P, H, PAST + DS], F32), ("Vb4", [P, 2, 512], F32),
                          ("Kb5", [P, H, PAST + DS], F32), ("Vb5", [P, 2, 512], F32)],
                         [("YH", [P, KT, NTOK], F32R)],
                         [("QX", [P, KT, NTOK], F32)],
                         [("ACC", [P, KT, NTOK], F32)]))
        T.update(overlay([("sq0", [P, 2, NC], F32), ("sq1", [P, 2, NC], F32), ("rstd", [P, NC], F32),
                          ("rstdp", [P, NC], F32), ("sqt", [P, NC], F32), ("sqa", [P, CH, NC], F32)],
                         [("wdr", [P, KT, 8], F32), ("wdh", [P, KT, 8], F32R), ("wdl", [P, KT, 8], F32R),
                          ("rpA", [P, 256], F32), ("rpB", [P, 256], F32), ("dts", [P, NT * 8, 6], F32), ("dtr", [P, NTOK], F32)],
                         [("xp0", [P, XP], F32), ("xp1", [P, XP], F32), ("acc", [P, NTOK], F32),
                          ("cvo", [P, KT, 27], F32), ("cvi", [P, KT, 24], F32)],
                         [("xs", [P, 512], F32), ("xdt", [P, 512], F32), ("ST", [P, 512], F32), ("zt", [P, 512], F32),
                          ("xdd", [P, 512], F32), 
                          ("sm", [P, 128], F32), ("yoT", [P, 512], F32)],
                         [("qkr0", [P, 2, 512], F32), ("qkr1", [P, 2, 512], F32), ("on", [P, 512], F32),
                          ("at_sm", [P, 64], F32)],
                         [("E01", [P, SEQ], F32), ("E11", [P, SEQ], F32), ("on_", [P, 512], F32), ("at_sm_", [P, 64], F32),
                          ("ATT1", [P, SEQ], F32), ("osq", [P, 512], F32)],
                         [("xm", [P, 32], F32), ("cV1", [P, 2, D], F32), ("QXh", [P, KT, P], F32R), ("QXl", [P, KT, P], F32R)],
                         [("xm_", [P, 32], F32), ("under_cV1", [P, 2, D], F32), ("mkT", [P, KT, MEM], F32)],
                         [(f"sg{i}", [P, NC], F32) for i in range(2)] + [(f"hr{i}", [P, NC], F32) for i in range(2)]))
        dt_t = sb("dt_t", [P, NT, SH])
        ad_t = sb("ad_t", [P, NT, SH])
        row = sb("row", [P, R_END])
        g = T.__getitem__

        bank = [ctx.enter_context(nc.psum_tensor(f"bank{i}", [P, 1024], F32)) for i in range(4)]
        B = [bank[i // 2][:, 512 * (i % 2):512 * (i % 2) + 512] for i in range(8)]
        TT = nc.vector.tensor_tensor
        TS = nc.vector.tensor_scalar
        STT = nc.vector.scalar_tensor_tensor
        CP = nc.vector.tensor_copy
        act_f = nc.scalar.activation
        mm = nc.tensor.matmul
        ident = cst[:, C_ID:C_ID + P]

        ld = {n: sem("ld_" + n) for n in ("cst", "vec", "row", "mem", "x0", "x1", "x2", "wdt", "scv", "h0", "Hb0", "xr")}
        w_raw = [sem(f"w_raw_in{i}") for i in range(2)]
        w_hi = sem("w_hi_done")
        w_ready = sem("w_ready")
        w_used = sem("w_used")
        setup = sem("setup_done")
        n_sq, n_pc, n_std, n_t, n_hi, n_lo, n_res = (sem("norm_" + x) for x in
                                                     ("squares", "pieces", "std", "scaled", "high", "ready", "residual"))
        p_sq, p_add, p_sum, p_std, p_t = (sem("post_" + x) for x in ("squares", "added", "sums", "std", "scaled"))
        lin_mm, lin_ev = sem("lin_mm"), sem("lin_evac")
        xb_mm, xb_ev = sem("xbc_mm"), sem("xbc_evac")
        tm_mm, tm_ev = sem("tm_mm"), sem("tm_evac")
        st_out = [sem(f"stage_out{i}") for i in range(4)]
        mem_mm, mem_ev, mem_out = sem("mem_mm"), sem("mem_evac"), sem("mem_out")
        dve_c, act_c = sem("dve_chain"), sem("act_chain")
        out_s = sem("out_stores")

        chain = {"dve": 0, "act": 0}

        def dlink(eng, ins):
            chain["dve"] += 1
            ins.then_inc(dve_c, 1)
            eng.wait_ge(dve_c, chain["dve"])

        def alink(eng, ins):
            chain["act"] += 1
            ins.then_inc(act_c, 1)
            eng.wait_ge(act_c, chain["act"])

        def three(out, pairs, release=()):
            n = len(pairs)
            for i, (ah, al, bh, bl) in enumerate(pairs):
                m = mm(out, ah, bh, start=(i == 0), stop=False)
                if i in release:
                    m.then_inc(w_used, 1)
                mm(out, ah, bl, start=False, stop=False)
                m = mm(out, al, bh, start=False, stop=(i == n - 1))
            return m

        P_MIX, P_MEM, P_X, P_FF, P_END = 0, 3, 4, 7, 10
        SPLIT_Y, SPLIT_OX = 4, 10
        split_no = {0: 0, 1: 1, 2: 2, 3: 3, 4: 7, 5: 8, 6: 9, 7: 13, 8: 14, 9: 15}

        def pre_sq(act, p, i, src, w):
            r = 4 * p + i
            if r >= 2:
                act.wait_ge(n_pc, r - 1)
            act_f(g(f"sq{r % 2}")[:, :, 0:w], src[:, 2 * i:2 * i + 2, :], ACT.Square).then_inc(n_sq, 1)

        def pre_std(act, p, w):
            act.wait_ge(n_pc, 4 * p + 4)
            if p:
                act.wait_ge(n_t, p)
            act_f(g("rstd")[:, 0:w], B[7][:, 0:w], ACT.Sqrt, bias=eps6[:, :], scale=1.0 / D).then_inc(n_std, 1)

        def pre_pe(pe, p, w):
            for i in range(4):
                pe.wait_ge(n_sq, 4 * p + i + 1)
                if p and i == 0:
                    pe.wait_ge(n_std, p)
                for k in range(2):
                    m = mm(B[7][:, 0:w], ones[:, :], g(f"sq{i % 2}")[:, k, 0:w], start=(i == 0 and k == 0),
                           stop=(i == 3 and k == 1))
                m.then_inc(n_pc, 1)

        def pre_dve(dve, p, src, tmp, lo, hi, gain, w):
            dve.wait_ge(n_std, p + 1)
            dlink(dve, nc.vector.reciprocal(g("rstd")[:, 0:w], g("rstd")[:, 0:w]))
            for k in range(KT):
                m = STT(out=tmp[:, k, :], in0=src[:, k, :], scalar=vec[:, gain + k:gain + k + 1],
                        in1=g("rstd")[:, 0:w], op0=ALU.mult, op1=ALU.mult)
            m.then_inc(n_t, 1)
            dve.wait_ge(n_t, p + 1)
            split_dve(dve, split_no[p], tmp, hi, lo)

        def split_dve(dve, n, src, hi, lo):
            dve.wait_ge(n_hi, n + 1)
            TT(lo, src, hi.bitcast(F32), ALU.subtract).then_inc(n_lo, 1)

        def pre_hi(act, p, tmp, hi):
            act.wait_ge(n_t, p + 1)
            act_f(hi, tmp, ACT.Copy).then_inc(n_hi, 1)

        def post_pe(pe, z):
            pe.wait_ge(p_add, post_added(z))
            if z:
                pe.wait_ge(p_std, z)
            mm(B[6][:, 0:NC], ones[:, :], g("sqa")[:, z % CH, :], start=True, stop=True).then_inc(p_sum, 1)

        def post_added(z):
            return 24 * (z // CH) + 12 + 4 * (z % CH) + 4

        def post_std(act, z):
            act.wait_ge(p_sum, z + 1)
            if z:
                act.wait_ge(p_t, z)
            act_f(g("rstdp")[:], B[6][:, 0:NC], ACT.Sqrt, bias=eps6[:, :], scale=1.0 / D).then_inc(p_std, 1)

        def post_dve(dve, z, src, res):
            dve.wait_ge(p_std, z + 1)
            dlink(dve, nc.vector.reciprocal(g("rstdp")[:], g("rstdp")[:]))
            TT(src, src, g("rstdp")[:].unsqueeze(1).broadcast_to([P, KT, NC]), ALU.mult).then_inc(p_t, 1)
            dve.wait_ge(p_t, z + 1)
            TT(res, res, src, ALU.add).then_inc(n_res, 1)

        def cs(c):
            return slice(NC * c, NC * c + NC)

        def lin_unit(pe, base, turn, q, xh, xl):
            blk, c, s = q // 12, q % 12 // 4, q % 4
            if c == 0:
                pe.wait_ge(w_ready, base + 4 * blk + s + 1)
            pe.wait_ge(lin_ev, 24 * turn + q + 1)
            three(B[q % 4][:, 0:NC],
                  [(whi[s][:, P * k:P * k + P], wlo[s][:, P * k:P * k + P], xh[:, k, cs(c)], xl[:, k, cs(c)])
                   for k in range(KT)],
                  release=((0,) if (c == 0 and s == 0) or (c == CH - 1 and s) else ())).then_inc(lin_mm, 1)

        def lin_dst(dst, q):
            blk, c, s = q // 12, q % 12 // 4, q % 4
            return dst[:, 4 * blk + s, cs(c)]

        def lin_copy(act, turn, q, dst):
            act.wait_ge(lin_mm, 24 * turn + q + 1)
            act_f(lin_dst(dst, q), B[q % 4][:, 0:NC], ACT.Copy).then_inc(lin_ev, 1)

        def lin_post(act, turn, pair, q, dst, gain):
            act.wait_ge(lin_mm, 24 * turn + q + 1)
            n = 24 * pair + q
            if n:
                act.wait_ge(p_add, n)
            act_f(g("sqt")[:], B[q % 4][:, 0:NC], ACT.Square).then_inc(p_sq, 1)
            m = 4 * (q // 12) + q % 4
            act_f(lin_dst(dst, q), B[q % 4][:, 0:NC], ACT.Copy, scale=vec[:, gain + m:gain + m + 1]).then_inc(lin_ev, 1)

        def post_add(dve, pair, q):
            dve.wait_ge(p_sq, 24 * pair + q + 1)
            a = g("sqa")[:, q % 12 // 4, :]
            if q < 12 and q % 4 == 0:
                CP(a, g("sqt")[:]).then_inc(p_add, 1)
            else:
                dve.wait_ge(p_add, 24 * pair + q)
                TT(a, a, g("sqt")[:], ALU.add).then_inc(p_add, 1)

        def yA(t):
            return g("yA2")[:, t % 2, :]

        def tok(t):
            return slice(P * t, P * t + P)

        def bc(ap, shape):
            return ap.broadcast_to(shape)

        def tm_no(kind, jj, t):
            return 18 * kind + 9 * jj + t

        s_dt, s_dtm, s_dtc, s_dtu = sem("dt_ready"), sem("dt_mm"), sem("dt_copies"), sem("dt_act")
        s_wdt = sem("wdt_split")
        cv_done, xc_done, cv_out = sem("conv_done"), sem("xbc_ready"), sem("conv_out")
        s_xsd = sem("ssd_skip")
        (s_cbm, s_p1, s_cols, s_exps, s_D, s_E, s_xb, s_mt, s_xdt, s_xdd, s_off, s_yd, s_stm, s_stu, s_yA, s_ysq,
         s_y, s_yt, s_yte) = (sem("ssd_" + n) for n in
                              ("masked", "first", "cols", "exps", "diff", "decay", "copies", "mixed", "xdt", "xdd", "yoff",
                               "ydiag", "states", "state", "yraw", "yrms", "ynorm", "ytrans", "yout"))
        ld_z = sem("ld_z")
        s_yo1, s_yo2, s_xb8, s_nb = sem("ssd_yoff_t"), sem("ssd_yoff_copy"), sem("ssd_xddb"), sem("ssd_newstate")
        s_nbm = sem("ssd_newstate_mm")
        ld_qk = [sem(f"ld_qk{i}") for i in range(2)]
        ld_v = sem("ld_v")
        a_lo, a_oc, b_kn, b_pn = sem("att_qk_low"), sem("att_out"), sem("smp_new_keys"), sem("smp_new_values")
        a_tr, a_tre, a_S, a_nb, a_exp, a_att, a_T, a_Te, a_pv, a_o, a_on, a_yt, a_yte = (
            sem("att_" + n) for n in ("qk_trans", "qk_copy", "scores", "max", "exp", "probs", "ptrans", "pcopy", "pv",
                                      "ocopy", "onorm", "otrans", "oout"))
        ld_kb = [sem(f"ld_kc{i}") for i in range(DB // 2)]
        b_q, b_S, b_nb, b_exp, b_p, b_T, b_Te, b_pv, b_o, b_ot, b_ote = (
            sem("smp_" + n) for n in ("qbd", "scores", "max", "exp", "probs", "ptrans", "pcopy", "pv", "ocopy", "otrans",
                                      "otok"))
        x_qh, x_ql, mk_h, mk_l = (sem("x_" + n) for n in ("q_high", "q_low", "k_high", "k_low"))
        ld_mk, ld_mv = sem("ld_mem_k"), sem("ld_mem_v")
        ld_ck, ld_cv = ([sem(f"ld_mem_cache_{x}{i}") for i in range(2)] for x in ("keys", "values"))
        x_S, x_nb, x_exp, x_p, x_T, x_Te, x_pv, x_o = (
            sem("x_" + n) for n in ("scores", "max", "exp", "probs", "ptrans", "pcopy", "pv", "out"))
        y_q, y_S, y_nb, y_exp, y_p, y_T, y_Te, y_pv, ys_o = (
            sem("xs_" + n) for n in ("qbd", "scores", "max", "exp", "probs", "ptrans", "pcopy", "pv", "out"))
        f_up, f_sg, f_hr, f_hh, f_hl, f_dn, f_de = (
            sem("ffn_" + n) for n in ("up", "silu", "hidden", "high", "low", "down", "down_add"))
        h_out, y_out = sem("h_store"), sem("y_store")
        rp_c, a_rs, ld_vs = sem("rope_chain"), sem("att_rms"), sem("ld_vs")

        block = ctx.enter_context(nc.Block())

        @block.sync
        def _(sp):
            sp.dma_start(vec[:], vecs).then_inc(ld["vec"], 16)
            sp.dma_start(g("H")[:, :, cs(0)], xT[:, :, cs(0)]).then_inc(ld["x0"], 16)
            for i in range(2):
                sp.dma_start(raw[i][:], wall[i]).then_inc(w_raw[i], 16)
            for c in range(1, CH):
                sp.dma_start(g("H")[:, :, cs(c)], xT[:, :, cs(c)]).then_inc(ld[f"x{c}"], 16)
            sp.dma_start(row[:], rows.partition_broadcast(P)).then_inc(ld["row"], 16)
            sp.dma_start(cst[:], consts).then_inc(ld["cst"], 16)

            def weights(n0, n1):
                with sp.Fori(n0 // 2, n1 // 2) as i:
                    for s in range(2):
                        sp.wait_ge(w_ready, 2 * i + s - 1)
                        sp.dma_start(raw[s][:], wall[2 * i + s]).then_inc(w_raw[s], 16)

            weights(2, I_WO + 4)
            sp.wait_ge(a_exp, 2 * H * (NT - 1))
            for b in range(6):
                if b == 5:
                    sp.wait_ge(b_q, 1)
                sp.dma_start(g(f"Kb{b}")[:, :, 0:PAST], kc[b]).then_inc(ld_kb[b // 2], 16)
                sp.dma_start(g(f"Vb{b}")[:], vc[b].rearrange("(t p) c -> p t c", p=P)).then_inc(ld_kb[b // 2], 16)
            sp.wait_ge(b_pv, 4)
            for c in range(CH):
                sp.dma_start(g("H")[:, :, cs(c)], xT[:, :, cs(c)]).then_inc(ld["xr"], 16)
            weights(I_WO + 4, I_WX)
            sp.wait_ge(n_lo, SPLIT_OX)
            sp.dma_start(g("mkT")[:], mk_o).then_inc(ld_mk, 16)
            weights(I_WX, I_WX + 2)
            sp.wait_ge(lin_mm, 48)
            for b in range(DB):
                if b >= 2:
                    sp.wait_ge(y_S, b - 1)
                sp.dma_start(g(f"cK{b % 2}")[:], cmk[b]).then_inc(ld_ck[b % 2], 16)
                if b == 0:
                    sp.dma_start(g("mvt")[:], mv_o.rearrange("(t p) c -> p t c", p=P)).then_inc(ld_mv, 16)
                if b >= 2:
                    sp.wait_ge(y_pv, b - 1)
                sp.dma_start(g(f"cV{b % 2}")[:], cmv[b].rearrange("(t p) c -> p t c", p=P)).then_inc(ld_cv[b % 2], 16)
            weights(I_WX + 2, N_ITEMS)

        @block.gpsimd
        def _(pool):
            pool.memset(one[:], 1.0).then_inc(w_hi, 1)
            pool.wait_ge(w_hi, 1)

            def split(n, s, first):
                pool.wait_ge(w_raw[s % 2], 16 * (n // 2 + 1) if first else (n - s % 2) * 8 + 16)
                if not first:
                    pool.wait_ge(w_used, n - 3)
                pool.tensor_tensor(whi[s][:], raw[s % 2][:], bc(one[:, 0:1], [P, WI]), ALU.mult).then_inc(w_hi, 1)
                pool.wait_ge(w_hi, n + 2)
                pool.tensor_tensor(wlo[s][:], raw[s % 2][:], whi[s][:].bitcast(F32), ALU.subtract).then_inc(w_ready, 1)

            for n in range(4):
                split(n, n, True)
            with pool.Fori(1, I_WO // 4) as i:
                for s in range(4):
                    split(4 * i + s, s, False)
            for s in range(3):
                split(I_WO + s, s, False)

            def by_head(ap):
                return ap.rearrange("p (h q) -> p h q", h=SH)

            xs, xdt, xdd = by_head(g("xs")[:]), by_head(g("xdt")[:]), by_head(g("xdd")[:])
            for t in range(NT):
                pool.wait_ge(s_xb, t + 1)
                if t:
                    pool.wait_ge(s_yd, t)
                pool.tensor_tensor(xdt, xs, bc(dt_t[:, t, :].unsqueeze(2), [P, SH, SP_]), ALU.mult).then_inc(s_xdt, 1)
                pool.wait_ge(s_xdt, t + 1)
                pool.wait_ge(s_exps, t + 1)
                if t:
                    pool.wait_ge(s_stm, t)
                pool.tensor_tensor(xdd, xdt, bc(g("sm")[:, 40:48].unsqueeze(2), [P, SH, SP_]), ALU.mult).then_inc(s_xdd, 1)
                pool.tensor_tensor(xs, xs, bc(row[:, R_DSK:R_DSK + SH].unsqueeze(2), [P, SH, SP_]), ALU.mult).then_inc(s_xsd, 1)

            split(I_WO + 3, 3, False)
            with pool.Fori(I_WO // 4 + 1, N_ITEMS // 4) as i:
                for s in range(4):
                    split(4 * i + s, s, False)
            for n in range(N_ITEMS // 4 * 4, N_ITEMS):
                split(n, n % 4, False)

        @block.tensor
        def _(pe):
            pe.wait_ge(setup, 1)
            pre_pe(pe, P_MIX, NC)
            pre_pe(pe, P_MIX + 1, NC)

            def tm_chunk(kind, jj):
                s = 2 * jj
                pe.wait_ge(w_ready, I_TM + 8 * kind + 2 * jj + 2)
                for t in range(NT):
                    if kind + jj == 0:
                        if t == 1:
                            pre_pe(pe, P_MIX + 2, NC)
                        pe.wait_ge(n_lo, t // 3 + 1)
                    if kind == 0 and jj == 1 and t == 3:
                        pre_pe(pe, P_MEM, MEM)
                    pe.wait_ge(tm_ev, tm_no(kind, jj, t) + 1)
                    three(B[(9 * jj + t) % 6][:, 0:256],
                          [(g("NH")[:, k, tok(t)], g("NL")[:, k, tok(t)],
                            whi[s + k // 4][:, 256 * (k % 4):256 * (k % 4) + 256],
                            wlo[s + k // 4][:, 256 * (k % 4):256 * (k % 4) + 256]) for k in range(KT)],
                          release=((0,) if t == 0 and kind + jj else (4,) if t == NT - 1 else ())).then_inc(tm_mm, 1)

            def mem_k(m):
                pe.wait_ge(w_ready, I_TM + 8 * (m // 4) + 4 + m % 4 + 1)
                if m >= 2:
                    pe.wait_ge(mem_ev, m - 1)
                three(B[6 + m % 2][:, 0:MEM], [(whi[m % 4][:, tok(k)], wlo[m % 4][:, tok(k)], g("mhi")[:, k, :],
                                                g("mlo")[:, k, :]) for k in range(KT)], release=(0,)).then_inc(mem_mm, 1)

            def mem_v(j):
                s = 2 * (j % 2)
                pe.wait_ge(w_ready, I_TM + 16 + 8 * (j // 2) + 4 + 2 * (j % 2) + 2)
                for t in range(2):
                    n = KT + 2 * j + t
                    pe.wait_ge(mem_ev, n - 1)
                    three(B[6 + n % 2][:, 0:256],
                          [(g("mhi")[:, k, tok(t)], g("mlo")[:, k, tok(t)],
                            whi[s + k // 4][:, 256 * (k % 4):256 * (k % 4) + 256],
                            wlo[s + k // 4][:, 256 * (k % 4):256 * (k % 4) + 256]) for k in range(KT)],
                          release=((0,) if t == 0 else (4,))).then_inc(mem_mm, 1)

            for kind in range(4):
                tm_chunk(kind, 0)
                tm_chunk(kind, 1)
                if kind == 0:
                    pe.wait_ge(n_lo, P_MEM + 1)
                if kind == 3:
                    pe.wait_ge(s_dt, 1)
                for i in range(4):
                    if kind < 2:
                        mem_k(4 * kind + i)
                    elif i % 2:
                        mem_v(2 * (kind - 2) + i // 2)
                if kind == 2:
                    pe.wait_ge(s_wdt, 1)
                    pe.wait_ge(mem_ev, 12)
                    for c in range(CH):
                        if c == 2:
                            pe.wait_ge(s_dtc, 1)
                        three(B[6 + c % 2][0:SH, 0:NC],
                              [(g("wdh")[:, k, :], g("wdl")[:, k, :], g("NH")[:, k, cs(c)], g("NL")[:, k, cs(c)])
                               for k in range(KT)]).then_inc(s_dtm, 1)
                    pe.wait_ge(s_dtc, CH)
                    for t in range(NT):
                        m = nc.tensor.transpose(B[7][:, SH * t:SH * t + SH], g("dtr")[0:SH, tok(t)], ident[0:SH, 0:SH])
                    m.then_inc(s_dtm, 1)
            pe.wait_ge(tm_ev, 6 + 72)
            with pe.Fori(0, KT // 4) as i:
                for s in range(4):
                    pe.wait_ge(w_ready, I_XB + s + 1 + 4 * i)
                    for c in range(CH):
                        pe.wait_ge(xb_ev, 3 * s + c + 1 + 12 * i)
                        three(B[3 * (s % 2) + c][:, 0:NC],
                              [(whi[s][:, P * k:P * k + P], wlo[s][:, P * k:P * k + P], g("NH")[:, k, cs(c)],
                                g("NL")[:, k, cs(c)]) for k in range(KT)],
                              release=((0,) if c == 0 else ())).then_inc(xb_mm, 1)

            XC = g("XC")

            def first_sums(t):
                tri = cst[:, C_TS:C_TS + P] if t == NT - 1 else cst[:, C_TP:C_TP + P]
                if t:
                    pe.wait_ge(s_D, 2 * t)
                for h in range(SH):
                    mm(B[h // 4][:, tok(h % 4)], bc(ad_t[:, t, h:h + 1], [P, P]), tri, start=True, stop=True)

            def first(t):
                smp = t == NT - 1
                tri = cst[:, C_TS:C_TS + P] if smp else cst[:, C_TP:C_TP + P]
                blk = cst[:, C_BS:C_BS + P] if smp else ones[:, :]
                if t:
                    pe.wait_ge(s_mt, t)
                    pe.wait_ge(s_xb, t)
                mm(B[2][:, 256:264], tri, ad_t[:, t, :], start=True, stop=True)
                mm(B[2][:, 264:272], blk, ad_t[:, t, :], start=True, stop=True)
                if smp:
                    for b in range(DB):
                        mm(B[2][:, 272 + 8 * b:280 + 8 * b], bc(cst[:, C_BB + b:C_BB + b + 1], [P, P]), ad_t[:, t, :],
                           start=True, stop=True)
                for gr in range(2):
                    mm(B[2][:, tok(gr)], XC[:, 4 + gr, tok(t)], XC[:, 6 + gr, tok(t)], start=True, stop=True)
                for j in range(4):
                    nc.tensor.transpose(B[3][:, tok(j)], XC[:, j, tok(t)], ident)
                if t >= 2:
                    pe.wait_ge(s_yte, t - 1)
                for j in range(2):
                    m = nc.tensor.transpose(B[4][:, tok(j)], XC[:, 4 + j, tok(t)], ident)
                m.then_inc(s_p1, 1)

            def from_state(t):
                if t:
                    pe.wait_ge(s_yA, t)
                if t < NT - 1:
                    pe.wait_ge(s_stu, t + 1)
                    for gr in range(2):
                        m = mm(B[5][:, 256 * gr:256 * gr + 256], XC[:, 6 + gr, tok(t)], g("ST")[:, 256 * gr:256 * gr + 256],
                               start=True, stop=True)
                    m.then_inc(s_off, 1)
                else:
                    pe.wait_ge(ld["h0"], 16)
                    for b in range(DB):
                        for j in range(4):
                            lo = P * t + DS * b
                            m = mm(B[5][:, P * j + DS * b:P * j + DS * b + DS], g("h0t")[:, b, tok(j)],
                                   XC[:, 6 + j // 2, lo:lo + DS], start=True, stop=True)
                    m.then_inc(s_yo1, 1)
                    pe.wait_ge(s_yo2, 1)
                    for j in range(4):
                        m = nc.tensor.transpose(B[5][:, tok(j)], g("yoT")[:, tok(j)], ident)
                    m.then_inc(s_off, 1)

            def y_turn(t):
                pe.wait_ge(s_y, t + 1)
                for j in range(4):
                    m = nc.tensor.transpose(B[4][:, tok(j)], yA(t)[:, tok(j)], ident)
                m.then_inc(s_yt, 1)

            pe.wait_ge(s_dt, 2)
            pe.wait_ge(xb_ev, 6 + 3 * KT)
            first_sums(0)
            pe.wait_ge(xc_done, KT)
            first(0)
            for t in range(NT):
                from_state(t)
                if t + 1 < NT:
                    first_sums(t + 1)
                pe.wait_ge(s_mt, t + 1)
                pe.wait_ge(s_xdt, t + 1)
                for h in range(SH):
                    m = mm(B[6][:, SP_ * h:SP_ * h + SP_], g("MT")[:, h, :], g("xdt")[:, SP_ * h:SP_ * h + SP_],
                           start=True, stop=True)
                m.then_inc(s_yd, 1)
                pe.wait_ge(s_xdd, t + 1)
                pe.wait_ge(s_xb, t + 1)
                if t < NT - 1:
                    for gr in range(2):
                        m = mm(B[7][:, 256 * gr:256 * gr + 256], g("Btm")[:, gr, :], g("xdd")[:, 256 * gr:256 * gr + 256],
                               start=True, stop=True)
                    m.then_inc(s_stm, 1)
                if t:
                    y_turn(t - 1)
                if t + 1 < NT:
                    first(t + 1)
            pe.wait_ge(s_yte, NT - 1)
            y_turn(NT - 1)

            def new_state(b):
                pe.wait_ge(s_xb8, b + 1)
                if b >= 2:
                    pe.wait_ge(s_nb, b - 1)
                for gr in range(2):
                    m = mm(B[b % 2][:, 256 * gr:256 * gr + 256], g("Btm")[:, gr, :],
                           yA(b)[:, 256 * gr:256 * gr + 256], start=True, stop=True)
                m.then_inc(s_nbm, 1)

            pe.wait_ge(s_yA, NT)
            for t in range(NT):
                if t < DB:
                    new_state(t)
                for w in range(2):
                    n = 2 * t + w
                    pe.wait_ge(ld_qk[t % 2], 32 * (t // 2 + 1))
                    if n >= 2:
                        pe.wait_ge(a_tre, n - 1)
                        pe.wait_ge(a_lo, n - 1)
                    for h in range(H):
                        m = nc.tensor.transpose(B[6 + w][:, tok(h)], g(f"qkr{t % 2}")[:, w, tok(h)], ident)
                    m.then_inc(a_tr, 1)
            pe.wait_ge(a_tre, 2 * NT)
            pe.wait_ge(a_lo, 2 * NT - 2)
            pe.wait_ge(s_nb, DB)
            pe.wait_ge(s_yte, NT)

            def scores(u):
                t, h = divmod(u, H)
                W = P * (t + 1)
                for c in range(2):
                    if u:
                        pe.wait_ge(a_exp, 2 * (u - 1) + c + 1)
                    r = slice(64 * c, 64 * c + 64)
                    for w0 in range(0, W, 512):
                        w1 = min(W, w0 + 512)
                        o = bank[c][:, w0:w1]
                        qh, ql, kh, kl = g("QTt")[r, h, tok(t)], g("QL")[r, h, tok(t)], g("KTt")[r, h, w0:w1], g("KL")[r, h, w0:w1]
                        mm(o, qh, kh, start=True, stop=False)
                        mm(o, qh, kl, start=False, stop=False)
                        m = mm(o, ql, kh, start=False, stop=True)
                    m.then_inc(a_S, 1)

            def probs_turn(u):
                pe.wait_ge(a_att, u + 1)
                if u:
                    pe.wait_ge(a_Te, u)
                for k in range(u // H + 1):
                    m = nc.tensor.transpose(B[4 + k // 4][:, tok(k % 4)], g(f"ATT{u % 2}")[:, tok(k)], ident)
                m.then_inc(a_T, 1)

            def values(u):
                t, h = divmod(u, H)
                if u == 0:
                    pe.wait_ge(ld_v, 16)
                pe.wait_ge(a_Te, u + 1)
                if h == 0 and t:
                    pe.wait_ge(a_oc, t)
                for k in range(t + 1):
                    m = mm(B[6][:, tok(h)], g("PTs")[:, tok(k)], g("V")[:, k, tok(h)], start=(k == 0), stop=(k == t))
                m.then_inc(a_pv, 1)

            def o_trans(t):
                pe.wait_ge(a_on, t + 1)
                if t:
                    pe.wait_ge(a_yte, t)
                for h in range(H):
                    m = nc.tensor.transpose(B[7][:, tok(h)], g("on")[:, tok(h)], ident)
                m.then_inc(a_yt, 1)

            U = H * (NT - 1)
            scores(0)
            for u in range(U):
                if u + 1 < U:
                    scores(u + 1)
                probs_turn(u)
                if u:
                    values(u - 1)
                if u % H == 3 and u > H:
                    o_trans(u // H - 1)
            values(U - 1)

            def s_scores(b):
                sl = b % 2
                pe.wait_ge(ld_kb[b // 2], 64)
                if b >= 2:
                    pe.wait_ge(b_exp, b - 1)
                pe.wait_ge(b_kn, b + 1)
                for h in range(H):
                    m = mm(B[sl][:, 0:PAST + DS], g("Qbd")[:, b, h, :], g(f"Kb{b}")[:, h, :], start=(h == 0),
                           stop=(h == H - 1))
                m.then_inc(b_S, 1)

            pe.wait_ge(b_q, 1)
            pe.wait_ge(a_exp, 2 * U)
            s_scores(0)
            for b in range(DB):
                sl = b % 2
                pe.wait_ge(b_p, b + 1)
                if b >= 2:
                    pe.wait_ge(b_Te, b - 1)
                for k in range(2):
                    nc.tensor.transpose(B[2 + sl][:, tok(k)], g("Pp")[:, sl, tok(k)], ident)
                nc.tensor.transpose(B[2 + sl][:, tok(2)], g("Pn")[:, b, :], ident).then_inc(b_T, 1)
                if b == 2:
                    o_trans(NT - 2)
                if b + 1 < DB:
                    s_scores(b + 1)
                pe.wait_ge(b_Te, b + 1)
                for h in range(H):
                    o = B[4 + b // 4][:, P * (b % 4) + 32 * h:P * (b % 4) + 32 * h + 32]
                    for k in range(2):
                        m = mm(o, g(f"Vb{b}")[:, k, tok(h)], g("PTb")[:, sl, P * k + 32 * h:P * k + 32 * h + 32], start=(k == 0),
                               stop=(k == 1))
                m.then_inc(b_pv, 1)
            pe.wait_ge(b_Te, DB)
            for i in range(2):
                for h in range(H):
                    m = mm(B[2 + i][:, :].rearrange("p (b r) -> p b r", b=4)[:, :, 32 * h:32 * h + 32], g("Vs")[:, tok(h)],
                           g("PTn")[:, 4 * i:4 * i + 4, 32 * h:32 * h + 32], start=True, stop=True)
                m.then_inc(b_pn, 1)
            pe.wait_ge(b_o, 1)
            pe.wait_ge(a_oc, NT - 1)
            for h in range(H):
                m = nc.tensor.transpose(B[6][:, tok(h)], g("oTs")[:, h, :], ident)
            m.then_inc(a_pv, 1)
            o_trans(NT - 1)

            YH, NH, NL = g("YH"), g("NH"), g("NL")

            def first(q):
                if q % 4 == 0 and q < 12:
                    pe.wait_ge(n_lo, SPLIT_Y + q // 4 + 1)
                lin_unit(pe, I_WO, 0, q, YH, NL)

            def second(q):
                if q % 4 == 0 and q < 12:
                    pe.wait_ge(n_lo, 7 + q // 4 + 1)
                lin_unit(pe, I_WQ, 1, q, NH, NL)

            def joined_pe(first, second, z0, p0, n_first, n_second):
                for q in range(n_first):
                    first(q)
                    if q == n_first - 8:
                        post_pe(pe, z0)
                    if q == n_first - 4:
                        post_pe(pe, z0 + 1)
                        pre_pe(pe, p0, NC)
                pre_pe(pe, p0 + 1, NC)
                for q in range(n_second):
                    second(q)
                    if q == 0:
                        post_pe(pe, z0 + 2)
                    if q == 5:
                        pre_pe(pe, p0 + 2, NC)

            joined_pe(first, second, 0, P_X, 24, 24)

            pe.wait_ge(lin_ev, 4 + 48)
            pe.wait_ge(mk_l, 1)

            def x_scores(t):
                pe.wait_ge(x_ql, t + 1)
                if t:
                    pe.wait_ge(x_exp, H * t)
                for h in range(H):
                    m = three(B[h // 2][:, MEM * (h % 2):MEM * (h % 2) + MEM],
                              [(g("QXh")[:, k, :], g("QXl")[:, k, :], g("mkh")[:, k, :], g("mkl")[:, k, :])
                               for k in (2 * h, 2 * h + 1)])
                m.then_inc(x_S, 1)

            def y_scores(b):
                pe.wait_ge(ld_ck[b % 2], 16 * (b // 2 + 1))
                pe.wait_ge(y_q, b + 1)
                if b:
                    pe.wait_ge(y_exp, b)
                for k in range(KT):
                    m = mm(B[6][0:64, 0:MEM], g("xQbd")[:, b % 2, 64 * k:64 * k + 64], g(f"cK{b % 2}")[:, k, :], start=(k == 0),
                           stop=(k == KT - 1))
                m.then_inc(y_S, 1)

            def x_trans(t):
                pe.wait_ge(x_p, t + 1)
                if t:
                    pe.wait_ge(x_Te, t)
                for h in range(H):
                    for k in range(2):
                        m = nc.tensor.transpose(B[2 + h // 2][:, tok(2 * (h % 2) + k)], g(f"xE{t % 2}")[:, h, tok(k)], ident)
                m.then_inc(x_T, 1)

            def y_trans(b):
                pe.wait_ge(y_p, b + 1)
                if b:
                    pe.wait_ge(ys_o, b)
                for k in range(2):
                    m = nc.tensor.transpose(B[7][:, 64 * k:64 * k + 64], g(f"sE{b % 2}")[:, tok(k)], ident[0:64, 0:64])
                m.then_inc(y_T, 1)

            def x_values(t):
                pe.wait_ge(x_Te, t + 1)
                if t == 0:
                    pe.wait_ge(ld_mv, 16)
                if t:
                    pe.wait_ge(x_o, t)
                for h in range(H):
                    for e in range(2):
                        for k in range(2):
                            m = mm(B[4 + h // 2][:, tok(2 * (h % 2) + e)], g("mvt")[:, k, tok(2 * h + e)],
                                   g("xPT")[:, tok(2 * h + k)], start=(k == 0), stop=(k == 1))
                m.then_inc(x_pv, 1)

            def y_values(b):
                pe.wait_ge(y_Te, b + 1)
                pe.wait_ge(ld_cv[b % 2], 16 * (b // 2 + 1))
                for h in range(H):
                    for e in range(2):
                        o = B[7][:, P + DS * (2 * h + e):P + DS * (2 * h + e) + DS]
                        for k in range(2):
                            m = mm(o, g(f"cV{b % 2}")[:, k, tok(2 * h + e)], g("sPT")[:, k, DS * h:DS * h + DS],
                                   start=(k == 0), stop=(k == 1))
                m.then_inc(y_pv, 1)

            x_scores(0)
            y_scores(0)
            for i in range(DB):
                if i + 1 < DB:
                    x_scores(i + 1)
                x_trans(i)
                if i + 1 < DB:
                    y_scores(i + 1)
                y_trans(i)
                x_values(i)
                y_values(i)

            def up_unit(q, p0, s0, ready):
                c, s = q // 4, q % 4
                if c == 0:
                    pe.wait_ge(w_ready, ready + s)
                if s % 2 == 0:
                    pe.wait_ge(f_hr, p0 + q // 2 + 1)
                w = (s0 + s) % 4
                three(B[2 * (q // 2 % 3) + q % 2][:, 0:NC],
                      [(whi[w][:, tok(k)], wlo[w][:, tok(k)], NH[:, k, cs(c)], NL[:, k, cs(c)]) for k in range(KT)],
                      release=((0,) if (c == 0 and s == 0) or (c == CH - 1 and s) else ())).then_inc(f_up, 1)

            def down(par, n0, s0, ready, hid):
                pe.wait_ge(w_ready, ready)
                pe.wait_ge(f_hl, hid)
                for q in range(3 * KT):
                    c, m_ = q // KT, q % KT
                    pe.wait_ge(f_de, n0 + q + 1)
                    three(B[6 + q % 2][:, 0:NC],
                          [(whi[(s0 + f) % 4][:, tok(m_)], wlo[(s0 + f) % 4][:, tok(m_)],
                            g(f"hid_h{par}{f}")[:, cs(c)], g(f"hid_l{par}{f}")[:, cs(c)]) for f in range(2)],
                          release=((0,) if q == 0 else (1,) if q == 3 * KT - 1 else ())).then_inc(f_dn, 1)

            def third(q):
                if q % 4 == 0 and q < 12:
                    pe.wait_ge(n_lo, SPLIT_OX + q // 4 + 1)
                lin_unit(pe, I_WX, 2, q, NH, NL)

            def fourth(q):
                if q % 4 == 0:
                    pe.wait_ge(n_lo, 13 + q // 4 + 1)
                up_unit(q, 0, 0, I_FF + 1)

            joined_pe(third, fourth, 3, P_FF, 24, 12)
            with pe.Fori(0, (NG - 1) // 2) as i:
                for x in range(2):
                    for q in range(12):
                        up_unit(q, 6 * (1 + x) + 12 * i, 2 * x, I_FF + 5 + 6 * x + 12 * i)
                    down(x, 24 * x + 48 * i, 2 * x, I_FF + 10 + 6 * x + 12 * i, 6 + 6 * x + 12 * i)
            last = 24 * (NG - 1)
            pe.wait_ge(w_ready, N_ITEMS)
            pe.wait_ge(f_hl, 6 * NG)
            pe.wait_ge(f_hr, 3 + 6 * NG)
            for q in range(3 * KT):
                c, m_ = q // KT, q % KT
                if q >= 6:
                    pe.wait_ge(f_de, 2 + last + q - 5)
                three(B[q % 6][:, 0:NC],
                      [(whi[f][:, tok(m_)], wlo[f][:, tok(m_)], g(f"hid_h0{f}")[:, cs(c)], g(f"hid_l0{f}")[:, cs(c)])
                       for f in range(2)]).then_inc(f_dn, 1)
                if q in (13, 21):
                    if q == 13:
                        pe.wait_ge(f_de, 2 + last)
                    pre_pe(pe, P_END + q // KT - 1, NC)
            pre_pe(pe, P_END + 2, NC)

        @block.scalar
        def _(act):
            H_, NH, NLf = g("H"), g("NH"), g("NLf")
            act.wait_ge(setup, 1)
            act.wait_ge(ld["vec"], 16)

            def pre_act(p, src, tmp, hi, w):
                for i in range(4):
                    pre_sq(act, p, i, src, w)
                pre_std(act, p, w)
                pre_hi(act, p, tmp, hi)

            for c in range(CH):
                act.wait_ge(ld[f"x{c}"], 16)
                for i in range(4):
                    pre_sq(act, P_MIX + c, i, H_[:, :, cs(c)], NC)
                if c:
                    pre_hi(act, P_MIX + c - 1, NLf[:, :, cs(c - 1)], NH[:, :, cs(c - 1)])
                pre_std(act, P_MIX + c, NC)
            pre_hi(act, P_MIX + CH - 1, NLf[:, :, cs(CH - 1)], NH[:, :, cs(CH - 1)])
            act.dma_start(g("mraw")[:], memT).then_inc(ld["mem"], 16)

            dram = [zs_d, q_d, k_o, v_o]

            def store(kind, jj):
                j = 2 * kind + jj
                act.wait_ge(tm_ev, 6 + 9 * (j + 1))
                act.dma_start(dram[kind].rearrange("(t p) c -> p t c", p=P)[:, :, 256 * jj:256 * jj + 256],
                              g(f"stg{j % 4}")[:]).then_inc(st_out[j % 4], 16)

            def tm_out(kind, jj, f):
                j = 2 * kind + jj
                if j >= 4:
                    act.wait_ge(st_out[j % 4], 16)
                for t in range(NT):
                    n = tm_no(kind, jj, t)
                    act.wait_ge(tm_mm, n + 1)
                    act_f(g(f"stg{j % 4}")[:, t, :], B[(9 * jj + t) % 6][:, 0:256], f).then_inc(tm_ev, 1)
                store(kind, jj)

            def mem_k_out(m):
                act.wait_ge(mem_mm, m + 1)
                act_f(g("mraw")[:, m, :], B[6 + m % 2][:, 0:MEM], ACT.Copy).then_inc(mem_ev, 1)

            def mem_v_out(j):
                for t in range(2):
                    n = KT + 2 * j + t
                    act.wait_ge(mem_mm, n + 1)
                    act_f(g("mvs")[:, t, 256 * j:256 * j + 256], B[6 + n % 2][:, 0:256], ACT.Copy).then_inc(mem_ev, 1)

            tm_out(0, 0, ACT.Silu)
            act.wait_ge(ld["mem"], 16)
            pre_act(P_MEM, g("mraw")[:], g("mraw")[:], g("mhi")[:], MEM)
            tm_out(0, 1, ACT.Silu)
            act.wait_ge(n_lo, P_MEM + 1)
            act.dma_start(g("wdr")[:], wdt).then_inc(ld["wdt"], 16)
            for m in range(4):
                mem_k_out(m)
            act.wait_ge(setup, 2)
            act_f(row[:, R_LAM:R_LAM + 2], row[:, R_LAM:R_LAM + 2], ACT.Exp).then_inc(s_dtu, 1)
            act_f(row[:, R_ALOG:R_ALOG + SH], row[:, R_ALOG:R_ALOG + SH], ACT.Exp).then_inc(s_dtu, 1)
            act.wait_ge(ld["wdt"], 16)
            act_f(g("wdh")[:], g("wdr")[:], ACT.Copy).then_inc(s_dtu, 1)
            store(1, 0)
            store(1, 1)
            for m in range(4, KT):
                mem_k_out(m)
            act.wait_ge(mem_ev, KT)
            act.dma_start(mk_o, g("mraw")[:]).then_inc(mem_out, 16)
            store(2, 0)
            store(2, 1)
            for j in range(2):
                mem_v_out(j)
            for c in range(CH):
                act.wait_ge(s_dtm, c + 1)
                act_f(g("dtr")[0:SH, cs(c)], B[6 + c % 2][0:SH, 0:NC], ACT.Copy).then_inc(s_dtc, 1)
            D6 = g("dts")
            act.wait_ge(s_dt, 1)
            act_f(D6[:, :, 1], D6[:, :, 0], ACT.Abs).then_inc(s_dtu, 1)
            act.wait_ge(s_dtu, 4)
            act_f(D6[:, :, 2], D6[:, :, 1], ACT.Exp, scale=-1.0).then_inc(s_dtu, 1)
            act.wait_ge(s_dtu, 5)
            act_f(D6[:, :, 3], D6[:, :, 2], ACT.Ln, bias=1.0).then_inc(s_dtu, 1)
            tm_out(3, 0, ACT.Copy)
            tm_out(3, 1, ACT.Copy)
            for j in range(2, 4):
                mem_v_out(j)
            act.wait_ge(mem_ev, 2 * KT)
            act.dma_start(mv_o.rearrange("(t p) c -> p t c", p=P), g("mvs")[:]).then_inc(mem_out, 16)
            act.wait_ge(s_dt, 2)
            act.dma_start(g("cvi")[:], sconv).then_inc(ld["scv"], 16)
            act.wait_ge(ld["scv"], 16)

            def xp_s(m):
                return g(f"xp{m % 2}")[:, 3 + SEQ:XP].rearrange("p (b s) -> p b s", b=DB)

            def silu(m):
                act.wait_ge(cv_done, m + 1)
                if m == 0:
                    for i in range(4):
                        act.wait_ge(st_out[i], 32)
                act_f(g("XC")[:, m, :], g("acc")[:], ACT.Silu).then_inc(xc_done, 1)

            for m in range(KT):
                if m >= 2:
                    act.wait_ge(cv_done, m - 1)
                act_f(xp_s(m)[:, :, 0:3], g("cvi")[:, m, :].rearrange("p (b s) -> p b s", b=DB), ACT.Copy)
                for c in range(CH):
                    act.wait_ge(xb_mm, 3 * m + c + 1)
                    src = B[3 * (m % 2) + c]
                    if c < 2:
                        act_f(g(f"xp{m % 2}")[:, 3 + NC * c:3 + NC * c + NC], src[:, 0:NC], ACT.Copy).then_inc(xb_ev, 1)
                    else:
                        w = SEQ - NC * c
                        act_f(g(f"xp{m % 2}")[:, 3 + NC * c:3 + SEQ], src[:, 0:w], ACT.Copy)
                        act_f(xp_s(m)[:, :, 3:], src[:, w:NC].rearrange("p (b s) -> p b s", b=DB), ACT.Copy).then_inc(xb_ev, 1)
                if m:
                    silu(m - 1)
            silu(KT - 1)
            act.dma_start(conv_o, g("cvo")[:]).then_inc(cv_out, 16)
            act.dma_start(g("h0t")[:], h0).then_inc(ld["h0"], 16)
            act.wait_ge(cv_out, 16)
            act.wait_ge(xc_done, KT)

            sm = g("sm")

            def y_rms(t):
                act.wait_ge(s_yA, t + 1)
                if t:
                    act.wait_ge(s_y, t)
                for gr in range(2):
                    x = act_f(g("sqs")[:, 256 * gr:256 * gr + 256], yA(t)[:, 256 * gr:256 * gr + 256], ACT.Square,
                              accum_out=sm[:, 112 + gr:113 + gr])
                alink(act, x)
                alink(act, act_f(sm[:, 114:116], sm[:, 112:114], ACT.Ln, bias=eps5[:, :], scale=1.0 / 256))
                act_f(sm[:, 116:118], sm[:, 114:116], ACT.Exp, scale=-0.5).then_inc(s_ysq, 1)

            def y_evac(t):
                act.wait_ge(s_yt, t + 1)
                for j in range(4):
                    x = act_f(g("YT")[:, j, tok(t)], B[4][:, tok(j)], ACT.Copy, scale=vec[:, V_SSM + j:V_SSM + j + 1])
                x.then_inc(s_yte, 1)

            for t in range(NT):
                smp = t == NT - 1
                if t:
                    act.wait_ge(s_yA, t)
                act.dma_start(g("zt")[:], zs_d[P * t:P * t + P, :]).then_inc(ld_z, 16)
                if smp:
                    act.dma_start(ssm_o[0], g("ST")[:]).then_inc(out_s, 16)
                act.wait_ge(s_p1, t + 1)
                if t:
                    act.wait_ge(s_stm, t)
                act_f(g("Btm")[:].rearrange("p a n -> p (a n)"), B[4][:, 0:256], ACT.Copy)
                act_f(g("xs")[:], B[3][:, :], ACT.Copy).then_inc(s_xb, 1)
                act.wait_ge(s_cols, t + 1)
                if smp:
                    act_f(sm[:, 48:112], sm[:, 48:112], ACT.Exp)
                act_f(sm[:, 24:48], sm[:, 0:24], ACT.Exp).then_inc(s_exps, 1)
                for i in range(2):
                    act.wait_ge(s_D, 2 * t + i + 1)
                    e = g("E")[:, 4 * i:4 * i + 4, :]
                    act_f(e, e, ACT.Exp).then_inc(s_E, 1)
                if smp:
                    act.wait_ge(s_yo1, 1)
                    act_f(g("yoT")[:], B[5][:, :], ACT.Copy).then_inc(s_yo2, 1)
                if t:
                    y_rms(t - 1)
                    y_evac(t - 1)
            y_rms(NT - 1)
            y_evac(NT - 1)

            def load_qk(t):
                if t >= 2:
                    act.wait_ge(a_tr, 2 * t - 2)
                act.dma_start(g(f"qkr{t % 2}")[:, 0, :], q_d[P * t:P * t + P, :]).then_inc(ld_qk[t % 2], 16)
                act.dma_start(g(f"qkr{t % 2}")[:, 1, :], k_o[P * t:P * t + P, :]).then_inc(ld_qk[t % 2], 16)

            load_qk(0)
            act.wait_ge(out_s, 16)
            load_qk(1)
            act.wait_ge(mem_out, 32)
            for t in range(NT):
                for w in range(2):
                    n = 2 * t + w
                    act.wait_ge(a_tr, n + 1)
                    if t < NT - 1:
                        dst = g("QTt" if w == 0 else "KTt")[:, :, tok(t)]
                    else:
                        dst = g("QTs" if w == 0 else "KTs")[:]
                    act_f(dst, B[6 + w][:, :].rearrange("p (h q) -> p h q", h=H), ACT.Copy).then_inc(a_tre, 1)
                if t + 2 < NT:
                    load_qk(t + 2)
                if t == DB - 1:
                    act.wait_ge(s_nb, DB)
                    act.dma_start(ssm_o[1:1 + DB].rearrange("b n q -> n b q"), g("h0t")[:]).then_inc(out_s, 16)
                    act.dma_start(g("V")[:], v_o.rearrange("(t p) c -> p t c", p=P)).then_inc(ld_v, 16)
            act.wait_ge(out_s, 32)
            act.wait_ge(a_tr, 2 * NT)
            asm = g("at_sm")

            def exps(u):
                t, h = divmod(u, H)
                W = P * (t + 1)
                a = 8 * (u % 2)
                for c in range(2):
                    act.wait_ge(a_nb, 2 * u + c + 1)
                    if u >= 2:
                        act.wait_ge(a_att, u - 1)
                    act_f(g(f"E{c}{u % 2}")[:, 0:W], bank[c][:, 0:W], ACT.Exp, bias=asm[:, a + c:a + c + 1], scale=0.125,
                          accum_out=asm[:, a + 2 + c:a + 3 + c]).then_inc(a_exp, 1)

            def copy_pt(u):
                act.wait_ge(a_T, u + 1)
                if u:
                    act.wait_ge(a_pv, u)
                W = P * (u // H + 1)
                for w0 in range(0, W, 512):
                    w1 = min(W, w0 + 512)
                    x = act_f(g("PTs")[:, w0:w1], B[4 + w0 // 512][:, 0:w1 - w0], ACT.Copy)
                x.then_inc(a_Te, 1)

            def o_norm(t):
                act.wait_ge(a_oc, t + 1)
                if t:
                    act.wait_ge(a_on, t)
                for h in range(H):
                    x = act_f(g("osq")[:, tok(h)], g("on")[:, tok(h)], ACT.Square, accum_out=asm[:, 40 + h:41 + h])
                alink(act, x)
                alink(act, act_f(asm[:, 44:48], asm[:, 40:44], ACT.Ln, bias=eps5[:, :], scale=1.0 / DH))
                act_f(asm[:, 48:52], asm[:, 44:48], ACT.Exp, scale=-0.5).then_inc(a_rs, 1)

            def o_evac(t):
                act.wait_ge(a_yt, t + 1)
                act_f(g("YT")[:, 4:8, tok(t)], B[7][:, :].rearrange("p (h q) -> p h q", h=H), ACT.Copy,
                      scale=vec[:, V_SUB:V_SUB + 1]).then_inc(a_yte, 1)

            U = H * (NT - 1)
            exps(0)
            for u in range(U):
                if u + 1 < U:
                    exps(u + 1)
                copy_pt(u)
                if u % H == 1 and u > H:
                    o_norm(u // H - 1)
                if u % H == 0 and u >= 2 * H:
                    o_evac(u // H - 2)

            def load_kb(b):
                act.dma_start(g(f"Kb{b}")[:, :, 0:PAST], kc[b]).then_inc(ld_kb[b // 2], 16)
                act.dma_start(g(f"Vb{b}")[:], vc[b].rearrange("(t p) c -> p t c", p=P)).then_inc(ld_kb[b // 2], 16)

            o_evac(NT - 3)
            act.wait_ge(a_pv, U)
            act.dma_start(g("Vs")[:], v_o[SEQ:NTOK, :]).then_inc(ld_vs, 16)
            for b in (6, 7):
                load_kb(b)
            act.wait_ge(ld_vs, 16)

            def s_exp(b):
                a = 8 * (b % 2)
                act.wait_ge(b_nb, b + 1)
                act_f(g("Es")[:, b % 2, :], B[b % 2][:, 0:PAST + DS], ACT.Exp, bias=asm[:, a:a + 1], scale=0.125,
                      accum_out=asm[:, a + 2:a + 3]).then_inc(b_exp, 1)

            s_exp(0)
            for b in range(DB):
                act.wait_ge(b_T, b + 1)
                if b >= 2:
                    act.wait_ge(b_pv, b - 1)
                act_f(g("PTn")[:, b, :], B[2 + b % 2][:, 256:384], ACT.Copy)
                act_f(g("PTb")[:, b % 2, :], B[2 + b % 2][:, 0:256], ACT.Copy).then_inc(b_Te, 1)
                if b + 1 < DB:
                    s_exp(b + 1)
                if b == 0:
                    o_norm(NT - 2)
                if b == 2:
                    o_evac(NT - 2)
            def y_high(c):
                act_f(g("YH")[:, :, cs(c)], g("YT")[:, :, cs(c)], ACT.Copy).then_inc(n_hi, 1)

            act.wait_ge(b_S, DB)
            act.wait_ge(a_yte, NT - 1)
            act.wait_ge(s_yte, NT)
            y_high(0)
            o_norm(NT - 1)
            y_high(1)
            o_evac(NT - 1)
            act.wait_ge(a_yte, NT)
            y_high(2)

            def squares(p, c, i0, i1):
                for i in range(i0, i1):
                    pre_sq(act, p + c, i, H_[:, :, cs(c)], NC)

            def joined_act(first, second, z0, p0, n_second, keep=None):
                for q in range(24):
                    if q == 20:
                        act.wait_ge(n_res, z0 + 1)
                        squares(p0, 0, 0, 2)
                        if keep:
                            keep(0)
                    if q == 23:
                        pre_hi(act, p0, NLf[:, :, cs(0)], NH[:, :, cs(0)])
                        act.wait_ge(n_res, z0 + 2)
                        squares(p0, 1, 0, 2)
                        if keep:
                            keep(1)
                    first(q)
                    if q == 16:
                        post_std(act, z0)
                    if q == 20:
                        post_std(act, z0 + 1)
                        squares(p0, 0, 2, 4)
                        pre_std(act, p0, NC)
                squares(p0, 1, 2, 4)
                pre_std(act, p0 + 1, NC)
                for q in range(n_second):
                    second(q)
                    if q == 0:
                        post_std(act, z0 + 2)
                        pre_hi(act, p0 + 1, NLf[:, :, cs(1)], NH[:, :, cs(1)])
                    if q == 2:
                        act.wait_ge(n_res, z0 + 3)
                        squares(p0, 2, 0, 2)
                        if keep:
                            keep(2)
                    if q == 3:
                        squares(p0, 2, 2, 4)
                        pre_std(act, p0 + 2, NC)
                        pre_hi(act, p0 + 2, NLf[:, :, cs(2)], NH[:, :, cs(2)])

            joined_act(lambda q: lin_post(act, 0, 0, q, g("MIX"), G_POSTMIX),
                       lambda q: lin_copy(act, 1, q, g("QX")), 0, P_X, 24)

            xm = g("xm")

            def x_exps(t):
                act.wait_ge(x_nb, t + 1)
                if t >= 2:
                    act.wait_ge(x_T, t - 1)
                for h in range(H):
                    act_f(g(f"xE{t % 2}")[:, h, :], B[h // 2][:, MEM * (h % 2):MEM * (h % 2) + MEM], ACT.Exp,
                          bias=xm[:, 4 + h:5 + h], scale=1.0 / 16, accum_out=xm[:, 8 + h:9 + h]).then_inc(x_exp, 1)

            def y_exps(b):
                act.wait_ge(y_nb, b + 1)
                if b >= 2:
                    act.wait_ge(y_T, b - 1)
                act_f(g(f"sE{b % 2}")[:, :], B[6][0:64, 0:MEM], ACT.Exp, bias=xm[0:64, 17:18], scale=1.0 / 16,
                      accum_out=xm[0:64, 18:19]).then_inc(y_exp, 1)

            def x_copy(t):
                act.wait_ge(x_T, t + 1)
                if t:
                    act.wait_ge(x_pv, t)
                for j in range(2):
                    x = act_f(g("xPT")[:, 512 * j:512 * j + 512], B[2 + j][:, :], ACT.Copy)
                x.then_inc(x_Te, 1)

            def y_copy(b):
                act.wait_ge(y_T, b + 1)
                if b:
                    act.wait_ge(y_pv, b)
                act_f(g("sPT")[:].rearrange("p a n -> p (a n)"), B[7][:, 0:128], ACT.Copy).then_inc(y_Te, 1)

            def q_high(t):
                if t:
                    act.wait_ge(x_S, t)
                act_f(g("QXh")[:], g("QX")[:, :, tok(t)], ACT.Copy).then_inc(x_qh, 1)

            act.wait_ge(lin_ev, 4 + 48)
            act.wait_ge(ld_mk, 16)
            act_f(g("mkh")[:], g("mkT")[:], ACT.Copy).then_inc(mk_h, 1)
            act.wait_ge(mk_l, 1)
            q_high(0)
            x_exps(0)
            q_high(1)
            y_exps(0)
            for i in range(DB):
                if i + 1 < DB:
                    x_exps(i + 1)
                x_copy(i)
                if i + 1 < DB:
                    y_exps(i + 1)
                y_copy(i)
                if i + 2 < DB:
                    q_high(i + 2)
            act.wait_ge(ys_o, DB)
            act.wait_ge(x_o, NT - 1)
            for c in range(CH):
                act_f(NH[:, :, cs(c)], g("QX")[:, :, cs(c)], ACT.Copy).then_inc(n_hi, 1)

            def keep(c):
                act.dma_start(h_d[:, :, cs(c)], H_[:, :, cs(c)]).then_inc(h_out, 16)

            def gate(n):
                act.wait_ge(f_up, 2 * n + 1)
                if n >= 2:
                    act.wait_ge(f_hr, 3 + n - 1)
                act_f(g(f"sg{n % 2}")[:], B[2 * (n % 3)][:, 0:NC], ACT.Silu).then_inc(f_sg, 1)

            def hid_high(n):
                gi, c, f = n // 6, n % 6 // 2, n % 2
                act.wait_ge(f_hr, 3 + n + 1)
                if n == 0:
                    act.wait_ge(h_out, 16 * CH)
                if n % 6 == 0 and gi >= 2:
                    act.wait_ge(f_dn, 24 * (gi - 1))
                act_f(g(f"hid_h{gi % 2}{f}")[:, cs(c)], g(f"hr{n % 2}")[:], ACT.Copy).then_inc(f_hh, 1)

            joined_act(lambda q: lin_post(act, 2, 1, q, g("QX"), G_POSTX), lambda q: None, 3, P_FF, 4, keep)
            for n in range(6 * NG):
                gate(n)
                hid_high(n)
            def store_y(c):
                act.wait_ge(n_res, 2 * CH + c + 1)
                act.dma_start(y_o[:, :, cs(c)], g("Hback")[:, :, cs(c)]).then_inc(y_out, 16)

            act.wait_ge(f_up, 12 * NG)
            for c in range(CH):
                act.dma_start(g("Hback")[:, :, cs(c)], h_d[:, :, cs(c)]).then_inc(ld["Hb0"], 16)
            act.wait_ge(f_hl, 6 * NG)
            for c in range(CH):
                act.wait_ge(f_de, 2 + 24 * (NG - 1) + KT * (c + 1))
                for i in range(4):
                    pre_sq(act, P_END + c, i, g("ACC")[:, :, cs(c)], NC)
                pre_std(act, P_END + c, NC)
                if c:
                    store_y(c - 1)
            store_y(CH - 1)
            act.wait_ge(y_out, 16 * CH)

        @block.vector
        def _(dve):
            link = lambda ins: dlink(dve, ins)
            H_, NH, NL, NLf = g("H"), g("NH"), g("NL"), g("NLf")
            nc.vector.memset(ones[:], 1.0)
            nc.vector.memset(eps6[:], 1e-6)
            nc.vector.memset(eps5[:], 1e-5).then_inc(setup, 1)
            nc.vector.memset(cred[:, 0:1], 0.0).then_inc(lin_ev, 4)
            nc.vector.memset(cred[:, 1:2], 0.0).then_inc(tm_ev, 6)
            nc.vector.memset(cred[:, 2:3], 0.0).then_inc(f_hr, 3)
            nc.vector.memset(cred[:, 3:4], 0.0).then_inc(f_de, 2)
            nc.vector.memset(cred[:, 4:5], 0.0).then_inc(xb_ev, 6)
            dve.wait_ge(ld["vec"], 16)
            for c in range(CH):
                pre_dve(dve, P_MIX + c, H_[:, :, cs(c)], NLf[:, :, cs(c)], NL[:, :, cs(c)], NH[:, :, cs(c)], G_PREMIX, NC)
            pre_dve(dve, P_MEM, g("mraw"), g("mraw")[:], g("mlo")[:], g("mhi")[:], G_MEM, MEM)
            dve.wait_ge(ld["row"], 16)
            lq = row[:, R_LAM:R_LAM + 256].rearrange("p (a b d) -> p a b d", a=2, b=2)
            link(TT(lq[:, :, 0, :], lq[:, :, 0, :], lq[:, :, 1, :], ALU.mult))
            link(nc.vector.tensor_reduce(lams[:], lq[:, :, 0, :], AX, ALU.add))
            CP(row[:, R_LAM:R_LAM + 2], lams[:]).then_inc(setup, 1)
            dve.wait_ge(s_dtu, 3)
            TT(g("wdl")[:], g("wdr")[:], g("wdh")[:].bitcast(F32), ALU.subtract).then_inc(s_wdt, 1)
            link(TT(nlam[:], row[:, R_LAM + 1:R_LAM + 2], row[:, R_LAM:R_LAM + 1], ALU.subtract))
            link(TS(nlam[:], nlam[:], -0.2, None, ALU.add))
            link(TS(row[:, R_ALOG:R_ALOG + SH], row[:, R_ALOG:R_ALOG + SH], -1.0, None, ALU.mult))
            dve.wait_ge(ld["cst"], 16)
            link(TT(coef[:], cst[:, C_C1:C_C1 + 1], nlam[:], ALU.mult))
            link(TT(coef[:], coef[:], cst[:, C_C0:C_C0 + 1], ALU.add))
            link(TS(vec[:, V_SUB:V_SUB + 1], vec[:, V_SUB:V_SUB + 1], 0.8, None, ALU.mult))
            for kind in (1, 2):
                for jj in range(2):
                    j = 2 * kind + jj
                    dve.wait_ge(tm_ev, 6 + 9 * j)
                    if j >= 4:
                        dve.wait_ge(st_out[j % 4], 16)
                    for t in range(NT):
                        n = tm_no(kind, jj, t)
                        dve.wait_ge(tm_mm, n + 1)
                        X = B[(9 * jj + t) % 6][:, 0:256].rearrange("p (g d) -> p g d", d=32)
                        cos = bc(cst[:, C_COS + 32 * t:C_COS + 32 * t + 32].unsqueeze(1), [P, 8, 32])
                        sin = bc(cst[:, C_SIN + 32 * t:C_SIN + 32 * t + 32].unsqueeze(1), [P, 8, 32])
                        A = g("rpA")[:].rearrange("p (g d) -> p g d", d=32)
                        R = g("rpB")[:].rearrange("p (g d) -> p g d", d=32)
                        TT(A, X, cos, ALU.mult)
                        TT(R, X, sin, ALU.mult).then_inc(rp_c, 1)
                        dve.wait_ge(rp_c, 2 * (n - 18) + 1)
                        A4 = g("rpA")[:].rearrange("p (g x d) -> p g x d", x=2, d=32)
                        R4 = g("rpB")[:].rearrange("p (g x d) -> p g x d", x=2, d=32)
                        O4 = g(f"stg{j % 4}")[:, t, :].rearrange("p (g x d) -> p g x d", x=2, d=32)
                        TT(O4[:, :, 0, :], A4[:, :, 0, :], R4[:, :, 1, :], ALU.subtract).then_inc(rp_c, 1)
                        TT(O4[:, :, 1, :], A4[:, :, 1, :], R4[:, :, 0, :], ALU.add).then_inc(tm_ev, 1)
                        dve.wait_ge(tm_ev, 6 + n + 1)
            D6 = g("dts")
            dve.wait_ge(s_dtm, CH + 1)
            TT(D6[:, :, 0].rearrange("p (t h) -> p t h", h=SH), B[7][:, 0:72].rearrange("p (t h) -> p t h", h=SH),
               bc(row[:, R_DTB:R_DTB + SH].unsqueeze(1), [P, NT, SH]), ALU.add).then_inc(s_dt, 1)
            dve.wait_ge(s_dtu, 6)
            u, e, ln = D6[:, :, 0], D6[:, :, 2], D6[:, :, 3]
            t1, t2 = D6[:, :, 4], D6[:, :, 5]
            link(TS(t1, e, 1.0, None, ALU.add))
            link(TS(t1, t1, -1.0, 1e-30, ALU.add, ALU.max))
            link(nc.vector.reciprocal(t2, t1))
            link(TT(t2, t2, e, ALU.mult))
            link(TT(t2, t2, ln, ALU.mult))
            link(TS(t1, e, 5.9e-8, None, ALU.min))
            link(TT(t2, t2, t1, ALU.max))
            link(TS(t1, u, 0.0, None, ALU.max))
            link(TT(dt_t[:].rearrange("p t h -> p (t h)"), t1, t2, ALU.add))
            TT(ad_t[:], dt_t[:], bc(row[:, R_ALOG:R_ALOG + SH].unsqueeze(1), [P, NT, SH]), ALU.mult).then_inc(s_dt, 1)
            dve.wait_ge(s_dt, 2)
            for i in range(2):
                link(nc.vector.memset(g(f"xp{i}")[:, 0:3], 0.0))
            acc = g("acc")
            accs = acc[:, SEQ:NTOK].rearrange("p (b s) -> p b s", b=DB)
            for m in range(KT):
                x = g(f"xp{m % 2}")
                xs_ = x[:, 3 + SEQ:XP].rearrange("p (b s) -> p b s", b=DB)
                dve.wait_ge(xb_ev, 6 + 3 * (m + 1))
                if m:
                    dve.wait_ge(xc_done, m)
                w = [vec[:, V_CW + 4 * m + j:V_CW + 4 * m + j + 1] for j in range(4)]
                cb = vec[:, V_CB + m:V_CB + m + 1]
                TS(acc[:, 0:SEQ], x[:, 0:SEQ], w[0], cb, ALU.mult, ALU.add)
                link(TS(accs, xs_[:, :, 0:DS], w[0], cb, ALU.mult, ALU.add))
                for j in range(1, 4):
                    STT(out=acc[:, 0:SEQ], in0=x[:, j:j + SEQ], scalar=w[j], in1=acc[:, 0:SEQ], op0=ALU.mult, op1=ALU.add)
                    if j < 3:
                        link(STT(out=accs, in0=xs_[:, :, j:j + DS], scalar=w[j], in1=accs, op0=ALU.mult, op1=ALU.add))
                    else:
                        STT(out=accs, in0=xs_[:, :, j:j + DS], scalar=w[j], in1=accs, op0=ALU.mult, op1=ALU.add)
                CP(g("cvo")[:, m, 0:3], x[:, SEQ:SEQ + 3])
                CP(g("cvo")[:, m, 3:27].rearrange("p (b s) -> p b s", b=DB), xs_[:, :, DS:DS + 3]).then_inc(cv_done, 1)

            dve.wait_ge(xc_done, KT)
            dve.wait_ge(cv_out, 16)
            sm, E, MT, xs, xdt, xdd, ST = (g(n) for n in ("sm", "E", "MT", "xs", "xdt", "xdd", "ST"))

            def heads(ap):
                return ap.rearrange("p (h q) -> p h q", h=SH)

            def y_scale(t):
                dve.wait_ge(s_ysq, t + 1)
                y = yA(t).rearrange("p (a q) -> p a q", a=2)
                TT(y, y, bc(sm[:, 116:118].unsqueeze(2), [P, 2, 256]), ALU.mult).then_inc(s_y, 1)

            nc.vector.memset(ST[:], 0.0).then_inc(s_stu, 1)
            for t in range(NT):
                smp = t == NT - 1
                tri = cst[:, C_TS:C_TS + P] if smp else cst[:, C_TP:C_TP + P]
                y = yA(t)
                dve.wait_ge(s_p1, t + 1)
                if t:
                    dve.wait_ge(s_mt, t)
                if smp:
                    CP(sm[:, 48:112], B[2][:, 272:336])
                link(CP(sm[:, 0:16], B[2][:, 256:272]))
                TT(sm[:, 16:24], sm[:, 8:16], sm[:, 0:8], ALU.subtract).then_inc(s_cols, 1)
                for h in range(SH):
                    m = TS(E[:, h, :], B[h // 4][:, tok(h % 4)], sm[:, h:h + 1], 0.0, ALU.subtract, ALU.min)
                    if h % 4 == 3:
                        m.then_inc(s_D, 1)
                TT(g("cbm")[:], B[2][:, 0:256].rearrange("p (a l) -> p a l", a=2), bc(tri.unsqueeze(1), [P, 2, P]),
                   ALU.mult).then_inc(s_cbm, 1)
                dve.wait_ge(s_cbm, t + 1)
                dve.wait_ge(s_E, 2 * t + 2)
                TT(MT[:].rearrange("p (a r) l -> p a r l", a=2), E[:].rearrange("p (a r) l -> p a r l", a=2),
                   bc(g("cbm")[:].unsqueeze(2), [P, 2, 4, P]), ALU.mult).then_inc(s_mt, 1)
                dve.wait_ge(s_off, t + 1)
                if t >= 2:
                    dve.wait_ge(s_yt, t - 1)
                m = TT(heads(y), heads(B[5][:, :]), bc(sm[:, 24:32].unsqueeze(2), [P, SH, SP_]), ALU.mult)
                if not smp:
                    m = TT(heads(ST[:]), heads(ST[:]), bc(sm[:, 32:40].unsqueeze(2), [P, SH, SP_]), ALU.mult)
                link(m)
                dve.wait_ge(s_xsd, t + 1)
                link(TT(y, y, xs[:], ALU.add))
                if t:
                    y_scale(t - 1)
                dve.wait_ge(s_yd, t + 1)
                link(TT(y, y, B[6][:, :], ALU.add))
                if not smp:
                    dve.wait_ge(s_stm, t + 1)
                    TT(ST[:], ST[:], B[7][:, :], ALU.add).then_inc(s_stu, 1)
                dve.wait_ge(ld_z, 16 * (t + 1))
                TT(y, y, g("zt")[:], ALU.mult).then_inc(s_yA, 1)
            dve.wait_ge(s_yA, NT)
            y_scale(NT - 1)
            dve.wait_ge(s_yt, NT)

            dve.wait_ge(s_xdd, NT)

            def part(b):
                if b >= 2:
                    dve.wait_ge(s_nbm, b - 1)
                TS(yA(b), xdd[:], cst[:, C_BB + b:C_BB + b + 1], None, ALU.mult).then_inc(s_xb8, 1)

            asm = g("at_sm")
            dve.wait_ge(mem_out, 32)
            part(0)
            for t in range(NT - 1):
                b = t
                if b + 1 < DB:
                    part(b + 1)
                hb = g("h0t")[:, b, :]
                link(TT(heads(hb), heads(hb), bc(sm[:, 48 + 8 * b:56 + 8 * b].unsqueeze(2), [P, SH, SP_]), ALU.mult))
                dve.wait_ge(s_nbm, b + 1)
                TT(hb, hb, B[b % 2][:, :], ALU.add).then_inc(s_nb, 1)
                for w in range(2):
                    dve.wait_ge(a_tre, 2 * t + w + 1)
                    hi = g("QTt" if w == 0 else "KTt")[:, :, tok(t)]
                    TT(g("QL" if w == 0 else "KL")[:, :, tok(t)], B[6 + w][:, :].rearrange("p (h q) -> p h q", h=H),
                       hi.bitcast(F32), ALU.subtract).then_inc(a_lo, 1)

            def maxes(u):
                t, h = divmod(u, H)
                W = P * (t + 1)
                a = 8 * (u % 2)
                for c in range(2):
                    dve.wait_ge(a_S, 2 * u + c + 1)
                    link(nc.vector.memset(bank[c][0:64, W - 64:W], BIG))
                    link(nc.vector.tensor_reduce(asm[:, a + 4 + c:a + 5 + c], bank[c][:, 0:W], AX, ALU.max))
                    TS(asm[:, a + c:a + c + 1], asm[:, a + 4 + c:a + 5 + c], -0.125, None, ALU.mult).then_inc(a_nb, 1)

            def r0(t):
                return asm[:, 32 + 4 * (t % 2):36 + 4 * (t % 2)]

            def probs(u):
                t, h = divmod(u, H)
                W = P * (t + 1)
                a = 8 * (u % 2)
                dve.wait_ge(a_exp, 2 * u + 2)
                nc.vector.reciprocal(r0(t)[:, h:h + 1], asm[:, a + 2:a + 3])
                link(nc.vector.reciprocal(asm[:, a + 7:a + 8], asm[:, a + 3:a + 4]))
                link(TT(asm[:, a + 7:a + 8], asm[:, a + 7:a + 8], nlam[:, :], ALU.mult))
                link(TT(asm[:, a + 7:a + 8], asm[:, a + 7:a + 8], asm[:, a + 2:a + 3], ALU.mult))
                if u >= 2:
                    dve.wait_ge(a_T, u - 1)
                STT(out=g(f"ATT{u % 2}")[:, 0:W], in0=g(f"E1{u % 2}")[:, 0:W], scalar=asm[:, a + 7:a + 8],
                    in1=g(f"E0{u % 2}")[:, 0:W], op0=ALU.mult, op1=ALU.add).then_inc(a_att, 1)

            on = g("on")[:].rearrange("p (h e) -> p h e", h=H)

            def o_copy(t):
                dve.wait_ge(a_pv, H * (t + 1) if t < NT - 1 else U + 1)
                if t:
                    dve.wait_ge(a_yt, t)
                b6 = B[6][:, :].rearrange("p (h e) -> p h e", h=H)
                if t < NT - 1:
                    TT(on, b6, bc(r0(t).unsqueeze(2), [P, H, DH]), ALU.mult).then_inc(a_oc, 1)
                else:
                    CP(on, b6).then_inc(a_oc, 1)

            def o_scale(t):
                dve.wait_ge(a_rs, t + 1)
                TT(on, on, bc(asm[:, 48:52].unsqueeze(2), [P, H, DH]), ALU.mult).then_inc(a_on, 1)

            U = H * (NT - 1)
            dve.wait_ge(out_s, 32)
            dve.wait_ge(a_tre, 2 * NT)
            maxes(0)
            for u in range(U):
                probs(u)
                if u % H == 1 and u > H:
                    o_copy(u // H - 1)
                if u % H == 3 and u > H:
                    o_scale(u // H - 1)
                if u + 1 < U:
                    maxes(u + 1)

            link(nc.vector.memset(g("Qbd")[:], 0.0))
            for h in range(H):
                for c in range(2):
                    r = slice(64 * c, 64 * c + 64)
                    m = CP(g("Qbd")[r, :, h, 32 * h + 16 * c:32 * h + 16 * c + 16],
                           g("QTs")[r, h, :].rearrange("p (b q) -> p b q", b=DB))
            m.then_inc(b_q, 1)

            def new_keys(b):
                CP(g(f"Kb{b}")[:, :, PAST:PAST + DS], g("KTs")[:, :, DS * b:DS * b + DS]).then_inc(b_kn, 1)

            for b in range(5):
                new_keys(b)
            dve.wait_ge(b_q, 1)
            new_keys(5)
            dve.wait_ge(a_pv, U)
            o_copy(NT - 2)
            link(nc.vector.memset(g("Pn")[:], 0.0))
            new_keys(6)
            new_keys(7)

            def s_max(b):
                a = 8 * (b % 2)
                dve.wait_ge(b_S, b + 1)
                link(nc.vector.tensor_reduce(asm[:, a + 4:a + 5], B[b % 2][:, 0:PAST + DS], AX, ALU.max))
                TS(asm[:, a:a + 1], asm[:, a + 4:a + 5], -0.125, None, ALU.mult).then_inc(b_nb, 1)

            s_max(0)
            for b in range(DB):
                a = 8 * (b % 2)
                dve.wait_ge(b_exp, b + 1)
                if b >= 2:
                    dve.wait_ge(b_T, b - 1)
                link(nc.vector.reciprocal(asm[:, a + 6:a + 7], asm[:, a + 2:a + 3]))
                link(TT(asm[:, a + 6:a + 7], asm[:, a + 6:a + 7], coef[:, :], ALU.mult))
                TS(g("Pp")[:, b % 2, :], g("Es")[:, b % 2, 0:PAST], asm[:, a + 6:a + 7], None, ALU.mult)
                TS(g("Pn")[:, b, DS * b:DS * b + DS], g("Es")[:, b % 2, PAST:PAST + DS], asm[:, a + 6:a + 7], None,
                   ALU.mult).then_inc(b_p, 1)
                if b + 1 < DB:
                    s_max(b + 1)
                if b == 1:
                    o_scale(NT - 2)
            for i in range(2):
                dve.wait_ge(b_pn, i + 1)
                ot = g("oTs")[:, :, 64 * i:64 * i + 64].rearrange("p h (b q) -> p b h q", b=4)
                for j in range(4):
                    part = B[(4 if j < 2 else 2) + i][:, :].rearrange("p (b h c q) -> p b h c q", b=4, h=H, c=2)[:, :, :, j % 2, :]
                    m = TT(ot, ot, part, ALU.add) if j else CP(ot, part)
                    if j < 3:
                        link(m)
                if i:
                    m.then_inc(b_o, 1)
            o_copy(NT - 1)

            for c in range(CH):
                split_dve(dve, SPLIT_Y + c, g("YT")[:, :, cs(c)], g("YH")[:, :, cs(c)], NL[:, :, cs(c)])
                if c == 0:
                    o_scale(NT - 1)
            dve.wait_ge(ld["xr"], 16 * CH)

            def joined_dve(pair, src, gain):
                z0, p0 = CH * pair, P_X if pair == 0 else P_FF

                def post(c):
                    post_dve(dve, z0 + c, src[:, :, cs(c)], H_[:, :, cs(c)])

                def pre(c):
                    dve.wait_ge(n_res, z0 + c + 1)
                    pre_dve(dve, p0 + c, H_[:, :, cs(c)], NLf[:, :, cs(c)], NL[:, :, cs(c)], NH[:, :, cs(c)], gain, NC)

                for q in range(24):
                    post_add(dve, pair, q)
                    if q == 16:
                        post(0)
                    if q == 20:
                        post(1)
                    if q == 21:
                        pre(0)
                pre(1)
                post(2)
                pre(2)

            joined_dve(0, g("MIX"), G_PREX)

            xm = g("xm")
            QX = g("QX")
            dve.wait_ge(lin_ev, 4 + 48)
            link(nc.vector.memset(g("xQbd")[:], 0.0))

            def q_low(t):
                dve.wait_ge(x_qh, t + 1)
                TT(g("QXl")[:], QX[:, :, tok(t)], g("QXh")[:].bitcast(F32), ALU.subtract).then_inc(x_ql, 1)

            def y_lay(b):
                if b >= 2:
                    dve.wait_ge(y_S, b - 1)
                diag = g("xQbd")[:, b % 2, :].rearrange("p (h x) -> p h x", h=H)[:, :, 0:128]
                CP(diag.rearrange("p h (k x) -> p h k x", k=2)[:, :, :, 0:DS],
                   QX[:, :, SEQ + DS * b:SEQ + DS * b + DS].rearrange("p (h k) q -> p h k q", k=2)).then_inc(y_q, 1)

            dve.wait_ge(mk_h, 1)
            TT(g("mkl")[:], g("mkT")[:], g("mkh")[:].bitcast(F32), ALU.subtract).then_inc(mk_l, 1)
            y_lay(0)
            y_lay(1)
            q_low(0)

            def x_max(t):
                dve.wait_ge(x_S, t + 1)
                for j in range(2):
                    m = nc.vector.tensor_reduce(xm[:, 2 * j:2 * j + 2], B[j][:, :].rearrange("p (a n) -> p a n", a=2), AX, ALU.max)
                link(m)
                TS(xm[:, 4:8], xm[:, 0:4], -1.0 / 16, None, ALU.mult).then_inc(x_nb, 1)

            def y_max(b):
                dve.wait_ge(y_S, b + 1)
                link(nc.vector.tensor_reduce(xm[0:64, 16:17], B[6][0:64, 0:MEM], AX, ALU.max))
                TS(xm[0:64, 17:18], xm[0:64, 16:17], -1.0 / 16, None, ALU.mult).then_inc(y_nb, 1)

            def x_probs(t):
                dve.wait_ge(x_exp, H * (t + 1))
                link(nc.vector.reciprocal(xm[:, 12:16], xm[:, 8:12]))
                e = g(f"xE{t % 2}")[:]
                TT(e, e, bc(xm[:, 12:16].unsqueeze(2), [P, H, MEM]), ALU.mult).then_inc(x_p, 1)

            def y_probs(b):
                dve.wait_ge(y_exp, b + 1)
                link(nc.vector.reciprocal(xm[0:64, 19:20], xm[0:64, 18:19]))
                e = g(f"sE{b % 2}")[:]
                TS(e, e, xm[0:64, 19:20], None, ALU.mult).then_inc(y_p, 1)

            def x_out(t):
                dve.wait_ge(x_pv, t + 1)
                for j in range(2):
                    m = CP(QX[:, 4 * j:4 * j + 4, tok(t)], B[4 + j][:, :].rearrange("p (a q) -> p a q", a=4))
                m.then_inc(x_o, 1)

            def y_out_(b):
                dve.wait_ge(y_pv, b + 1)
                CP(QX[:, :, SEQ + DS * b:SEQ + DS * b + DS], B[7][:, P:2 * P].rearrange("p (a q) -> p a q", a=KT)).then_inc(ys_o, 1)

            x_max(0)
            q_low(1)
            y_max(0)
            x_probs(0)
            y_probs(0)
            for i in range(DB):
                if i + 1 < DB:
                    x_max(i + 1)
                    y_max(i + 1)
                    if i + 2 < DB:
                        y_lay(i + 2)
                    x_probs(i + 1)
                    y_probs(i + 1)
                    if i + 2 < DB:
                        q_low(i + 2)
                x_out(i)
                y_out_(i)

            for c in range(CH):
                split_dve(dve, SPLIT_OX + c, QX[:, :, cs(c)], NH[:, :, cs(c)], NL[:, :, cs(c)])
            joined_dve(1, QX, G_PREF)
            ACC = g("ACC")

            def hidden(gi):
                for n in range(6 * gi, 6 * gi + 6):
                    c, f = n % 6 // 2, n % 2
                    dve.wait_ge(f_sg, n + 1)
                    dve.wait_ge(f_up, 2 * n + 2)
                    if n >= 2:
                        dve.wait_ge(f_hh, n - 1)
                    TT(g(f"hr{n % 2}")[:], g(f"sg{n % 2}")[:], B[2 * (n % 3) + 1][:, 0:NC], ALU.mult).then_inc(f_hr, 1)
                    dve.wait_ge(f_hh, n + 1)
                    TT(g(f"hid_l{gi % 2}{f}")[:, cs(c)], g(f"hr{n % 2}")[:],
                       g(f"hid_h{gi % 2}{f}")[:, cs(c)].bitcast(F32), ALU.subtract).then_inc(f_hl, 1)

            def add_down(gi, q, bank_):
                dve.wait_ge(f_dn, 24 * gi + q + 1)
                a = ACC[:, q % KT, cs(q // KT)]
                if gi == 0:
                    CP(a, bank_[:, 0:NC]).then_inc(f_de, 1)
                else:
                    TT(a, a, bank_[:, 0:NC], ALU.add).then_inc(f_de, 1)

            def last_norm(c):
                dve.wait_ge(n_std, P_END + c + 1)
                link(nc.vector.reciprocal(g("rstd")[:], g("rstd")[:]))
                a = ACC[:, :, cs(c)]
                for k in range(KT):
                    m = STT(out=a[:, k, :], in0=a[:, k, :], scalar=vec[:, G_POSTF + k:G_POSTF + k + 1], in1=g("rstd")[:],
                            op0=ALU.mult, op1=ALU.mult)
                m.then_inc(n_t, 1)
                dve.wait_ge(n_t, P_END + c + 1)
                dve.wait_ge(ld["Hb0"], 16 * CH)
                hb = g("Hback")[:, :, cs(c)]
                TT(hb, hb, a, ALU.add).then_inc(n_res, 1)

            hidden(0)
            for gi in range(1, NG):
                hidden(gi)
                for q in range(3 * KT):
                    add_down(gi - 1, q, B[6 + q % 2])
            for q in range(3 * KT):
                add_down(NG - 1, q, B[q % 6])
                if q == 17:
                    last_norm(0)
            last_norm(1)
            last_norm(2)


def _consts():
    p = np.arange(P)
    c = np.zeros((P, C_END), np.float32)
    c[:, C_ID:C_ID + P] = np.eye(P)
    c[:, C_TP:C_TP + P] = p[:, None] <= p[None, :]
    same = p[:, None] // DS == p[None, :] // DS
    c[:, C_TS:C_TS + P] = same & (p[:, None] <= p[None, :])
    c[:, C_BS:C_BS + P] = same
    c[:, C_BB:C_BB + DB] = p[:, None] // DS == np.arange(DB)
    c[:, C_C1] = p // DS % 2
    c[:, C_C0] = 1 - c[:, C_C1]
    pos = np.concatenate([np.arange(SEQ), PAST + np.arange(NS) % DS]).astype(np.float32)
    inv = np.power(np.float32(10000.0), -np.arange(0, 64, 2, dtype=np.float32) / np.float32(64))
    ang = (pos[:, None] * inv[None, :]).astype(np.float32).reshape(NT, P, 32).transpose(1, 0, 2).reshape(P, -1)
    c[:, C_COS:C_COS + 288] = np.cos(ang.astype(np.float64))
    c[:, C_SIN:C_SIN + 288] = np.sin(ang.astype(np.float64))
    return c


def kernel(x_prompt, x_sample, cache_attn_k, cache_attn_v, state_ssm, state_conv, cache_mem_k, cache_mem_v,
           mem_prompt, w_in, conv_w, conv_b, dt_bias, a_log, d_skip, ssm_norm_w,
           lam_q1, lam_k1, lam_q2, lam_k2, subln_w, w_out, g_mem, wq_x, wk_x, wv_x, wo_x,
           g_pre_mix, g_post_mix, g_pre_x, g_post_x, g_pre_ffn, g_post_ffn, w_gate, w_up, w_down):
    import concourse.bacc as _bacc
    from concourse.bass_utils import run_bass_kernel_spmd as _run

    A = np.asarray

    def feat(x):
        x = A(x)
        return x.T.reshape(-1, P, x.shape[0]).transpose(1, 0, 2)

    def fm(w):
        w = A(w)
        return w.reshape(w.shape[0] // P, P, -1, P).transpose(2, 1, 0, 3).reshape(-1, P, WI)

    def tm(w):
        w = A(w)
        return w.reshape(2, 4, P, -1, 256).transpose(3, 0, 2, 1, 4).reshape(-1, P, WI)

    x = np.concatenate([A(x_prompt)[0], A(x_sample).reshape(NS, D)])
    wi = A(w_in)[0]
    q0 = 512 + 1024 + 8
    gate, upw, down = fm(A(w_gate)[0]), fm(A(w_up)[0]), A(w_down)[0].reshape(FT, P, D)
    ups = [np.stack([gate[2 * g], upw[2 * g], gate[2 * g + 1], upw[2 * g + 1]]) for g in range(NG)]
    downs = [down[2 * g:2 * g + 2] for g in range(NG)]
    ff = [ups[0]]
    for g in range(1, NG):
        ff += [ups[g], downs[g - 1]]
    ff.append(downs[-1])
    mix, wk, wv = tm(np.concatenate([wi[:, 0:512], wi[:, q0:]], axis=1)), fm(A(wk_x)[0]), tm(A(wv_x)[0])
    wall = np.concatenate([mix[0:4], wk[0:4], mix[4:8], wk[4:8], mix[8:12], wv[0:4], mix[12:16], wv[4:8],
                           fm(wi[:, 512:1536]), fm(A(w_out)[0]), fm(A(wq_x)[0]), fm(A(wo_x)[0])] + ff)
    gains = [A(v)[0].reshape(KT, P).T for v in (g_mem, g_pre_mix, g_post_mix, g_pre_x, g_post_x, g_pre_ffn, g_post_ffn)]
    vecs = np.concatenate(gains + [A(conv_w)[0].T.reshape(KT, P, 4).transpose(1, 0, 2).reshape(P, 32),
                                   A(conv_b)[0].reshape(KT, P).T, A(ssm_norm_w)[0].reshape(4, P).T,
                                   A(subln_w)[0].reshape(P, 1)], axis=1)
    rows = np.concatenate([A(v)[0] for v in (dt_bias, a_log, d_skip, lam_q1, lam_k1, lam_q2, lam_k2)])
    arrays = {
        "xT": feat(x),
        "memT": feat(A(mem_prompt)[0]),
        "wall": wall,
        "wdt": wi[:, 1536:1544].reshape(KT, P, 8).transpose(1, 0, 2),
        "consts": _consts(),
        "vecs": vecs,
        "rows": rows,
        "kc": A(cache_attn_k)[0].reshape(DB, PAST, H, DH).transpose(0, 3, 2, 1),
        "vc": A(cache_attn_v)[0].reshape(DB, PAST, 512),
        "h0": A(state_ssm)[0].reshape(DB, 512, P).transpose(2, 0, 1),
        "sconv": A(state_conv)[0].reshape(DB, 3, KT, P).transpose(3, 2, 0, 1).reshape(P, KT, 24),
        "cmk": A(cache_mem_k)[0].reshape(DB, MEM, KT, P).transpose(0, 3, 2, 1),
        "cmv": A(cache_mem_v)[0].reshape(DB, MEM, D),
    }
    arrays = {k: np.ascontiguousarray(v) for k, v in arrays.items()}
    outs = {"y": (P, KT, NTOK), "k": (NTOK, 512), "v": (NTOK, 512), "ssm": (1 + DB, P, 512), "conv": (P, KT, 27),
            "mk": (P, KT, MEM), "mv": (MEM, D)}
    scratch = {"zs": (NTOK, 512), "q": (NTOK, 512), "h": (P, KT, NTOK)}
    nc = _bacc.Bacc("TRN2", target_bir_lowering=False, num_devices=1)
    args = [nc.dram_tensor("in_" + k, a.shape, mybir.dt.from_np(a.dtype), kind="ExternalInput").ap()
            for k, a in arrays.items()]
    args += [nc.dram_tensor("out_" + k, s, F32, kind="ExternalOutput").ap() for k, s in outs.items()]
    args += [nc.dram_tensor("scratch_" + k, s, F32, kind="Internal").ap() for k, s in scratch.items()]
    build(nc, *args)
    r = _run(nc, [{"in_" + k: a for k, a in arrays.items()}], core_ids=[0]).results[0]
    o = {k: r["out_" + k] for k in outs}
    y = o["y"].transpose(2, 1, 0).reshape(NTOK, D)
    conv = o["conv"].transpose(2, 1, 0).reshape(27, D)
    ssm = o["ssm"].transpose(0, 2, 1).reshape(1 + DB, SH, SP_, P)
    return (y[:SEQ][None], y[SEQ:].reshape(DB, DS, D),
            o["k"][:SEQ].reshape(1, 1, SEQ, 4, 2, 64), o["v"][:SEQ].reshape(1, 1, SEQ, 4, 128),
            ssm[:1][None], conv[:3].reshape(1, 1, 3, D),
            o["mk"].transpose(2, 1, 0).reshape(1, 1, MEM, 4, 256), o["mv"].reshape(1, 1, MEM, 4, 256),
            o["k"][SEQ:].reshape(1, DB, DS, 4, 2, 64), o["v"][SEQ:].reshape(1, DB, DS, 4, 128),
            ssm[1:][None], conv[3:].reshape(1, DB, 3, D))
```
